# Optimizing a Trainium2 kernel written in Bass

```python
import jax, jax.numpy as jnp
from jax import lax
import numpy as np

D_MODEL = 2048
BATCH = 1
SEQ = 512
DEPTH = 1

GRID_W = 64
ROPE_THETA = 10000.0
Q_BLOCK = 128
RMS_EPS = 1e-6

MLA_HEADS = 8
MLA_Q_RANK = 512
MLA_KV_RANK = 256
MLA_NOPE_DIM = 128
MLA_ROPE_DIM = 64
MLA_V_DIM = 128

GQA_HEADS = 8
GQA_KV_HEADS = 2
GQA_HEAD_DIM = 128
GQA_GROUP = GQA_HEADS // GQA_KV_HEADS

N_EXPERTS = 16
EC_CAPACITY = 2
EXPERT_FF = 1024

IN_WIDTHS = (
    MLA_Q_RANK,
    MLA_KV_RANK,
    MLA_ROPE_DIM,
    GQA_HEADS * GQA_HEAD_DIM,
    GQA_KV_HEADS * GQA_HEAD_DIM,
    GQA_KV_HEADS * GQA_HEAD_DIM,
    D_MODEL,
    D_MODEL,
)
IN_COLS = sum(IN_WIDTHS)
IN_SPLITS = tuple(int(s) for s in np.cumsum(IN_WIDTHS)[:-1])

kernel_name = "hybrid_mla_gqa_axial_ec_moe_encoder"

def _rmsnorm(x, g):
    xf = x.astype(jnp.float32)
    y = xf * lax.rsqrt(jnp.mean(xf * xf, axis=-1, keepdims=True) + RMS_EPS)
    return (y * g.astype(jnp.float32)).astype(x.dtype)

def _rope_angles(pos, dim):
    half = dim // 2
    freqs = ROPE_THETA ** (-jnp.arange(half, dtype=jnp.float32) / half)
    return pos.astype(jnp.float32)[:, None] * freqs[None, :]

def _rope(x, ang):
    cos = jnp.cos(ang).astype(x.dtype)
    sin = jnp.sin(ang).astype(x.dtype)
    x1, x2 = jnp.split(x, 2, axis=-1)
    return jnp.concatenate([x1 * cos - x2 * sin, x1 * sin + x2 * cos], axis=-1)

def _axial_rope(x, ang_row, ang_col):
    xr, xc = jnp.split(x, 2, axis=-1)
    return jnp.concatenate([_rope(xr, ang_row), _rope(xc, ang_col)], axis=-1)

def _query_blocks(q):
    *lead, s, d = q.shape
    qb = q.reshape(*lead, s // Q_BLOCK, Q_BLOCK, d)
    return jnp.moveaxis(qb, -3, 0)

def _merge_blocks(ob):
    ob = jnp.moveaxis(ob, 0, -3)
    return ob.reshape(*ob.shape[:-3], -1, ob.shape[-1])

def _mla_attention(qn, qr, kn, kr, v):
    scale = (MLA_NOPE_DIM + MLA_ROPE_DIM) ** -0.5

    def block(args):
        qn_b, qr_b = args
        s = (jnp.einsum('bhqd,bhkd->bhqk', qn_b, kn, preferred_element_type=jnp.float32)
             + jnp.einsum('bhqr,bkr->bhqk', qr_b, kr, preferred_element_type=jnp.float32)) * scale
        p = jax.nn.softmax(s, axis=-1).astype(v.dtype)
        return jnp.einsum('bhqk,bhkd->bhqd', p, v)

    return _merge_blocks(lax.map(block, (_query_blocks(qn), _query_blocks(qr))))

def _gqa_attention(q, k, v):
    scale = GQA_HEAD_DIM ** -0.5

    def block(q_b):
        s = jnp.einsum('bngqd,bnkd->bngqk', q_b, k, preferred_element_type=jnp.float32) * scale
        p = jax.nn.softmax(s, axis=-1).astype(v.dtype)
        return jnp.einsum('bngqk,bnkd->bngqd', p, v)

    return _merge_blocks(lax.map(block, _query_blocks(q)))

def _expert_choice_ffn(h, w_router, w_e_gate, w_e_up, w_e_down):
    b, s, d = h.shape
    cap = EC_CAPACITY * s // N_EXPERTS
    logits = jnp.einsum('bsd,de->bse', h, w_router, preferred_element_type=jnp.float32)
    aff = jax.nn.softmax(logits, axis=-1)
    vals, idx = lax.top_k(jnp.swapaxes(aff, 1, 2), cap)
    xg = jax.vmap(lambda hb, ib: hb[ib])(h, idx)
    a = jnp.einsum('becd,edf->becf', xg, w_e_gate)
    u = jnp.einsum('becd,edf->becf', xg, w_e_up)
    y = jnp.einsum('becf,efd->becd', jax.nn.silu(a) * u, w_e_down)
    y = y * vals.astype(y.dtype)[..., None]
    return jax.vmap(lambda ib, yb: jnp.zeros((s, d), yb.dtype).at[ib.reshape(-1)].add(yb.reshape(-1, d)))(idx, y)

def _layer(x, c, w_ada, b_ada, g_mix, w_in, g_cq, g_ckv, w_uq, w_ukv, g_qn, g_kn,
           w_br_a, w_br_b, w_out, g_ffn, w_router, w_e_gate, w_e_up, w_e_down,
           ang_1d, ang_row, ang_col):
    b, s, d = x.shape
    mod = jnp.einsum('bd,de->be', jax.nn.silu(c), w_ada) + b_ada
    sh1, sc1, gt1, sh2, sc2, gt2 = jnp.split(mod[:, None, :], 6, axis=-1)

    h = _rmsnorm(x, g_mix) * (1 + sc1) + sh1
    z = h @ w_in
    cq, ckv, kr, qg, kg, vg, gate_a, gate_b = jnp.split(z, IN_SPLITS, axis=-1)

    q = (_rmsnorm(cq, g_cq) @ w_uq).reshape(b, s, MLA_HEADS, MLA_NOPE_DIM + MLA_ROPE_DIM)
    q = q.transpose(0, 2, 1, 3)
    qn, qr = q[..., :MLA_NOPE_DIM], _rope(q[..., MLA_NOPE_DIM:], ang_1d)
    kv = (_rmsnorm(ckv, g_ckv) @ w_ukv).reshape(b, s, MLA_HEADS, MLA_NOPE_DIM + MLA_V_DIM)
    kv = kv.transpose(0, 2, 1, 3)
    kn, va = kv[..., :MLA_NOPE_DIM], kv[..., MLA_NOPE_DIM:]
    kr = _rope(kr, ang_1d)
    o_a = _mla_attention(qn, qr, kn, kr, va)
    o_a = o_a.transpose(0, 2, 1, 3).reshape(b, s, MLA_HEADS * MLA_V_DIM)

    qb = _rmsnorm(qg.reshape(b, s, GQA_HEADS, GQA_HEAD_DIM), g_qn).transpose(0, 2, 1, 3)
    kb = _rmsnorm(kg.reshape(b, s, GQA_KV_HEADS, GQA_HEAD_DIM), g_kn).transpose(0, 2, 1, 3)
    vb = vg.reshape(b, s, GQA_KV_HEADS, GQA_HEAD_DIM).transpose(0, 2, 1, 3)
    qb = _axial_rope(qb, ang_row, ang_col).reshape(b, GQA_KV_HEADS, GQA_GROUP, s, GQA_HEAD_DIM)
    kb = _axial_rope(kb, ang_row, ang_col)
    o_b = _gqa_attention(qb, kb, vb).reshape(b, GQA_HEADS, s, GQA_HEAD_DIM)
    o_b = o_b.transpose(0, 2, 1, 3).reshape(b, s, GQA_HEADS * GQA_HEAD_DIM)

    merged = jax.nn.sigmoid(gate_a) * (o_a @ w_br_a) + jax.nn.sigmoid(gate_b) * (o_b @ w_br_b)
    x = x + gt1 * (merged @ w_out)

    h2 = _rmsnorm(x, g_ffn) * (1 + sc2) + sh2
    x = x + gt2 * _expert_choice_ffn(h2, w_router, w_e_gate, w_e_up, w_e_down)
    return x

def setup_inputs(seed: int = 0) -> dict:
    key = jax.random.key(seed)
    ks = jax.random.split(key, 24)
    f32 = jnp.float32
    L = DEPTH

    def w(k, shape, fan_in):
        return jax.random.normal(k, shape, f32) * (fan_in ** -0.5)

    def gain(k, shape):
        return 1.0 + 0.02 * jax.random.normal(k, shape, f32)

    return {
        "x": jax.random.normal(ks[0], (BATCH, SEQ, D_MODEL), f32),
        "c": jax.random.normal(ks[1], (BATCH, D_MODEL), f32),
        "w_ada": w(ks[2], (L, D_MODEL, 6 * D_MODEL), D_MODEL),
        "b_ada": 0.02 * jax.random.normal(ks[3], (L, 6 * D_MODEL), f32),
        "g_mix": gain(ks[4], (L, D_MODEL)),
        "w_in": w(ks[5], (L, D_MODEL, IN_COLS), D_MODEL),
        "g_cq": gain(ks[6], (L, MLA_Q_RANK)),
        "g_ckv": gain(ks[7], (L, MLA_KV_RANK)),
        "w_uq": w(ks[8], (L, MLA_Q_RANK, MLA_HEADS * (MLA_NOPE_DIM + MLA_ROPE_DIM)), MLA_Q_RANK),
        "w_ukv": w(ks[9], (L, MLA_KV_RANK, MLA_HEADS * (MLA_NOPE_DIM + MLA_V_DIM)), MLA_KV_RANK),
        "g_qn": gain(ks[10], (L, GQA_HEAD_DIM)),
        "g_kn": gain(ks[11], (L, GQA_HEAD_DIM)),
        "w_br_a": w(ks[12], (L, MLA_HEADS * MLA_V_DIM, D_MODEL), MLA_HEADS * MLA_V_DIM),
        "w_br_b": w(ks[13], (L, GQA_HEADS * GQA_HEAD_DIM, D_MODEL), GQA_HEADS * GQA_HEAD_DIM),
        "w_out": w(ks[14], (L, D_MODEL, D_MODEL), D_MODEL),
        "g_ffn": gain(ks[15], (L, D_MODEL)),
        "w_router": w(ks[16], (L, D_MODEL, N_EXPERTS), D_MODEL),
        "w_e_gate": w(ks[17], (L, N_EXPERTS, D_MODEL, EXPERT_FF), D_MODEL),
        "w_e_up": w(ks[18], (L, N_EXPERTS, D_MODEL, EXPERT_FF), D_MODEL),
        "w_e_down": w(ks[19], (L, N_EXPERTS, EXPERT_FF, D_MODEL), EXPERT_FF),
        "g_final": gain(ks[20], (D_MODEL,)),
    }

def reference(x, c, w_ada, b_ada, g_mix, w_in, g_cq, g_ckv, w_uq, w_ukv, g_qn, g_kn,
              w_br_a, w_br_b, w_out, g_ffn, w_router, w_e_gate, w_e_up, w_e_down, g_final):
    s = x.shape[1]
    rows = s // GRID_W
    t = jnp.arange(s)
    row = jnp.repeat(jnp.arange(rows), GRID_W)
    col = jnp.tile(jnp.arange(GRID_W), rows)
    ang_1d = _rope_angles(t, MLA_ROPE_DIM)
    ang_row = _rope_angles(row, GQA_HEAD_DIM // 2)
    ang_col = _rope_angles(col, GQA_HEAD_DIM // 2)
    for l in range(DEPTH):
        x = _layer(x, c, w_ada[l], b_ada[l], g_mix[l], w_in[l], g_cq[l], g_ckv[l], w_uq[l],
                   w_ukv[l], g_qn[l], g_kn[l], w_br_a[l], w_br_b[l], w_out[l], g_ffn[l],
                   w_router[l], w_e_gate[l], w_e_up[l], w_e_down[l], ang_1d, ang_row, ang_col)
    return _rmsnorm(x, g_final)


_drawn_inputs = setup_inputs


def setup_inputs(seed=0):
    import zlib

    import numpy as np

    out = dict(_drawn_inputs(seed))
    spreads = {}
    factors = {'g_mix': 6.085,
     'g_cq': 8.0,
     'g_ckv': 8.0,
     'g_qn': 8.0,
     'g_kn': 7.905,
     'g_ffn': 2.917,
     'g_final': 2.875}
    for name, (base, spread) in spreads.items():
        noise = np.random.default_rng([zlib.crc32(name.encode()), seed]).standard_normal(out[name].shape)
        drawn = base * np.exp(spread * noise) if base else spread * noise
        out[name] = __import__('jax').numpy.asarray(drawn.astype(out[name].dtype))
    for name, factor in factors.items():
        out[name] = (out[name] * factor).astype(out[name].dtype)
    return out
```

```python
import math
from contextlib import ExitStack

import numpy as np
import concourse.bass as bass
from concourse import mybir

P = 128
D = 2048
S = 512
T = S // P
KD = D // P
QR, KVR, ROPE, DH = 512, 256, 64, 128
HM, HG, KVG = 8, 8, 2
LAT = QR + KVR + ROPE
GQ = (HG + 2 * KVG) * DH
NE, FF = 16, 1024
CAP = 2 * S // NE
W = 512
EPS = 1e-6
MLA_SCALE = float(DH + ROPE) ** -0.5
GQA_SCALE = float(DH) ** -0.5
NSTAGE, NSPLIT = 8, 2
ADA_W, NADA = 1024, 4
ADA_BLOCKS = 6 * D // ADA_W
ADA_FIRST = 2 * D // ADA_W
N_Z, N_GATE = 0, 40
N_BR = N_GATE + 64
N_OUT = N_BR + 32
N_EXP = N_OUT + 32
G_Z, G_GATE = 0, 20
G_BR = G_GATE + 32
G_OUT = G_BR + 32
G_EXP = G_OUT + 16
PAIRS = NE // 2
DOWN = [(0, 0), (0, 1), (1, 0), (1, 1), (0, 2), (0, 3), (1, 2), (1, 3)] + [(j, k) for j in (2, 3) for k in range(4)]
C_ID, C_FOLD, C_IOTA, C_QTAB = 0, 128, 192, 256
C_KC, C_KS, C_GC, C_GS, C_END = 768, 896, 1024, 1280, 1536


def shape_constants():
    half = ROPE // 2
    freqs = (np.float32(10000.0) ** (-np.arange(half, dtype=np.float32) / np.float32(half))).astype(np.float32)

    def tables(pos):
        a = pos.astype(np.float32)[:, None] * freqs[None, :]
        return np.cos(a).astype(np.float32), np.sin(a).astype(np.float32)

    t = np.arange(S)
    c1, s1 = tables(t)
    cr, sr = tables(t // 64)
    cc, sc = tables(t % 64)
    k = np.zeros((P, C_END), np.float32)
    k[:, C_ID:C_ID + P] = np.eye(P)
    k[:, C_FOLD:C_FOLD + 64] = np.concatenate([np.eye(64), np.eye(64)])
    k[:, C_IOTA:C_IOTA + 64] = np.arange(64)[None, :]
    k[:, C_QTAB:C_QTAB + S] = np.concatenate([c1.T, c1.T, -s1.T, s1.T])

    def by_tile(a):
        return a.reshape(T, P, -1).transpose(1, 0, 2).reshape(P, -1)

    k[:, C_KC:C_KS] = by_tile(c1)
    k[:, C_KS:C_GC] = by_tile(s1)
    k[:, C_GC:C_GS] = by_tile(np.concatenate([cr, cc], 1))
    k[:, C_GS:C_END] = by_tile(np.concatenate([sr, sc], 1))
    return k


def encoder_block(nc, x, c, w_ada, b_ada, g_mix, w_in, g_cq, g_ckv, w_uq, w_ukv, g_qn, g_kn,
                  w_br_a, w_br_b, w_out, g_ffn, w_router, w_e_gate, w_e_up, w_e_down, g_final,
                  consts, sig_gates, out):
    F32, F32R = mybir.dt.float32, mybir.dt.float32r
    ALU, ACT, AX = mybir.AluOpType, mybir.ActivationFunctionType, mybir.AxisListType
    ds = bass.ds

    x_v = x[0].rearrange("(t p) d -> p t d", p=P)
    out_v = out[0].rearrange("(t p) d -> p t d", p=P)
    w_ada_v = w_ada[0].rearrange("(k p) n -> p k n", p=P)
    w_in_v = w_in[0].rearrange("(k p) n -> p k n", p=P)
    w_uq_v = w_uq[0].rearrange("(k p) n -> p k n", p=P)
    w_ukv_v = w_ukv[0].rearrange("(k p) n -> p k n", p=P)
    w_bra_v = w_br_a[0].rearrange("(k p) n -> p k n", p=P)
    w_brb_v = w_br_b[0].rearrange("(k p) n -> p k n", p=P)
    w_out_v = w_out[0].rearrange("(k p) n -> p k n", p=P)
    w_router_v = w_router[0].rearrange("(k p) n -> p k n", p=P)
    w_gate_v = w_e_gate[0].rearrange("e (k p) n -> e p k n", p=P)
    w_up_v = w_e_up[0].rearrange("e (k p) n -> e p k n", p=P)
    w_down_v = w_e_down[0].rearrange("e (k p) n -> e p k n", p=P)
    sig_v = sig_gates.rearrange("(m p) s -> p m s", p=P)

    ctx = ExitStack()
    with ctx:
        KB = 1024
        sizes = {"ring": 48 * KB, "ada": 20 * KB, "A": 64 * KB, "B": 37 * KB, "C": 32 * KB, "small": 6 * KB + 512}
        arena_at = (nc.sbuf_base + 31) // 32 * 32
        ctx.enter_context(nc.sbuf_tensor("arena", [P, sum(sizes.values()) // 4], F32))
        start = arena_at
        base = {}
        for name, size in sizes.items():
            base[name] = start
            start += size

        def at(region, offset, name, shape, dt=F32):
            size = 4 * math.prod(shape[1:])
            assert offset + size <= sizes[region], (name, offset, size)
            return nc.alloc_sbuf_tensor_at(name, shape, dt, offset=base[region] + offset)

        stage = at("ring", 0, "stage", [P, NSTAGE, 2, W])
        w_hi = at("ring", 32 * KB, "w_hi", [P, NSPLIT, 2, W], F32R)
        w_lo = at("ring", 40 * KB, "w_lo", [P, NSPLIT, 2, W], F32R)
        ada_tile = at("ada", 0, "ada_tile", [P, NADA, ADA_W])
        ada_acc = at("ada", 16 * KB, "ada_acc", [P, ADA_W])
        wq = at("ada", 0, "wq", [P, 2, 4, 256])
        wkv = at("ada", 8 * KB, "wkv", [P, 2, 2, 256])
        q_stage = at("ada", 0, "q_stage", [P, T, DH])
        k_stage = at("ada", 2 * KB, "k_stage", [P, T, DH])
        cqT = at("ada", 12 * KB, "cqT", [P, 4, S])
        gt_row = at("ada", 0, "gt_row", [P, D])
        sel = at("ada", 8 * KB, "sel", [P, T, 2, CAP])
        selT = at("ada", 10 * KB, "selT", [P, S], F32R)
        gu = at("ada", 12 * KB, "gu", [P, 2, W])
        sgm = at("ada", 16 * KB, "sgm", [P, 256])
        h32e = at("ada", 17 * KB, "h32e", [P, 256])
        xg32 = at("ada", 18 * KB, "xg32", [P, 4, P])
        h2T = at("ada", 12 * KB, "h2T", [P, 2, S])
        w_rt = at("ada", 16 * KB, "w_rt", [P, KD, NE])
        hT_hi = at("A", 0, "hT_hi", [P, KD, S], F32R)
        hT_lo = at("A", 32 * KB, "hT_lo", [P, KD, S], F32R)
        oT_hi = at("A", 0, "oT_hi", [P, KD, S], F32R)
        oT_lo = at("A", 32 * KB, "oT_lo", [P, KD, S], F32R)
        mT_hi = at("A", 0, "mT_hi", [P, KD, S], F32R)
        mT_lo = at("A", 32 * KB, "mT_lo", [P, KD, S], F32R)
        xgT = at("A", 0, "xgT", [P, KD, 2, P], F32R)
        heT = at("A", 16 * KB, "heT", [P, 8, P], F32R)
        ysum = at("A", 24 * KB, "ysum", [P, 4, W])
        y_hi = at("A", 32 * KB, "y_hi", [P, 4, W], F32R)
        y_lo = at("A", 40 * KB, "y_lo", [P, 4, W], F32R)
        ytmp = at("A", 48 * KB, "ytmp", [64, W])
        junk2 = at("A", 50 * KB, "junk2", [P, D])
        affT = at("A", 20 * KB, "affT", [NE, S])
        work = at("A", 22 * KB, "work", [NE, 2, S])
        gt_m = at("A", 26 * KB, "gt_m", [NE, S])
        eq_m = at("A", 28 * KB, "eq_m", [NE, S])
        rank = at("A", 30 * KB, "rank", [NE, S])
        slotT = at("A", 58 * KB, "slotT", [NE, S])
        res = at("A", 0, "res", [P, 2, D])
        x_sb = at("B", 0, "x_sb", [P, T, D])
        zc = at("B", 0, "zc", [P, T, LAT])
        zg = at("B", 13 * KB, "zg", [P, T, GQ])
        mT = at("B", 0, "mT", [P, KD, S])
        x1 = at("B", 0, "x1", [P, T, D])
        probs1 = at("B", 0, "probs1", [P, T, S])
        h32 = at("C", 0, "h32", [P, 4, S])
        junk = at("C", 8 * KB, "junk", [P, D])
        sig = at("C", 0, "sig", [P, 4, S])
        g_row = at("C", 16 * KB, "g_row", [P, HG + KVG, DH])
        rope_kc = at("C", 21 * KB, "rope_kc", [P, T, 32])
        rope_ks = at("C", 21 * KB + 512, "rope_ks", [P, T, 32])
        rope_gc = at("C", 22 * KB, "rope_gc", [P, T, 2, 32])
        rope_gs = at("C", 23 * KB, "rope_gs", [P, T, 2, 32])
        NR = (HG + KVG) * 2 * 32
        r_a = at("C", 8 * KB, "r_a", [P, HG + KVG, 2, 32])
        r_b = at("C", 8 * KB + 4 * NR, "r_b", [P, HG + KVG, 2, 32])
        r_c = at("C", 24 * KB, "r_c", [P, HG + KVG, 2, 32])
        r_d = at("C", 24 * KB + 4 * NR, "r_d", [P, HG + KVG, 2, 32])
        kr2 = at("C", 30 * KB, "kr2", [P, T, P])
        probs0 = at("C", 0, "probs0", [P, T, S])
        pT = at("C", 8 * KB, "pT", [P, 2, S])
        qn = at("C", 12 * KB, "qn", [P, S])
        qr = at("C", 14 * KB, "qr", [P, S])
        kn = at("C", 16 * KB, "kn", [P, S])
        v_sb = at("C", 18 * KB, "v_sb", [P, 2, T, DH])
        krT = at("C", 22 * KB, "krT", [P, S])
        ckvT = at("C", 24 * KB, "ckvT", [P, 2, S])
        sg_in = at("C", 0, "sg_in", [P, 2, 4, S])
        m_tmp = at("C", 16 * KB, "m_tmp", [P, S])
        diag = at("C", 18 * KB, "diag", [P, 4, P])
        xn = at("C", 0, "xn", [P, T, D])
        gf_row = at("C", 0, "gf_row", [P, D])
        probs = [probs0, probs1]

        small_at = [0]

        def small(name, shape, dt=F32):
            o = small_at[0]
            small_at[0] += (4 * math.prod(shape[1:]) + 31) // 32 * 32
            return at("small", o, name, shape, dt)

        ident = small("ident", [P, P])
        foldm = small("foldm", [P, 64])
        iota = small("iota", [P, 64])
        qtab = small("qtab", [P, S])
        ones = small("ones", [P, P])
        modcol = small("modcol", [P, 96])
        bcol = small("bcol", [P, 96])
        pcol = small("pcol", [P, 54])
        siluc = small("siluc", [P, 16])
        a1 = small("a1", [P, KD])
        ssq = small("ssq", [P, 16])
        rstd = small("rstd", [P, 16])
        zssq = small("zssq", [P, 16, T])
        zr = small("zr", [P, 16, T])
        eps_c = small("eps_c", [P, 1])
        nmax = small("nmax", [P, 2, 8])
        rsum = small("rsum", [P, 2, 8])
        aff = small("aff", [P, T, NE + 2])
        slots = small("slots", [P, T, NE + 2])
        lmx = small("lmx", [P, 8])
        val = small("val", [P, 1])
        m8 = small("m8", [NE, 8])
        cnt = small("cnt", [NE, 2])
        prow = at("C", 24 * KB, "prow", [54, P])
        brow = at("C", 26 * KB, "brow", [96, P])

        bank = [ctx.enter_context(nc.psum_tensor(f"bank{i}", [P, W], F32)) for i in range(8)]

        def sem(name):
            return ctx.enter_context(nc.semaphore(name))

        stage_full = [sem(f"stage_full{i}") for i in range(NSTAGE)]
        hi_ready, lo_ready, chunk_used = sem("hi_ready"), sem("lo_ready"), sem("chunk_used")
        acc_done, acc_free = sem("acc_done"), sem("acc_free")
        consts_in, x_in, rows_in = sem("consts_in"), sem("x_in"), sem("rows_in")
        cols_done, cols_ready, sigc_ready, siluc_ready = sem("cols_done"), sem("cols_ready"), sem("sigc_ready"), sem("siluc_ready")
        ada_full = [sem(f"ada_full{i}") for i in range(NADA)]
        ada_done, ada_col_done, ada_col_ready = sem("ada_done"), sem("ada_col_done"), sem("ada_col_ready")
        act_seq, dve_seq, pool_seq = sem("act_seq"), sem("dve_seq"), sem("pool_seq")
        std_ready, rstd_ready, xn_ready = sem("std_ready"), sem("rstd_ready"), sem("xn_ready")
        xT_done, h32_ready, hT_hi_ready, hT_lo_ready = sem("xT_done"), sem("h32_ready"), sem("hT_hi_ready"), sem("hT_lo_ready")
        tab_in = sem("tab_in")
        zstd_ready, zr_ready, zpost_ready = sem("zstd_ready"), sem("zr_ready"), sem("zpost_ready")
        sig_out = [sem(f"sig_out{i}") for i in range(4)]
        pro_done, pro_ready = sem("pro_done"), sem("pro_ready")
        hw_full = [sem("hw_full0"), sem("hw_full1")]
        qn_done, qr_done, kn_done, v_done = sem("qn_done"), sem("qr_done"), sem("kn_done"), sem("v_done")
        qn_ready, qr_ready, kn_ready, v_ready = sem("qn_ready"), sem("qr_ready"), sem("kn_ready"), sem("v_ready")
        qs_ready, ks_ready = sem("qs_ready"), sem("ks_ready")
        s_done, nmax_ready, exp_done, p_ready = sem("s_done"), sem("nmax_ready"), sem("exp_done"), sem("p_ready")
        nmx_seq, rinv_seq = sem("nmx_seq"), sem("rinv_seq")
        pT_done, pT_ready, pv_done, o_hi, o_lo = sem("pT_done"), sem("pT_ready"), sem("pv_done"), sem("o_hi"), sem("o_lo")
        sg_full = [sem("sg_full0"), sem("sg_full1")]
        diag_ready, row_done, row_ready = sem("diag_ready"), sem("row_done"), sem("row_ready")
        mT_ready, m_hi, m_lo, x1_in, x1_ready = sem("mT_ready"), sem("m_hi"), sem("m_lo"), sem("x1_in"), sem("x1_ready")
        wr_in, std2_ready, rstd2_ready, xn2_ready = sem("wr_in"), sem("std2_ready"), sem("rstd2_ready"), sem("xn2_ready")
        h2T_done, h2T_ready, logit_done = sem("h2T_done"), sem("h2T_ready"), sem("logit_done")
        lsub_ready, lexp_ready, aff_ready, affT_done, slotT_ready, slots_done = (
            sem("lsub_ready"), sem("lexp_ready"), sem("aff_ready"), sem("affT_done"), sem("slotT_ready"), sem("slots_done"))
        sel_ready, selT_done, selT_ready, val_done, val_ready = sem("sel_ready"), sem("selT_done"), sem("selT_ready"), sem("val_done"), sem("val_ready")
        gather_done, xg32_ready, xg_hi, xg_ready = sem("gather_done"), sem("xg32_ready"), sem("xg_hi"), sem("xg_ready")
        fold_done, sgm_ready, he32_ready, he_hi, he_ready = (
            sem("fold_done"), sem("sgm_ready"), sem("he32_ready"), sem("he_hi"), sem("he_ready"))
        he_mid = sem("he_mid")
        ytmp_ready, y32_ready, yhi_ready, ylo_ready = sem("ytmp_ready"), sem("y32_ready"), sem("yhi_ready"), sem("ylo_ready")
        scat_done, scat_added = sem("scat_done"), sem("scat_added")
        gf_in, std3_ready, rstd3_ready, res_ready = sem("gf_in"), sem("std3_ready"), sem("rstd3_ready"), sem("res_ready")
        stored = [sem("stored0"), sem("stored1")]

        block = ctx.enter_context(nc.Block())

        def wait_bank(eng, blk, b, n_end):
            if b < 3:
                eng.wait_ge(acc_done, 3 * blk + b + 1)
            else:
                eng.wait_ge(chunk_used, n_end + NSPLIT)

        @block.sync
        def _(sp):
            def load_chunk(n, c, src):
                sp.wait_ge(lo_ready, n + 1)
                width = src.shape[2]
                sp.dma_start(stage[:, c % NSTAGE, :, 0:width], src).then_inc(stage_full[c % NSTAGE], 16)

            def load_ada(m, k, r):
                sp.wait_ge(ada_done, m + 1)
                sp.dma_start(ada_tile[:, k % NADA, :], w_ada_v[:, k, ds(r * ADA_W, ADA_W)]).then_inc(ada_full[k % NADA], 16)

            for row, n, src in ((0, 16, g_mix[0]), (16, 16, g_ffn[0]), (32, 16, c[0]), (48, 4, g_cq[0]), (52, 2, g_ckv[0])):
                sp.dma_start(prow[row:row + n, :], src.rearrange("(k p) -> k p", p=P)).then_inc(rows_in, 16)
            sp.dma_start(brow[:, :], b_ada[0].rearrange("(k p) -> k p", p=P)).then_inc(rows_in, 16)
            for dst, a, b in ((ident, C_ID, C_FOLD), (foldm, C_FOLD, C_IOTA), (iota, C_IOTA, C_QTAB), (qtab, C_QTAB, C_KC)):
                sp.dma_start(dst[:, :], consts[:, a:b]).then_inc(consts_in, 16)
            for t in range(T):
                sp.dma_start(x_sb[:, t, :], x_v[:, t, :]).then_inc(x_in, 16)
            with sp.Fori(0, ADA_FIRST) as r:
                for k in range(KD):
                    load_ada(KD * r + k, k, r)
            for c8 in range(8):
                load_chunk(N_Z + c8, c8, w_in_v[:, 2 * c8:2 * c8 + 2, 0:QR])
            for c8 in range(8):
                load_chunk(N_Z + 8 + c8, c8, w_in_v[:, 2 * c8:2 * c8 + 2, QR:LAT])
            with sp.Fori(0, 3) as j:
                for c8 in range(8):
                    load_chunk(N_Z + 16 + 8 * j + c8, c8, w_in_v[:, 2 * c8:2 * c8 + 2, ds(LAT + W * j, W)])
            with sp.Fori(0, 8) as j:
                for c8 in range(8):
                    load_chunk(N_GATE + 8 * j + c8, c8, w_in_v[:, 2 * c8:2 * c8 + 2, ds(LAT + GQ + W * j, W)])
                    for k in (2 * c8, 2 * c8 + 1):
                        load_ada(KD * (j + ADA_FIRST) + k, k, j + ADA_FIRST)

            def head_weights(b, H):
                sp.dma_start(wq[:, b, :, 0:192], w_uq_v[:, :, ds(H * 192, 192)]).then_inc(hw_full[b], 16)
                sp.dma_start(wq[:, b, :, 192:224], w_uq_v[:, :, ds(H * 192 + 160, 32)]).then_inc(hw_full[b], 16)
                sp.dma_start(wq[:, b, :, 224:256], w_uq_v[:, :, ds(H * 192 + 128, 32)]).then_inc(hw_full[b], 16)
                sp.dma_start(wkv[:, b, :, :], w_ukv_v[:, :, ds(H * 256, 256)]).then_inc(hw_full[b], 16)

            for c4 in range(4):
                load_chunk(N_BR + c4, c4, w_bra_v[:, 2 * c4:2 * c4 + 2, 0:W])
            for c4 in range(4):
                load_chunk(N_BR + 4 + c4, 4 + c4, w_brb_v[:, 2 * c4:2 * c4 + 2, 0:W])
            sp.wait_ge(ada_done, NADA + KD * ADA_BLOCKS)
            head_weights(0, 0)
            head_weights(1, 1)
            with sp.Fori(0, 3) as i:
                for b in range(2):
                    sp.wait_ge(v_done, 2 * i + b + 1)
                    head_weights(b, 2 * i + 2 + b)

            def load_gates(ab, j):
                sp.dma_start(sg_in[:, ab, :, :], sig_v[:, ds(KD * ab + 4 * j, 4), :]).then_inc(sg_full[ab], 16)

            for i in range(4):
                sp.wait_ge(sig_out[i], 16 * 9)
            sp.wait_ge(o_lo, 2 + HM + HG)
            load_gates(0, 0)
            load_gates(1, 0)
            with sp.Fori(1, 4) as j:
                for c4 in range(4):
                    load_chunk(N_BR + 8 * j + c4, c4, w_bra_v[:, 2 * c4:2 * c4 + 2, ds(W * j, W)])
                sp.wait_ge(acc_free, G_BR + 8 * j)
                load_gates(0, j)
                for c4 in range(4):
                    load_chunk(N_BR + 8 * j + 4 + c4, 4 + c4, w_brb_v[:, 2 * c4:2 * c4 + 2, ds(W * j, W)])
                sp.wait_ge(acc_free, G_BR + 8 * j + 4)
                load_gates(1, j)
            for c8 in range(8):
                load_chunk(N_OUT + c8, c8, w_out_v[:, 2 * c8:2 * c8 + 2, 0:W])
            sp.wait_ge(m_lo, KD)
            for t in range(T):
                sp.dma_start(x1[:, t, :], x_v[:, t, :]).then_inc(x1_in, 16)
            with sp.Fori(1, 4) as j:
                for c8 in range(8):
                    load_chunk(N_OUT + 8 * j + c8, c8, w_out_v[:, 2 * c8:2 * c8 + 2, ds(W * j, W)])
            sp.dma_start(w_rt[:, :, :], w_router_v).then_inc(wr_in, 16)
            with sp.Fori(0, PAIRS) as p:
                for e in range(2):
                    n0 = N_EXP + 96 * p + 48 * e
                    for a in range(4):
                        w_v = (w_gate_v, w_up_v)[a % 2]
                        jb = a // 2
                        for c8 in range(8):
                            load_chunk(n0 + 8 * a + c8, c8, w_v[2 * p + e][:, 2 * c8:2 * c8 + 2, jb * W:(jb + 1) * W])
                    for i, (jd, kc) in enumerate(DOWN):
                        load_chunk(n0 + 32 + i, i % 8, w_down_v[2 * p + e][:, 2 * kc:2 * kc + 2, jd * W:(jd + 1) * W])
            sp.wait_ge(xg_ready, 4 * (PAIRS + 1))
            sp.dma_start(gf_row[:, :], g_final.partition_broadcast(P)).then_inc(gf_in, 16)
            for t in range(T):
                sp.wait_ge(res_ready, t + 1)
                sp.dma_start(out_v[:, t, :], res[:, t % 2, :]).then_inc(stored[t % 2], 16)
            for i in range(2):
                sp.wait_ge(stored[i], 16 * T // 2)

        @block.tensor
        def _(pe):
            mm = nc.tensor.matmul
            pe.sem_inc(chunk_used, NSPLIT)
            pe.wait_ge(rows_in, 16 * 6)
            pe.wait_ge(consts_in, 16 * 4)
            nc.tensor.transpose(bank[5][:, 0:54], prow[:, :], ident[0:54, 0:54])
            nc.tensor.transpose(bank[5][:, 64:160], brow[:, :], ident[0:96, 0:96]).then_inc(cols_done, 1)

            def ada_columns(r):
                pe.wait_ge(ada_done, KD * r + KD + NADA)
                pe.wait_ge(ada_col_ready, r + 1)
                for i in range(8):
                    last = mm(bank[4][:, i:i + 1], ada_acc[:, i * P:(i + 1) * P], ones[:, 0:1], start=True, stop=True)
                last.then_inc(ada_col_done, 1)

            with pe.Fori(0, ADA_FIRST) as r:
                ada_columns(r)

            def dense_block(n0, g0, chunks, k0, act_hi, act_lo, weights_stationary, width=W, ready=None, before=None):
                for cc in range(chunks):
                    if before is not None:
                        before(cc)
                    if ready is not None:
                        pe.wait_ge(ready, 2 * cc + 2)
                    pe.wait_ge(hi_ready, n0 + cc + 1)
                    s = (k0 // 2 + cc) % NSPLIT
                    for b in range(4):
                        if cc == 0:
                            pe.wait_ge(acc_free, g0 + b + 1)
                        passes = [(act_hi, w_hi), (act_lo, w_hi), (act_hi, w_lo)]
                        for i, (a, w) in enumerate(passes):
                            if b == 0 and i == 2:
                                pe.wait_ge(lo_ready, n0 + cc + 1 + NSTAGE)
                            for kk in range(2):
                                first = cc == 0 and i == 0 and kk == 0
                                end = cc == chunks - 1 and i == 2 and kk == 1
                                k = 2 * cc + kk + k0
                                if weights_stationary:
                                    last = mm(bank[b][:, :], w[:, s, kk, b * P:(b + 1) * P], a[:, k, :], start=first, stop=end)
                                else:
                                    last = mm(bank[b][:, 0:width], a[:, k, b * P:(b + 1) * P], w[:, s, kk, 0:width], start=first, stop=end)
                        if b == 3:
                            last.then_inc(chunk_used, 1)
                        elif cc == chunks - 1:
                            last.then_inc(acc_done, 1)

            pe.wait_ge(xn_ready, T)
            pe.wait_ge(ada_col_ready, ADA_FIRST + 1)
            def transpose_x(k):
                if k >= 4:
                    pe.wait_ge(h32_ready, k - 3)
                for t in range(T):
                    last = nc.tensor.transpose(bank[4 + k % 4][:, t * P:(t + 1) * P], x_sb[:, t, k * P:(k + 1) * P], ident[:, :])
                last.then_inc(xT_done, 1)

            for k in range(4):
                transpose_x(k)

            def transposes_ahead(cc):
                for k in (2 * cc + 4, 2 * cc + 5):
                    if k < KD:
                        transpose_x(k)

            dense_block(N_Z, G_Z, 8, 0, hT_hi, hT_lo, False, ready=hT_lo_ready, before=transposes_ahead)
            dense_block(N_Z + 8, G_Z + 4, 8, 0, hT_hi, hT_lo, False, width=LAT - QR)
            with pe.Fori(0, 3) as j:
                dense_block(N_Z + 16 + 8 * j, G_Z + 8 + 4 * j, 8, 0, hT_hi, hT_lo, False)
            with pe.Fori(0, 8) as j:
                dense_block(N_GATE + 8 * j, G_GATE + 4 * j, 8, 0, hT_hi, hT_lo, True)
                ada_columns(j + ADA_FIRST)

            pe.wait_ge(zpost_ready, 1)
            pe.wait_ge(ada_col_ready, ADA_BLOCKS + 1)
            for i in range(7):
                if i >= 4:
                    pe.wait_ge(pro_ready, i - 3)
                for t in range(T):
                    src = kr2[:, t, :] if i == 6 else zc[:, t, i * P:(i + 1) * P]
                    last = nc.tensor.transpose(bank[4 + i % 4][:, t * P:(t + 1) * P], src, ident[:, :])
                last.then_inc(pro_done, 1)

            def project_mla(H, b, use):
                pe.wait_ge(hw_full[b], 64 * use)
                pe.wait_ge(o_lo, H + 1)
                for k in range(4):
                    last = mm(bank[4][:, :], wq[:, b, k, 0:P], cqT[:, k, :], start=k == 0, stop=k == 3)
                last.then_inc(qn_done, 1)
                pe.wait_ge(v_ready, H + 1)
                for k in range(4):
                    last = mm(bank[5][:, :], wq[:, b, k, P:2 * P], cqT[:, k, :], start=k == 0, stop=k == 3)
                last.then_inc(qr_done, 1)
                pe.wait_ge(qn_ready, H + 1)
                for k in range(2):
                    last = mm(bank[4][:, :], wkv[:, b, k, 0:P], ckvT[:, k, :], start=k == 0, stop=k == 1)
                last.then_inc(kn_done, 1)
                pe.wait_ge(qr_ready, H + 1)
                for t in range(T):
                    for k in range(2):
                        last = mm(bank[5][:, t * P:(t + 1) * P], ckvT[:, k, t * P:(t + 1) * P], wkv[:, b, k, P:2 * P],
                                  start=k == 0, stop=k == 1)
                last.then_inc(v_done, 1)

            def scores_mla(H):
                pe.wait_ge(kn_ready, H + 1)
                for qb in range(4):
                    pe.wait_ge(exp_done, 4 * H + qb + 1)
                    mm(bank[qb][:, :], qn[:, qb * P:(qb + 1) * P], kn[:, :], start=True, stop=False)
                    mm(bank[qb][:, :], qr[:, qb * P:(qb + 1) * P], krT[:, :], start=False, stop=True).then_inc(s_done, 1)

            def attend(Hp, b):
                pe.wait_ge(p_ready, Hp + 1)

                def times_v(kt):
                    pe.wait_ge(pT_ready, 4 * Hp + kt + 3)
                    mm(bank[4][:, :], v_sb[:, b, kt, :], pT[:, kt % 2, :], start=kt == 0, stop=kt == 3).then_inc(pv_done, 1)

                for kt in range(4):
                    pe.wait_ge(pT_ready, 4 * Hp + kt + 1)
                    for qb in range(4):
                        last = nc.tensor.transpose(bank[6 + kt % 2][:, qb * P:(qb + 1) * P],
                                                   probs[b][:, qb, kt * P:(kt + 1) * P], ident[:, :])
                    last.then_inc(pT_done, 1)
                    if kt >= 1:
                        times_v(kt - 1)
                times_v(3)

            pe.wait_ge(pro_ready, 7)
            project_mla(0, 0, 1)
            scores_mla(0)
            with pe.Fori(0, 3) as i:
                project_mla(2 * i + 1, 1, i + 1)
                scores_mla(2 * i + 1)
                attend(2 * i, 0)
                project_mla(2 * i + 2, 0, i + 2)
                scores_mla(2 * i + 2)
                attend(2 * i + 1, 1)
            project_mla(7, 1, 4)
            scores_mla(7)
            attend(6, 0)
            with pe.Fori(0, 2) as n:
                for g in range(4):
                    H = 4 * n + g + HM
                    pe.wait_ge(qs_ready, 4 * n + g + 1)
                    pe.wait_ge(o_lo, H + 1)
                    for t in range(T):
                        last = nc.tensor.transpose(bank[4][:, t * P:(t + 1) * P], q_stage[:, t, :], ident[:, :])
                    last.then_inc(qn_done, 1)
                    if g == 0:
                        pe.wait_ge(ks_ready, n + 1)
                        pe.wait_ge(v_ready, HM + 1)
                        for t in range(T):
                            last = nc.tensor.transpose(bank[5][:, t * P:(t + 1) * P], k_stage[:, t, :], ident[:, :])
                        last.then_inc(kn_done, 1)
                        pe.wait_ge(kn_ready, n + HM + 1)
                    pe.wait_ge(qn_ready, H + 1)
                    for qb in range(4):
                        pe.wait_ge(exp_done, 4 * H + qb + 1)
                        mm(bank[qb][:, :], qn[:, qb * P:(qb + 1) * P], kn[:, :], start=True, stop=True).then_inc(s_done, 1)
                    pe.wait_ge(v_ready, H + 1)
                    attend(H - 1, (g + 1) % 2)
            pe.wait_ge(v_ready, HM + HG + 1)
            attend(HM + HG - 1, 1)

            def gate_row(m):
                for q in range(4):
                    pe.wait_ge(diag_ready, 4 * m + q + 1)
                    if q or m:
                        pe.wait_ge(row_ready, 4 * m + q)
                    mm(bank[5][:, :], ones[:, :], diag[:, :, :], start=True, stop=True).then_inc(row_done, 1)

            gate_row(0)
            pe.wait_ge(o_lo, HM + HG + 2)
            with pe.Fori(0, 4) as j:
                dense_block(N_BR + 8 * j, G_BR + 8 * j, 4, 0, oT_hi, oT_lo, True)
                dense_block(N_BR + 4 + 8 * j, G_BR + 4 + 8 * j, 4, 8, oT_hi, oT_lo, True)
            with pe.Fori(0, 4) as j:
                dense_block(N_OUT + 8 * j, G_OUT + 4 * j, 8, 0, mT_hi, mT_lo, False, ready=m_lo)

            gate_row(1)
            pe.wait_ge(xn2_ready, T)
            pe.wait_ge(wr_in, 16)
            pe.wait_ge(acc_free, G_EXP + 4)
            for k in range(KD + 1):
                if k < KD:
                    if k >= 4:
                        pe.wait_ge(h2T_ready, k - 3)
                    elif k == 1:
                        pe.wait_ge(row_ready, 8)
                    for t in range(T):
                        last = nc.tensor.transpose(bank[4 + k % 4][:, t * P:(t + 1) * P], xn[:, t, k * P:(k + 1) * P], ident[:, :])
                    last.then_inc(h2T_done, 1)
                if k >= 1:
                    pe.wait_ge(h2T_ready, k)
                    for t in range(T):
                        last = mm(bank[t][:, 0:NE], h2T[:, (k - 1) % 2, t * P:(t + 1) * P], w_rt[:, k - 1, :],
                                  start=k == 1, stop=k == KD)
                    last.then_inc(logit_done, 1)
            pe.wait_ge(aff_ready, 1)
            for t in range(T):
                last = nc.tensor.transpose(bank[4][0:NE, t * P:(t + 1) * P], aff[:, t, 0:NE], ident[:, :])
            last.then_inc(affT_done, 1)
            pe.wait_ge(slotT_ready, 1)
            for t in range(T):
                last = nc.tensor.transpose(bank[5][:, t * NE:(t + 1) * NE], slotT[:, t * P:(t + 1) * P], ident[0:NE, 0:NE])
            last.then_inc(slots_done, 1)

            def gather(u):
                for i in range(4):
                    for t in range(T):
                        last = mm(bank[4 + u][:, i * P:(i + 1) * P], xn[:, t, (4 * u + i) * P:(4 * u + i + 1) * P],
                                  sel[:, t, :, :], start=t == 0, stop=t == T - 1)
                last.then_inc(gather_done, 1)

            pe.wait_ge(sel_ready, 1)
            for u in range(4):
                gather(u)

            with pe.Fori(0, PAIRS) as p:
                for e in range(2):
                    n0 = N_EXP + 96 * p + 48 * e
                    g0 = G_EXP + 16 * p + 8 * e
                    pe.wait_ge(xg_ready, 4 * p + 4)

                    def expert_chunk(cc, b, first, end, acts):
                        if first:
                            pe.wait_ge(acc_free, g0 + (cc // 8 if cc < 32 else 4 + DOWN[cc - 32][0]) + 1)
                        pe.wait_ge(hi_ready, n0 + cc + 1)
                        for kk in range(2):
                            mm(bank[b][:, :], acts[kk], w_hi[:, cc % 2, kk, :], start=first and kk == 0, stop=False)
                        pe.wait_ge(lo_ready, n0 + cc + 1 + NSTAGE)
                        for kk in range(2):
                            last = mm(bank[b][:, :], acts[kk], w_lo[:, cc % 2, kk, :], start=False, stop=end and kk == 1)
                        last.then_inc(chunk_used, 1)

                    def fold(jb):
                        pe.wait_ge(acc_free, g0 + 2 * jb + 6)
                        for s in range(2):
                            for f in range(4):
                                last = mm(bank[4 + jb][:, s * 256 + f * 64:s * 256 + (f + 1) * 64], gu[:, s, f * P:(f + 1) * P],
                                          foldm[:, :], start=True, stop=True)
                        last.then_inc(fold_done, 1)

                    def scatter(jd):
                        pe.wait_ge(selT_ready, p + 1)
                        pe.wait_ge(ylo_ready, 4 * p + jd + 1)
                        for t in range(T):
                            pe.wait_ge(scat_added, 16 * p + 4 * jd + t + 1)
                            mm(bank[4 + t][:, :], selT[:, t * P:(t + 1) * P], y_hi[:, jd, :], start=True, stop=False)
                            mm(bank[4 + t][:, :], selT[:, t * P:(t + 1) * P], y_lo[:, jd, :], start=False, stop=True)\
                                .then_inc(scat_done, 1)

                    for cc in range(48):
                        if cc < 32:
                            a, c8 = cc // 8, cc % 8
                            expert_chunk(cc, a, c8 == 0, c8 == 7, [xgT[:, 2 * c8 + kk, e, :] for kk in range(2)])
                        else:
                            jd, kc = DOWN[cc - 32]
                            if cc == 32:
                                pe.wait_ge(he_ready, 4 * p + 2 * e + 3)
                            if cc == 36:
                                pe.wait_ge(he_ready, 4 * p + 2 * e + 4)
                            expert_chunk(cc, jd, kc == 0, kc == 3, [heT[:, 2 * kc + kk, :] for kk in range(2)])
                        if cc == 2 and e == 0:
                            pe.wait_ge(scat_added, 16 * p + 4)
                            for t in range(T):
                                last = nc.tensor.transpose(bank[6][:, t * P:(t + 1) * P], sel[:, t, :, :], ident[:, :])
                            last.then_inc(selT_done, 1)
                            for t in range(T):
                                last = mm(bank[7][:, 0:2], sel[:, t, :, :], aff[:, t, ds(2 * p, 2)], start=t == 0, stop=t == T - 1)
                            last.then_inc(val_done, 1)
                        if cc == 18:
                            fold(0)
                        if cc == 33:
                            fold(1)
                        if e == 1:
                            if 36 <= cc < 40:
                                if cc == 36:
                                    pe.wait_ge(sel_ready, p + 2)
                                    pe.wait_ge(selT_ready, p + 1)
                                    pe.wait_ge(val_ready, p + 1)
                                gather(cc - 36)
                            if cc == 41:
                                pe.wait_ge(xg32_ready, 4 * p + 8)
                                scatter(0)
                            if cc == 43:
                                scatter(1)
                            if cc == 46:
                                scatter(2)
                            if cc == 47:
                                scatter(3)

        @block.scalar
        def _(act):
            A = nc.scalar.activation

            def hi(n, c, width=W):
                act.wait_ge(stage_full[c % NSTAGE], 2 * (n - c % NSTAGE) + 16)
                act.wait_ge(chunk_used, n + 1)
                A(w_hi[:, c % NSPLIT, :, 0:width], stage[:, c % NSTAGE, :, 0:width], ACT.Copy).then_inc(hi_ready, 1)

            act.sem_inc(acc_free, 4)
            act.sem_inc(exp_done, 4)
            act.sem_inc(v_ready, 1)
            act.wait_ge(cols_ready, 2)
            A(siluc[:, :], pcol[:, 32:48], ACT.Sigmoid).then_inc(sigc_ready, 1)
            for t in range(T):
                act.wait_ge(x_in, 16 * T)
                if t:
                    act.wait_ge(act_seq, t)
                A(junk[:, :], x_sb[:, t, :], ACT.Square, accum_out=ssq[:, t:t + 1]).then_inc(act_seq, 1)
            act.wait_ge(act_seq, 4)
            A(rstd[:, 0:T], ssq[:, 0:T], ACT.Sqrt, bias=eps_c[:, :], scale=1.0 / D).then_inc(std_ready, 1)
            act.wait_ge(rstd_ready, 1)
            for t in range(T):
                A(x_sb[:, t, :], x_sb[:, t, :], ACT.Copy, scale=rstd[:, 4 + t:5 + t]).then_inc(xn_ready, 1)

            for cc in range(8):
                for k in (2 * cc, 2 * cc + 1):
                    act.wait_ge(h32_ready, k + 1)
                    A(hT_hi[:, k, :], h32[:, k % 4, :], ACT.Copy).then_inc(hT_hi_ready, 1)
                hi(N_Z + cc, cc)

            def latent_block(g, n_next, width_next, col, parts, squares):
                for b in range(4):
                    wait_bank(act, g // 4, b, n_next)
                    w = sum(q for q, _ in parts)
                    A(zc[:, b, col:col + w], bank[b][:, 0:w], ACT.Copy).then_inc(acc_free, 1)
                    if b == 0:
                        hi(n_next, 0, width_next)
                for b in range(4):
                    act.wait_ge(acc_free, g + b + 5)
                    act.wait_ge(act_seq, squares + b)
                    size, stat = parts[0]
                    A(junk[:, 0:size], zc[:, b, col:col + size], ACT.Square, accum_out=zssq[:, stat, b:b + 1]).then_inc(act_seq, 1)

            latent_block(G_Z, N_Z + 8, LAT - QR, 0, [(QR, 12)], 4)
            for cc in range(1, 8):
                hi(N_Z + 8 + cc, cc, LAT - QR)
            latent_block(G_Z + 4, N_Z + 16, W, QR, [(KVR, 13), (ROPE, 15)], 8)
            with act.Fori(0, 3) as j:
                for cc in range(1, 8):
                    hi(N_Z + 16 + 8 * j + cc, cc)
                for b in range(4):
                    wait_bank(act, 2 + j, b, N_Z + 24 + 8 * j)
                    A(zg[:, b, ds(W * j, W)], bank[b][:, :], ACT.Copy).then_inc(acc_free, 1)
                    if b == 0:
                        hi(N_Z + 24 + 8 * j, 0)
                for b in range(4):
                    act.wait_ge(acc_free, G_Z + 8 + 4 * j + b + 5)
                    for i in range(4):
                        act.wait_ge(act_seq, 12 + 16 * j + 4 * b + i)
                        A(junk[:, 0:P], zg[:, b, ds(W * j + P * i, P)], ACT.Square,
                          accum_out=zssq[:, ds(4 * j + i, 1), b]).then_inc(act_seq, 1)
            act.wait_ge(act_seq, 4 + 8 + 48)
            A(zr[:, 0:12, :], zssq[:, 0:12, :], ACT.Sqrt, bias=eps_c[:, :], scale=1.0 / DH)
            A(zr[:, 12, :], zssq[:, 12, :], ACT.Sqrt, bias=eps_c[:, :], scale=1.0 / QR)
            A(zr[:, 13, :], zssq[:, 13, :], ACT.Sqrt, bias=eps_c[:, :], scale=1.0 / KVR).then_inc(zstd_ready, 1)

            with act.Fori(0, 8) as j:
                for cc in range(1, 8):
                    hi(N_GATE + 8 * j + cc, cc)
                for b in range(4):
                    wait_bank(act, G_GATE // 4 + j, b, N_GATE + 8 + 8 * j)
                    act.wait_ge(sig_out[b], 16 * j + 16)
                    A(sig[:, b, :], bank[b][:, :], ACT.Sigmoid).then_inc(acc_free, 1)
                    if b == 0:
                        hi(N_GATE + 8 + 8 * j, 0)
                    act.wait_ge(acc_free, G_GATE + 4 * j + b + 5)
                    act.dma_start(sig_v[:, ds(4 * j + b, 1), :], sig[:, b:b + 1, :]).then_inc(sig_out[b], 16)

            def head_inputs_mla(H, b):
                act.wait_ge(qn_done, H + 1)
                A(qn[:, :], bank[4][:, :], ACT.Copy).then_inc(qn_ready, 1)
                act.wait_ge(kn_done, H + 1)
                A(kn[:, :], bank[4][:, :], ACT.Copy).then_inc(kn_ready, 1)
                act.wait_ge(v_done, H + 1)
                A(v_sb[:, b, :, :], bank[5][:, :].rearrange("p (t d) -> p t d", t=T), ACT.Copy).then_inc(v_ready, 1)

            def exponentials(H, b, scale):
                for qb in range(4):
                    act.wait_ge(nmax_ready, 4 * H + qb + 1)
                    A(probs[b][:, qb, :], bank[qb][:, :], ACT.Exp, bias=nmax[:, b, 4 + qb:5 + qb], scale=scale,
                      accum_out=rsum[:, b, qb:qb + 1]).then_inc(exp_done, 1)

            def output_hi(Hp):
                act.wait_ge(pv_done, 4 * Hp + 6)
                A(oT_hi[:, ds(Hp, 1), :], bank[4][:, :].unsqueeze(1), ACT.Copy).then_inc(o_hi, 1)

            for i in range(4):
                act.wait_ge(sig_out[i], 16 * 9)
            act.wait_ge(pro_ready, 7)
            head_inputs_mla(0, 0)
            exponentials(0, 0, MLA_SCALE)
            with act.Fori(0, 3) as i:
                for b in (1, 0):
                    H = 2 * i + 2 - b
                    head_inputs_mla(H, b)
                    exponentials(H, b, MLA_SCALE)
                    output_hi(H - 1)
            head_inputs_mla(7, 1)
            exponentials(7, 1, MLA_SCALE)
            output_hi(6)
            with act.Fori(0, 2) as n:
                for g in range(4):
                    H = 4 * n + g + HM
                    act.wait_ge(qn_done, H + 1)
                    A(qn[:, :], bank[4][:, :], ACT.Copy).then_inc(qn_ready, 1)
                    if g == 0:
                        act.wait_ge(kn_done, n + HM + 1)
                        A(kn[:, :], bank[5][:, :], ACT.Copy).then_inc(kn_ready, 1)
                    exponentials(H, g % 2, GQA_SCALE)
                    output_hi(H - 1)
            output_hi(HM + HG - 1)

            with act.Fori(0, 4) as j:
                for half in range(2):
                    for cc in range(1, 4):
                        hi(N_BR + 8 * j + 4 * half + cc, 4 * half + cc)
                    hi(N_BR + 8 * j + 4 * half + 4, (4 * half + 4) % 8)
            act.wait_ge(chunk_used, N_OUT + NSPLIT)
            for cc in range(8):
                for k in (2 * cc, 2 * cc + 1):
                    act.wait_ge(mT_ready, k + 1)
                    A(mT_hi[:, k, :], mT[:, k, :], ACT.Copy).then_inc(m_hi, 1)
                if cc:
                    hi(N_OUT + cc, cc)
            with act.Fori(0, 3) as j:
                for cc in range(8):
                    hi(N_OUT + 8 + 8 * j + cc, cc)

            for t in range(T):
                act.wait_ge(x1_ready, 4 * T)
                act.wait_ge(act_seq, 60 + t)
                A(junk2[:, :], x1[:, t, :], ACT.Square, accum_out=ssq[:, 4 + t:5 + t]).then_inc(act_seq, 1)
            act.wait_ge(act_seq, 64)
            A(rstd[:, 8:12], ssq[:, 4:8], ACT.Sqrt, bias=eps_c[:, :], scale=1.0 / D).then_inc(std2_ready, 1)
            act.wait_ge(rstd2_ready, 1)
            for t in range(T):
                A(xn[:, t, :], x1[:, t, :], ACT.Copy, scale=rstd[:, 12 + t:13 + t]).then_inc(xn2_ready, 1)
            act.wait_ge(lsub_ready, 1)
            A(aff[:, :, 0:NE], slots[:, :, 0:NE], ACT.Exp).then_inc(lexp_ready, 1)

            def xg_round(u, count):
                act.wait_ge(xg32_ready, count)
                A(xgT[:, 4 * u:4 * u + 4, :, 0:64], xg32[:, :, :].rearrange("p k (e c) -> p k e c", e=2), ACT.Copy).then_inc(xg_hi, 1)

            for u in range(4):
                xg_round(u, u + 1)
            with act.Fori(0, PAIRS) as p:
                for e in range(2):
                    n0 = N_EXP + 96 * p + 48 * e
                    g0 = G_EXP + 16 * p + 8 * e

                    def gu_copy(a):
                        act.wait_ge(chunk_used, n0 + 8 * a + 8 + NSPLIT)
                        if a >= 2:
                            act.wait_ge(fold_done, 4 * p + 2 * e + 1)
                        else:
                            act.wait_ge(he_ready, 4 * p + 2 * e + 2)
                        A(gu[:, a % 2, :], bank[a][:, :], ACT.Copy).then_inc(acc_free, 1)

                    def sigmoid_gate(jb):
                        act.wait_ge(fold_done, 4 * p + 2 * e + jb + 1)
                        A(sgm[:, :], bank[4 + jb][:, 0:256], ACT.Sigmoid).then_inc(sgm_ready, 1)

                    def he_round(jb):
                        act.wait_ge(he32_ready, 4 * p + 2 * e + jb + 1)
                        A(heT[:, 4 * jb:4 * jb + 4, 0:64], h32e[:, :].rearrange("p (f c) -> p f c", f=4), ACT.Copy).then_inc(he_hi, 1)

                    def y_lower(jd):
                        act.wait_ge(chunk_used, n0 + 33 + DOWN.index((jd, 3)) + NSPLIT)
                        act.wait_ge(acc_free, g0 + jd + 8)
                        A(ytmp[:, :], bank[jd][64:128, :], ACT.Copy).then_inc(ytmp_ready, 1)

                    def y_round(jd):
                        act.wait_ge(y32_ready, 4 * p + jd + 1)
                        A(y_hi[:, jd, :], ysum[:, jd, :], ACT.Copy).then_inc(yhi_ready, 1)

                    for cc in range(48):
                        hi(n0 + cc, cc)
                        if cc == 4 and e == 0:
                            act.wait_ge(selT_done, p + 1)
                            A(selT[:, :], bank[6][:, :], ACT.Copy).then_inc(selT_ready, 1)
                        if cc in (9, 17, 25, 33):
                            gu_copy(cc // 8 - 1)
                        if cc == 20:
                            sigmoid_gate(0)
                        if cc == 22:
                            he_round(0)
                        if cc == 35:
                            sigmoid_gate(1)
                        if cc == 36:
                            he_round(1)
                        if cc in (39, 41, 45, 47):
                            y_lower((39, 41, 45, 47).index(cc))
                        if e == 1:
                            if 39 <= cc < 43:
                                xg_round(cc - 39, 4 * p + 4 + cc - 39 + 1)
                            if cc in (40, 42, 46, 47):
                                y_round((40, 42, 46, 47).index(cc))

            for t in range(T):
                act.wait_ge(scat_added, 4 + 16 * PAIRS)
                act.wait_ge(act_seq, 64 + t)
                A(junk2[:, :], x1[:, t, :], ACT.Square, accum_out=ssq[:, 8 + t:9 + t]).then_inc(act_seq, 1)
                act.wait_ge(act_seq, 64 + t + 1)
                A(ssq[:, 12 + t:13 + t], ssq[:, 8 + t:9 + t], ACT.Sqrt, bias=eps_c[:, :], scale=1.0 / D).then_inc(std3_ready, 1)

        @block.vector
        def _(dve):
            V = nc.vector
            seq = [0]

            def link(ins):
                seq[0] += 1
                ins.then_inc(dve_seq, 1)
                dve.wait_ge(dve_seq, seq[0])

            def lo(n, c, width=W):
                dve.wait_ge(hi_ready, n + 1)
                V.tensor_tensor(w_lo[:, c % NSPLIT, :, 0:width], stage[:, c % NSTAGE, :, 0:width],
                                w_hi[:, c % NSPLIT, :, 0:width].bitcast(F32), ALU.subtract).then_inc(lo_ready, 1)

            dve.sem_inc(lo_ready, NSTAGE)
            dve.sem_inc(ada_done, NADA)
            dve.sem_inc(ada_col_done, 1)
            dve.sem_inc(ada_col_ready, 1)
            dve.sem_inc(o_lo, 2)
            dve.sem_inc(pT_ready, 2)
            dve.sem_inc(pv_done, 2)
            for s in sig_out:
                dve.sem_inc(s, 16)
            dve.sem_inc(he_ready, 2)
            dve.sem_inc(scat_added, 4)
            V.memset(ones[:, :], 1.0)
            V.memset(aff[:, :, NE:NE + 2], 0.0)
            V.memset(eps_c[:, :], EPS)
            dve.wait_ge(cols_done, 1)
            V.tensor_copy(pcol[:, :], bank[5][:, 0:54]).then_inc(cols_ready, 1)
            V.tensor_copy(bcol[:, :], bank[5][:, 64:160]).then_inc(cols_ready, 1)
            dve.wait_ge(sigc_ready, 1)
            V.tensor_tensor(siluc[:, :], siluc[:, :], pcol[:, 32:48], ALU.mult).then_inc(siluc_ready, 1)
            dve.wait_ge(siluc_ready, 1)

            def ada_step(m, k, r, turn):
                dve.wait_ge(ada_full[k % NADA], 16 * turn)
                if k == 0:
                    dve.wait_ge(ada_col_done, r + 1)
                    V.tensor_scalar(ada_acc[:, :], ada_tile[:, 0, :], siluc[:, 0:1], None, ALU.mult).then_inc(ada_done, 1)
                else:
                    dve.wait_ge(ada_done, m + NADA)
                    V.scalar_tensor_tensor(ada_acc[:, :], ada_tile[:, k % NADA, :], siluc[:, k:k + 1], ada_acc[:, :],
                                           ALU.mult, ALU.add).then_inc(ada_done, 1)

            def ada_finish(r):
                dve.wait_ge(ada_col_done, r + 2)
                V.tensor_tensor(modcol[:, ds(8 * r, 8)], bank[4][:, 0:8], bcol[:, ds(8 * r, 8)], ALU.add).then_inc(ada_col_ready, 1)

            with dve.Fori(0, ADA_FIRST) as r:
                for k in range(KD):
                    ada_step(KD * r + k, k, r, 4 * r + k // NADA + 1)
                ada_finish(r)
            dve.wait_ge(std_ready, 1)
            V.reciprocal(rstd[:, 4:8], rstd[:, 0:4]).then_inc(rstd_ready, 1)
            dve.wait_ge(ada_col_ready, ADA_FIRST + 1)
            link(V.scalar_tensor_tensor(a1[:, :], modcol[:, 16:32], 1.0, pcol[:, 0:16], ALU.add, ALU.mult))
            def h_lo(k):
                dve.wait_ge(hT_hi_ready, k + 1)
                V.tensor_tensor(hT_lo[:, k, :], h32[:, k % 4, :], hT_hi[:, k, :].bitcast(F32), ALU.subtract).then_inc(hT_lo_ready, 1)

            for k in range(KD):
                dve.wait_ge(xT_done, k + 1)
                V.tensor_scalar(h32[:, k % 4, :], bank[4 + k % 4][:, :], a1[:, k:k + 1], modcol[:, k:k + 1],
                                ALU.mult, ALU.add).then_inc(h32_ready, 1)
                if k >= 1:
                    h_lo(k - 1)
                if k >= 3 and k % 2:
                    lo(N_Z + k // 2 - 1, k // 2 - 1)
            h_lo(KD - 1)
            lo(N_Z + 7, 7)
            for cc in range(8):
                lo(N_Z + 8 + cc, cc, LAT - QR)
            lo(N_Z + 16, 0)
            with dve.Fori(0, 3) as j:
                for cc in range(1, 9):
                    lo(N_Z + 16 + 8 * j + cc, cc)
            dve.wait_ge(zstd_ready, 1)
            V.reciprocal(zr[:, 0:14, :], zr[:, 0:14, :]).then_inc(zr_ready, 1)
            with dve.Fori(0, 8) as j:
                for cc in range(8):
                    lo(N_GATE + 1 + 8 * j + cc, cc + 1)
                    for k in (2 * cc, 2 * cc + 1):
                        ada_step(KD * (j + ADA_FIRST) + k, k, j + ADA_FIRST, 4 * (j + ADA_FIRST) + k // NADA + 1)
                ada_finish(j + ADA_FIRST)

            for i in range(4):
                dve.wait_ge(sig_out[i], 16 * 9)
            for i in range(7):
                dve.wait_ge(pro_done, i + 1)
                src = bank[4 + i % 4][:, :]
                if i < 4:
                    ins = V.tensor_scalar(cqT[:, i, :], src, pcol[:, 48 + i:49 + i], None, ALU.mult)
                elif i < 6:
                    dve.wait_ge(pro_done, 7)
                    ins = V.tensor_scalar(ckvT[:, i - 4, :], src, pcol[:, 48 + i:49 + i], None, ALU.mult)
                else:
                    ins = V.tensor_copy(krT[:, :], src)
                ins.then_inc(pro_ready, 1)

            def qr_rotate(H):
                dve.wait_ge(qr_done, H + 1)
                V.tensor_tensor(qr[:, :], bank[5][:, :], qtab[:, :], ALU.mult).then_inc(qr_ready, 1)

            def negative_max(H, b, scale):
                for qb in range(4):
                    dve.wait_ge(s_done, 4 * H + qb + 1)
                    V.tensor_reduce(nmax[:, b, qb:qb + 1], bank[qb][:, :], AX.X, ALU.max).then_inc(nmx_seq, 1)
                    dve.wait_ge(nmx_seq, 4 * H + qb + 1)
                    V.tensor_scalar(nmax[:, b, 4 + qb:5 + qb], nmax[:, b, qb:qb + 1], -scale, None, ALU.mult).then_inc(nmax_ready, 1)

            def output_lo(Hp):
                dve.wait_ge(o_hi, Hp + 1)
                V.tensor_tensor(oT_lo[:, ds(Hp, 1), :], bank[4][:, :].unsqueeze(1), oT_hi[:, ds(Hp, 1), :].bitcast(F32),
                                ALU.subtract).then_inc(o_lo, 1)

            def probs_transposed(Hp):
                for kt in range(4):
                    dve.wait_ge(pT_done, 4 * Hp + kt + 1)
                    dve.wait_ge(pv_done, 4 * Hp + kt + 1)
                    V.tensor_copy(pT[:, kt % 2, :], bank[6 + kt % 2][:, :]).then_inc(pT_ready, 1)

            def normalise(H, b):
                dve.wait_ge(exp_done, 4 * H + 8)
                V.reciprocal(rsum[:, b, 4:8], rsum[:, b, 0:4]).then_inc(rinv_seq, 1)
                dve.wait_ge(rinv_seq, H + 1)
                for qb in range(4):
                    last = V.tensor_scalar(probs[b][:, qb, :], probs[b][:, qb, :], rsum[:, b, 4 + qb:5 + qb], None, ALU.mult)
                last.then_inc(p_ready, 1)

            qr_rotate(0)
            negative_max(0, 0, MLA_SCALE)
            normalise(0, 0)
            with dve.Fori(0, 3) as i:
                for b in (1, 0):
                    H = 2 * i + 2 - b
                    qr_rotate(H)
                    negative_max(H, b, MLA_SCALE)
                    probs_transposed(H - 1)
                    output_lo(H - 1)
                    normalise(H, b)
            qr_rotate(7)
            negative_max(7, 1, MLA_SCALE)
            probs_transposed(6)
            output_lo(6)
            normalise(7, 1)
            with dve.Fori(0, 2) as n:
                for g in range(4):
                    H = 4 * n + g + HM
                    negative_max(H, g % 2, GQA_SCALE)
                    probs_transposed(H - 1)
                    output_lo(H - 1)
                    normalise(H, g % 2)
            probs_transposed(HM + HG - 1)
            output_lo(HM + HG - 1)

            def gate_row(m, col):
                for q in range(4):
                    if q or m:
                        dve.wait_ge(row_done, 4 * m + q)
                    V.tensor_tensor(diag[:, :, :], ident[:, :].unsqueeze(1).broadcast_to([P, 4, P]),
                                    modcol[:, col + 4 * q:col + 4 * q + 4].unsqueeze(2).broadcast_to([P, 4, P]),
                                    ALU.mult).then_inc(diag_ready, 1)
                    dve.wait_ge(row_done, 4 * m + q + 1)
                    V.tensor_copy(gt_row[:, q * W:(q + 1) * W], bank[5][:, :]).then_inc(row_ready, 1)

            gate_row(0, 32)
            with dve.Fori(0, 4) as j:
                for half in range(2):
                    n0 = N_BR + 8 * j + 4 * half
                    g0 = G_BR + 8 * j + 4 * half
                    for cc in range(1, 4):
                        lo(n0 + cc, 4 * half + cc)
                    dve.wait_ge(sg_full[half], 16 * j + 16)
                    for b in range(4):
                        wait_bank(dve, G_BR // 4 + 2 * j + half, b, n0 + 4)
                        m_b = mT[:, ds(4 * j + b, 1), :]
                        gate = sg_in[:, half, b:b + 1, :]
                        prod = bank[b][:, :].unsqueeze(1)
                        if half == 0:
                            V.tensor_tensor(m_b, prod, gate, ALU.mult).then_inc(acc_free, 1)
                        else:
                            V.tensor_tensor(m_tmp[:, :].unsqueeze(1), prod, gate, ALU.mult).then_inc(acc_free, 1)
                            dve.wait_ge(acc_free, g0 + b + 5)
                            V.tensor_tensor(m_b, m_b, m_tmp[:, :].unsqueeze(1), ALU.add).then_inc(mT_ready, 1)
                            dve.wait_ge(mT_ready, 4 * j + b + 1)
                        if b == 0:
                            lo(n0 + 4, (4 * half + 4) % 8)
            for k in range(KD):
                dve.wait_ge(m_hi, k + 1)
                V.tensor_tensor(mT_lo[:, k, :], mT[:, k, :], mT_hi[:, k, :].bitcast(F32), ALU.subtract).then_inc(m_lo, 1)
                if k >= 3 and k % 2:
                    lo(N_OUT + k // 2, k // 2)

            def add_out(j, n_next):
                for b in range(4):
                    wait_bank(dve, G_OUT // 4 + j, b, N_OUT + 8 * j + 8)
                    V.tensor_tensor(m_tmp[:, :], bank[b][:, :], gt_row[:, ds(W * j, W)], ALU.mult).then_inc(acc_free, 1)
                    dve.wait_ge(acc_free, G_OUT + 4 * j + b + 5)
                    V.tensor_tensor(x1[:, b, ds(W * j, W)], x1[:, b, ds(W * j, W)], m_tmp[:, :], ALU.add).then_inc(x1_ready, 1)
                    dve.wait_ge(x1_ready, 4 * j + b + 1)
                    if b == 0 and n_next is not None:
                        lo(n_next, 0)

            dve.wait_ge(x1_in, 16 * T)
            add_out(0, N_OUT + 8)
            with dve.Fori(1, 3) as j:
                for cc in range(1, 8):
                    lo(N_OUT + 8 * j + cc, cc)
                add_out(j, N_OUT + 8 + 8 * j)
            for cc in range(1, 8):
                lo(N_OUT + 24 + cc, cc)
            add_out(3, None)

            dve.wait_ge(x1_ready, 16)
            gate_row(1, 80)
            dve.wait_ge(std2_ready, 1)
            V.reciprocal(rstd[:, 12:16], rstd[:, 8:12]).then_inc(rstd2_ready, 1)
            link(V.scalar_tensor_tensor(a1[:, :], modcol[:, 64:80], 1.0, pcol[:, 16:32], ALU.add, ALU.mult))
            for k in range(KD):
                dve.wait_ge(h2T_done, k + 1)
                if k >= 2:
                    dve.wait_ge(logit_done, k - 1)
                V.tensor_scalar(h2T[:, k % 2, :], bank[4 + k % 4][:, :], a1[:, k:k + 1], modcol[:, 48 + k:49 + k],
                                ALU.mult, ALU.add).then_inc(h2T_ready, 1)
            dve.wait_ge(logit_done, KD)
            for t in range(T):
                last = V.tensor_copy(slots[:, t, 0:NE], bank[t][:, 0:NE])
            link(last)
            link(V.tensor_reduce(lmx[:, 0:4], slots[:, :, 0:NE], AX.X, ALU.max))
            V.tensor_tensor(slots[:, :, 0:NE], slots[:, :, 0:NE], lmx[:, 0:4].unsqueeze(2).broadcast_to([P, T, NE]),
                            ALU.subtract).then_inc(lsub_ready, 1)
            dve.wait_ge(lexp_ready, 1)
            link(V.tensor_reduce(lmx[:, 4:8], aff[:, :, 0:NE], AX.X, ALU.add))
            link(V.reciprocal(lmx[:, 0:4], lmx[:, 4:8]))
            V.tensor_tensor(aff[:, :, 0:NE], aff[:, :, 0:NE], lmx[:, 0:4].unsqueeze(2).broadcast_to([P, T, NE]),
                            ALU.mult).then_inc(aff_ready, 1)
            dve.wait_ge(affT_done, 1)
            link(V.tensor_copy(affT[:, :], bank[4][0:NE, :]))
            src = affT[:, :]
            for i in range(CAP // 8):
                link(V.max(m8[:, :], src))
                if i < CAP // 8 - 1:
                    link(V.match_replace(work[:, i % 2, :], m8[:, :], src, -1.0))
                    src = work[:, i % 2, :]
            link(V.tensor_scalar(gt_m[:, :], affT[:, :], m8[:, 7:8], 0.0, ALU.is_gt, ALU.add, accum_out=cnt[:, 0:1]))
            link(V.tensor_scalar(cnt[:, 1:2], cnt[:, 0:1], -1.0, float(CAP), ALU.mult, ALU.add))
            link(V.tensor_scalar(eq_m[:, :], affT[:, :], m8[:, 7:8], None, ALU.is_equal))
            link(V.tensor_tensor_scan(rank[:, :], eq_m[:, :], eq_m[:, :], 0.0, ALU.add, ALU.bypass))
            link(V.scalar_tensor_tensor(eq_m[:, :], rank[:, :], cnt[:, 1:2], eq_m[:, :], ALU.is_le, ALU.mult))
            link(V.tensor_tensor(gt_m[:, :], gt_m[:, :], eq_m[:, :], ALU.add))
            link(V.tensor_tensor_scan(rank[:, :], gt_m[:, :], gt_m[:, :], 0.0, ALU.add, ALU.bypass))
            link(V.tensor_tensor(rank[:, :], rank[:, :], gt_m[:, :], ALU.mult))
            V.tensor_scalar(slotT[:, :], rank[:, :], -1.0, None, ALU.add).then_inc(slotT_ready, 1)
            V.memset(slots[:, :, NE:NE + 2], -1.0)
            dve.wait_ge(slots_done, 1)
            link(V.tensor_copy(slots[:, :, 0:NE], bank[5][:, 0:T * NE].rearrange("p (t e) -> p t e", t=T)))

            def select(p):
                for t in range(T):
                    last = V.tensor_tensor(sel[:, t, :, :], iota[:, :].unsqueeze(1).broadcast_to([P, 2, CAP]),
                                           slots[:, t, ds(2 * p, 2)].unsqueeze(2).broadcast_to([P, 2, CAP]), ALU.is_equal)
                last.then_inc(sel_ready, 1)

            def modulate(u, count):
                dve.wait_ge(gather_done, count)
                if not isinstance(count, int) or count > 1:
                    dve.wait_ge(xg_ready, count - 1)
                for i in range(4):
                    k = 4 * u + i
                    last = V.tensor_scalar(xg32[:, i, :], bank[4 + u][:, i * P:(i + 1) * P], a1[:, k:k + 1], modcol[:, 48 + k:49 + k],
                                           ALU.mult, ALU.add)
                last.then_inc(xg32_ready, 1)

            def xg_lo(u, count):
                dve.wait_ge(xg_hi, count)
                V.tensor_tensor(xgT[:, 4 * u:4 * u + 4, :, 64:128], xg32[:, :, :].rearrange("p k (e c) -> p k e c", e=2),
                                xgT[:, 4 * u:4 * u + 4, :, 0:64].bitcast(F32), ALU.subtract).then_inc(xg_ready, 1)

            select(0)
            for u in range(4):
                modulate(u, u + 1)
                xg_lo(u, u + 1)
            with dve.Fori(0, PAIRS) as p:
                for e in range(2):
                    n0 = N_EXP + 96 * p + 48 * e
                    g0 = G_EXP + 16 * p + 8 * e

                    def swiglu(jb):
                        dve.wait_ge(sgm_ready, 4 * p + 2 * e + jb + 1)
                        dve.wait_ge(he_ready, 4 * p + 2 * e + jb + 2)
                        V.tensor_tensor(h32e[:, :], bank[4 + jb][:, 0:256], sgm[:, :], ALU.mult).then_inc(he_mid, 1)
                        dve.wait_ge(he_mid, 4 * p + 2 * e + jb + 1)
                        V.tensor_tensor(h32e[:, :], bank[4 + jb][:, 256:512], h32e[:, :], ALU.mult).then_inc(he32_ready, 1)

                    def he_lo(jb):
                        dve.wait_ge(he_hi, 4 * p + 2 * e + jb + 1)
                        V.tensor_tensor(heT[:, 4 * jb:4 * jb + 4, 64:128], h32e[:, :].rearrange("p (f c) -> p f c", f=4),
                                        heT[:, 4 * jb:4 * jb + 4, 0:64].bitcast(F32), ALU.subtract).then_inc(he_ready, 1)

                    def y_add(jd):
                        dve.wait_ge(ytmp_ready, 8 * p + 4 * e + jd + 1)
                        V.tensor_tensor(ysum[64 * e:64 * e + 64, jd, :], bank[jd][0:64, :], ytmp[:, :], ALU.add)\
                            .then_inc(acc_free, 1)
                        if e == 1:
                            dve.wait_ge(acc_free, g0 + jd + 9)
                            if jd == 0:
                                dve.wait_ge(val_ready, p + 1)
                            V.scalar_tensor_tensor(ysum[:, jd, :], ysum[:, jd, :], val[:, 0:1], gt_row[:, jd * W:(jd + 1) * W],
                                                   ALU.mult, ALU.mult).then_inc(y32_ready, 1)

                    def y_lo_part(jd):
                        dve.wait_ge(yhi_ready, 4 * p + jd + 1)
                        V.tensor_tensor(y_lo[:, jd, :], ysum[:, jd, :], y_hi[:, jd, :].bitcast(F32), ALU.subtract).then_inc(ylo_ready, 1)

                    def add_scattered(jd):
                        for t in range(T):
                            dve.wait_ge(scat_done, 16 * p + 4 * jd + t + 1)
                            V.tensor_tensor(x1[:, t, jd * W:(jd + 1) * W], x1[:, t, jd * W:(jd + 1) * W], bank[4 + t][:, :],
                                            ALU.add).then_inc(scat_added, 1)

                    for cc in range(48):
                        lo(n0 + cc, cc)
                        if cc == 4 and e == 0:
                            dve.wait_ge(val_done, p + 1)
                            V.tensor_copy(val[0:64, :], bank[7][0:64, 0:1])
                            V.tensor_copy(val[64:128, :], bank[7][64:128, 1:2]).then_inc(val_ready, 1)
                        if cc == 20:
                            swiglu(0)
                        if cc == 22:
                            he_lo(0)
                        if cc == 35:
                            swiglu(1)
                        if cc == 36:
                            he_lo(1)
                        if e == 1 and cc == 34:
                            dve.wait_ge(selT_ready, p + 1)
                            select(p + 1)
                        if cc in (39, 41, 45, 47):
                            y_add((39, 41, 45, 47).index(cc))
                        if e == 1:
                            if 39 <= cc < 43:
                                xg_lo(cc - 39, 4 * p + 4 + cc - 39 + 1)
                            if 38 <= cc < 42:
                                modulate(cc - 38, 4 * p + 4 + cc - 38 + 1)
                            if cc in (40, 42, 46, 47):
                                y_lo_part((40, 42, 46, 47).index(cc))
                            if cc == 43:
                                add_scattered(0)
                            if cc == 45:
                                add_scattered(1)
                            if cc == 47:
                                add_scattered(2)
                                add_scattered(3)

            dve.wait_ge(gf_in, 16)
            for t in range(T):
                dve.wait_ge(std3_ready, t + 1)
                if t >= 2:
                    dve.wait_ge(stored[t % 2], 16 * (t // 2))
                link(V.reciprocal(rstd[:, t:t + 1], ssq[:, 12 + t:13 + t]))
                V.scalar_tensor_tensor(res[:, t % 2, :], x1[:, t, :], rstd[:, t:t + 1], gf_row[:, :], ALU.mult, ALU.mult)\
                    .then_inc(res_ready, 1)

        @block.gpsimd
        def _(pool):
            G = nc.gpsimd
            seq = [0]

            def link(ins):
                seq[0] += 1
                ins.then_inc(pool_seq, 1)
                pool.wait_ge(pool_seq, seq[0])

            pool.wait_ge(cols_done, 1)
            pool.wait_ge(h32_ready, KD)
            pool.wait_ge(zr_ready, 1)
            loads = [(rope_kc[:, :, :], consts[:, C_KC:C_KS]), (rope_ks[:, :, :], consts[:, C_KS:C_GC]),
                     (rope_gc[:, :, :, :], consts[:, C_GC:C_GS]), (rope_gs[:, :, :, :], consts[:, C_GS:C_END])]
            for dst, src in loads[:2]:
                pool.dma_start(dst, src.rearrange("p (t f) -> p t f", t=T)).then_inc(tab_in, 16)
            for dst, src in loads[2:]:
                pool.dma_start(dst, src.rearrange("p (t h f) -> p t h f", t=T, h=2)).then_inc(tab_in, 16)
            for h in range(HG + KVG):
                g = g_qn if h < HG else g_kn
                pool.dma_start(g_row[:, h, :], g[0].partition_broadcast(P)).then_inc(tab_in, 16)
            pool.wait_ge(tab_in, 16 * (4 + HG + KVG))
            for t in range(T):
                G.tensor_scalar(zc[:, t, 0:QR], zc[:, t, 0:QR], zr[:, 12, t:t + 1], None, ALU.mult)
                G.tensor_scalar(zc[:, t, QR:QR + KVR], zc[:, t, QR:QR + KVR], zr[:, 13, t:t + 1], None, ALU.mult)
            kr1, kr_2 = zc[:, :, 768:800], zc[:, :, 800:832]
            ta, tb = r_a[:, 0:4, 0, :], r_b[:, 0:4, 0, :]
            tc_, td = r_c[:, 0:4, 0, :], r_d[:, 0:4, 0, :]
            G.tensor_tensor(ta, kr1, rope_kc[:, :, :], ALU.mult)
            G.tensor_tensor(tb, kr_2, rope_ks[:, :, :], ALU.mult)
            G.tensor_tensor(tc_, kr1, rope_ks[:, :, :], ALU.mult)
            link(G.tensor_tensor(td, kr_2, rope_kc[:, :, :], ALU.mult))
            for o in (0, 64):
                G.tensor_tensor(kr2[:, :, o:o + 32], ta, tb, ALU.subtract)
                ins = G.tensor_tensor(kr2[:, :, o + 32:o + 64], tc_, td, ALU.add)
            link(ins)
            NH = HG + KVG
            for t in range(T):
                z4 = zg[:, t, 0:NH * DH].rearrange("p (h d) -> p h d", h=NH)
                z5 = zg[:, t, 0:NH * DH].rearrange("p (h r d) -> p h r d", h=NH, r=2)
                x1_, x2_ = z5[:, :, :, 0:32], z5[:, :, :, 32:64]
                cos = rope_gc[:, t, :, :].unsqueeze(1).broadcast_to([P, NH, 2, 32])
                sin = rope_gs[:, t, :, :].unsqueeze(1).broadcast_to([P, NH, 2, 32])
                link(G.tensor_tensor(z4, z4, zr[:, 0:NH, t].unsqueeze(2).broadcast_to([P, NH, DH]), ALU.mult))
                link(G.tensor_tensor(z4, z4, g_row[:, :, :], ALU.mult))
                G.tensor_tensor(r_a[:, :, :, :], x1_, cos, ALU.mult)
                G.tensor_tensor(r_b[:, :, :, :], x2_, sin, ALU.mult)
                G.tensor_tensor(r_c[:, :, :, :], x1_, sin, ALU.mult)
                link(G.tensor_tensor(r_d[:, :, :, :], x2_, cos, ALU.mult))
                G.tensor_tensor(x1_, r_a[:, :, :, :], r_b[:, :, :, :], ALU.subtract)
                ins = G.tensor_tensor(x2_, r_c[:, :, :, :], r_d[:, :, :, :], ALU.add)
                if t < T - 1:
                    link(ins)
                else:
                    ins.then_inc(zpost_ready, 1)
            pool.wait_ge(zpost_ready, 1)
            for h in range(HG):
                H = HM + h
                pool.wait_ge(qn_done, H)
                if h % 4 == 0:
                    pool.wait_ge(v_done, HM)
                    pool.wait_ge(kn_done, h // 4 + HM)
                    k_head = (HG + h // 4) * DH
                    G.tensor_copy(k_stage[:, :, :], zg[:, :, k_head:k_head + DH]).then_inc(ks_ready, 1)
                G.tensor_copy(q_stage[:, :, :], zg[:, :, h * DH:(h + 1) * DH]).then_inc(qs_ready, 1)
                pool.wait_ge(pv_done, 4 * H - 2)
                v_head = (HG + KVG + h // 4) * DH
                G.tensor_copy(v_sb[:, h % 2, :, :], zg[:, :, v_head:v_head + DH]).then_inc(v_ready, 1)


_INS = ["x", "c", "w_ada", "b_ada", "g_mix", "w_in", "g_cq", "g_ckv", "w_uq", "w_ukv", "g_qn", "g_kn",
        "w_br_a", "w_br_b", "w_out", "g_ffn", "w_router", "w_e_gate", "w_e_up", "w_e_down", "g_final"]


def kernel(**inputs):
    import numpy as _np
    import concourse.bacc as _bacc
    from concourse import mybir as _mybir
    from concourse.bass_utils import run_bass_kernel_spmd as _run

    nc = _bacc.Bacc("TRN2", target_bir_lowering=False, num_devices=1)
    arrays, args = {}, []
    for name in _INS:
        a = _np.ascontiguousarray(inputs[name])
        arrays[f"in_{name}"] = a
        args.append(nc.dram_tensor(f"in_{name}", a.shape, _mybir.dt.from_np(a.dtype), kind="ExternalInput").ap())
    k = shape_constants()
    arrays["in_consts"] = k
    args.append(nc.dram_tensor("in_consts", k.shape, _mybir.dt.float32, kind="ExternalInput").ap())
    args.append(nc.dram_tensor("sig_gates", (2 * D, S), _mybir.dt.float32, kind="Internal").ap())
    args.append(nc.dram_tensor("out_0", (1, S, D), _mybir.dt.float32, kind="ExternalOutput").ap())
    encoder_block(nc, *args)
    r = _run(nc, [arrays], core_ids=[0])
    return r.results[0]["out_0"]
```

```python
import math
from contextlib import ExitStack

import numpy as np
import concourse.bass as bass
from concourse import mybir

P = 128
D = 2048
S = 512
T = S // P
KD = D // P
QR, KVR, ROPE, DH = 512, 256, 64, 128
HM, HG, KVG = 8, 8, 2
LAT = QR + KVR + ROPE
GQ = (HG + 2 * KVG) * DH
NE, FF = 16, 1024
CAP = 2 * S // NE
W = 512
EPS = 1e-6
MLA_SCALE = float(DH + ROPE) ** -0.5
GQA_SCALE = float(DH) ** -0.5
NSTAGE, NSPLIT = 8, 2
ADA_W, NADA = 1024, 4
ADA_BLOCKS = 6 * D // ADA_W
ADA_FIRST = 2 * D // ADA_W
N_Z, N_GATE = 0, 40
N_BR = N_GATE + 64
N_OUT = N_BR + 32
N_EXP = N_OUT + 32
G_Z, G_GATE = 0, 20
G_BR = G_GATE + 32
G_OUT = G_BR + 32
G_EXP = G_OUT + 16
PAIRS = NE // 2
DOWN = [(j, k) for j in range(3) for k in (0, 1)] + [(j, k) for j in range(3) for k in (2, 3)] + [(3, k) for k in range(4)]
RAW_SLOTS = (2, 5, 7)
SPLIT_CC = [cc for cc in range(-NSTAGE, 48) if cc % NSTAGE not in RAW_SLOTS]
SPLIT_PER_EXPERT = sum(cc >= 0 for cc in SPLIT_CC)


def split_index(cc):
    return SPLIT_CC.index(cc) - SPLIT_CC.index(0)
C_ID, C_FOLD, C_IOTA, C_QTAB = 0, 128, 192, 256
C_KC, C_KS, C_GC, C_GS, C_END = 768, 896, 1024, 1280, 1536


def shape_constants():
    half = ROPE // 2
    freqs = (np.float32(10000.0) ** (-np.arange(half, dtype=np.float32) / np.float32(half))).astype(np.float32)

    def tables(pos):
        a = pos.astype(np.float32)[:, None] * freqs[None, :]
        return np.cos(a).astype(np.float32), np.sin(a).astype(np.float32)

    t = np.arange(S)
    c1, s1 = tables(t)
    cr, sr = tables(t // 64)
    cc, sc = tables(t % 64)
    k = np.zeros((P, C_END), np.float32)
    k[:, C_ID:C_ID + P] = np.eye(P)
    k[:, C_FOLD:C_FOLD + 64] = np.concatenate([np.eye(64), np.eye(64)])
    k[:, C_IOTA:C_IOTA + 64] = np.arange(64)[None, :]
    k[:, C_QTAB:C_QTAB + S] = np.concatenate([c1.T, c1.T, -s1.T, s1.T])

    def by_tile(a):
        return a.reshape(T, P, -1).transpose(1, 0, 2).reshape(P, -1)

    k[:, C_KC:C_KS] = by_tile(c1)
    k[:, C_KS:C_GC] = by_tile(s1)
    k[:, C_GC:C_GS] = by_tile(np.concatenate([cr, cc], 1))
    k[:, C_GS:C_END] = by_tile(np.concatenate([sr, sc], 1))
    return k


def encoder_block(nc, x, c, w_ada, b_ada, g_mix, w_in, g_cq, g_ckv, w_uq, w_ukv, g_qn, g_kn,
                  w_br_a, w_br_b, w_out, g_ffn, w_router, w_e_gate, w_e_up, w_e_down, g_final,
                  consts, sig_gates, out):
    F32, F32R = mybir.dt.float32, mybir.dt.float32r
    ALU, ACT, AX = mybir.AluOpType, mybir.ActivationFunctionType, mybir.AxisListType
    ds = bass.ds

    x_v = x[0].rearrange("(t p) d -> p t d", p=P)
    out_v = out[0].rearrange("(t p) d -> p t d", p=P)
    w_ada_v = w_ada[0].rearrange("(k p) n -> p k n", p=P)
    w_in_v = w_in[0].rearrange("(k p) n -> p k n", p=P)
    w_uq_v = w_uq[0].rearrange("(k p) n -> p k n", p=P)
    w_ukv_v = w_ukv[0].rearrange("(k p) n -> p k n", p=P)
    w_bra_v = w_br_a[0].rearrange("(k p) n -> p k n", p=P)
    w_brb_v = w_br_b[0].rearrange("(k p) n -> p k n", p=P)
    w_out_v = w_out[0].rearrange("(k p) n -> p k n", p=P)
    w_router_v = w_router[0].rearrange("(k p) n -> p k n", p=P)
    w_gate_v = w_e_gate[0].rearrange("e (k p) n -> e p k n", p=P)
    w_up_v = w_e_up[0].rearrange("e (k p) n -> e p k n", p=P)
    w_down_v = w_e_down[0].rearrange("e (k p) n -> e p k n", p=P)
    sig_v = sig_gates.rearrange("(m p) s -> p m s", p=P)

    ctx = ExitStack()
    with ctx:
        KB = 1024
        sizes = {"ring": 48 * KB, "ada": 20 * KB, "A": 64 * KB, "B": 37 * KB, "C": 32 * KB, "small": 6 * KB + 512}
        arena_at = (nc.sbuf_base + 31) // 32 * 32
        ctx.enter_context(nc.sbuf_tensor("arena", [P, sum(sizes.values()) // 4], F32))
        start = arena_at
        base = {}
        for name, size in sizes.items():
            base[name] = start
            start += size

        def at(region, offset, name, shape, dt=F32):
            size = 4 * math.prod(shape[1:])
            assert offset + size <= sizes[region], (name, offset, size)
            return nc.alloc_sbuf_tensor_at(name, shape, dt, offset=base[region] + offset)

        stage = at("ring", 0, "stage", [P, NSTAGE, 2, W])
        w_hi = at("ring", 32 * KB, "w_hi", [P, NSPLIT, 2, W], F32R)
        w_lo = at("ring", 40 * KB, "w_lo", [P, NSPLIT, 2, W], F32R)
        ada_tile = at("ada", 0, "ada_tile", [P, NADA, ADA_W])
        ada_acc = at("ada", 16 * KB, "ada_acc", [P, ADA_W])
        wq = at("ada", 0, "wq", [P, 2, 4, 256])
        wkv = at("ada", 8 * KB, "wkv", [P, 2, 2, 256])
        q_stage = at("ada", 0, "q_stage", [P, T, DH])
        k_stage = at("ada", 2 * KB, "k_stage", [P, T, DH])
        cqT = at("ada", 12 * KB, "cqT", [P, 4, S])
        gt_row = at("ada", 0, "gt_row", [P, D])
        sel = at("ada", 8 * KB, "sel", [P, T, 2, CAP])
        selT = at("ada", 10 * KB, "selT", [P, S], F32R)
        gu = at("ada", 12 * KB, "gu", [P, 2, W])
        sgm = at("ada", 16 * KB, "sgm", [P, 256])
        h32e = at("ada", 17 * KB, "h32e", [P, 256])
        xg32 = at("ada", 18 * KB, "xg32", [P, 4, P])
        h2T = at("ada", 12 * KB, "h2T", [P, 2, S])
        w_rt = at("ada", 16 * KB, "w_rt", [P, KD, NE])
        hT_hi = at("A", 0, "hT_hi", [P, KD, S], F32R)
        hT_lo = at("A", 32 * KB, "hT_lo", [P, KD, S], F32R)
        oT_hi = at("A", 0, "oT_hi", [P, KD, S], F32R)
        oT_lo = at("A", 32 * KB, "oT_lo", [P, KD, S], F32R)
        mT_hi = at("A", 0, "mT_hi", [P, KD, S], F32R)
        mT_lo = at("A", 32 * KB, "mT_lo", [P, KD, S], F32R)
        xgT = [at("A", 0, "xgT0", [P, KD, 2, P], F32R), at("A", 48 * KB, "xgT1", [P, KD, 2, P], F32R)]
        heT = at("A", 16 * KB, "heT", [P, 8, P], F32R)
        ysum = at("A", 24 * KB, "ysum", [P, 4, W])
        y_hi = at("A", 32 * KB, "y_hi", [P, 4, W], F32R)
        y_lo = at("A", 40 * KB, "y_lo", [P, 4, W], F32R)
        ytmp = at("A", 20 * KB, "ytmp", [64, W])
        junk2 = at("A", 50 * KB, "junk2", [P, D])
        affT = at("A", 20 * KB, "affT", [NE, S])
        work = at("A", 22 * KB, "work", [NE, 2, S])
        gt_m = at("A", 26 * KB, "gt_m", [NE, S])
        eq_m = at("A", 28 * KB, "eq_m", [NE, S])
        rank = at("A", 30 * KB, "rank", [NE, S])
        slotT = at("A", 58 * KB, "slotT", [NE, S])
        res = at("A", 0, "res", [P, 2, D])
        x_sb = at("B", 0, "x_sb", [P, T, D])
        zc = at("B", 0, "zc", [P, T, LAT])
        zg = at("B", 13 * KB, "zg", [P, T, GQ])
        mT = at("B", 0, "mT", [P, KD, S])
        x1 = at("B", 0, "x1", [P, T, D])
        probs1 = at("B", 0, "probs1", [P, T, S])
        h32 = at("C", 0, "h32", [P, 4, S])
        junk = at("C", 8 * KB, "junk", [P, D])
        sig = at("C", 0, "sig", [P, 4, S])
        g_row = at("C", 16 * KB, "g_row", [P, HG + KVG, DH])
        rope_kc = at("C", 21 * KB, "rope_kc", [P, T, 32])
        rope_ks = at("C", 21 * KB + 512, "rope_ks", [P, T, 32])
        rope_gc = at("C", 22 * KB, "rope_gc", [P, T, 2, 32])
        rope_gs = at("C", 23 * KB, "rope_gs", [P, T, 2, 32])
        NR = (HG + KVG) * 2 * 32
        r_a = at("C", 8 * KB, "r_a", [P, HG + KVG, 2, 32])
        r_b = at("C", 8 * KB + 4 * NR, "r_b", [P, HG + KVG, 2, 32])
        r_c = at("C", 24 * KB, "r_c", [P, HG + KVG, 2, 32])
        r_d = at("C", 24 * KB + 4 * NR, "r_d", [P, HG + KVG, 2, 32])
        kr2 = at("C", 30 * KB, "kr2", [P, T, P])
        probs0 = at("C", 0, "probs0", [P, T, S])
        pT = at("C", 8 * KB, "pT", [P, 2, S])
        qn = at("C", 12 * KB, "qn", [P, S])
        qr = at("C", 14 * KB, "qr", [P, S])
        kn = at("C", 16 * KB, "kn", [P, S])
        v_sb = at("C", 18 * KB, "v_sb", [P, 2, T, DH])
        krT = at("C", 22 * KB, "krT", [P, S])
        ckvT = at("C", 24 * KB, "ckvT", [P, 2, S])
        sg_in = at("C", 0, "sg_in", [P, 2, 4, S])
        m_tmp = at("C", 16 * KB, "m_tmp", [P, S])
        diag = at("C", 18 * KB, "diag", [P, 4, P])
        xn = at("C", 0, "xn", [P, T, D])
        gf_row = at("C", 0, "gf_row", [P, D])
        probs = [probs0, probs1]

        small_at = [0]

        def small(name, shape, dt=F32):
            o = small_at[0]
            small_at[0] += (4 * math.prod(shape[1:]) + 31) // 32 * 32
            return at("small", o, name, shape, dt)

        ident = small("ident", [P, P])
        foldm = small("foldm", [P, 64])
        iota = small("iota", [P, 64])
        qtab = small("qtab", [P, S])
        ones = small("ones", [P, P])
        modcol = small("modcol", [P, 96])
        bcol = small("bcol", [P, 96])
        pcol = small("pcol", [P, 54])
        siluc = small("siluc", [P, 16])
        a1 = small("a1", [P, KD])
        ssq = small("ssq", [P, 16])
        rstd = small("rstd", [P, 16])
        zssq = small("zssq", [P, 16, T])
        zr = small("zr", [P, 16, T])
        eps_c = small("eps_c", [P, 1])
        nmax = small("nmax", [P, 2, 8])
        rsum = small("rsum", [P, 2, 8])
        aff = small("aff", [P, T, NE + 2])
        slots = small("slots", [P, T, NE + 2])
        lmx = small("lmx", [P, 8])
        val = small("val", [P, 1])
        m8 = small("m8", [NE, 8])
        cnt = small("cnt", [NE, 2])
        prow = at("C", 24 * KB, "prow", [54, P])
        brow = at("C", 26 * KB, "brow", [96, P])

        bank = [ctx.enter_context(nc.psum_tensor(f"bank{i}", [P, W], F32)) for i in range(8)]

        def sem(name):
            return ctx.enter_context(nc.semaphore(name))

        stage_full = [sem(f"stage_full{i}") for i in range(NSTAGE)]
        hi_ready, lo_ready, chunk_used = sem("hi_ready"), sem("lo_ready"), sem("chunk_used")
        acc_done, acc_free = sem("acc_done"), sem("acc_free")
        consts_in, x_in, rows_in = sem("consts_in"), sem("x_in"), sem("rows_in")
        cols_done, cols_ready, sigc_ready, siluc_ready = sem("cols_done"), sem("cols_ready"), sem("sigc_ready"), sem("siluc_ready")
        ada_full = [sem(f"ada_full{i}") for i in range(NADA)]
        ada_done, ada_col_done, ada_col_ready = sem("ada_done"), sem("ada_col_done"), sem("ada_col_ready")
        act_seq, dve_seq, pool_seq = sem("act_seq"), sem("dve_seq"), sem("pool_seq")
        std_ready, rstd_ready, xn_ready = sem("std_ready"), sem("rstd_ready"), sem("xn_ready")
        xT_done, h32_ready, hT_hi_ready, hT_lo_ready = sem("xT_done"), sem("h32_ready"), sem("hT_hi_ready"), sem("hT_lo_ready")
        tab_in = sem("tab_in")
        zstd_ready, zr_ready, zpost_ready = sem("zstd_ready"), sem("zr_ready"), sem("zpost_ready")
        sig_out = [sem(f"sig_out{i}") for i in range(4)]
        pro_done, pro_ready = sem("pro_done"), sem("pro_ready")
        hw_full = [sem("hw_full0"), sem("hw_full1")]
        qn_done, qr_done, kn_done, v_done = sem("qn_done"), sem("qr_done"), sem("kn_done"), sem("v_done")
        qn_ready, qr_ready, kn_ready, v_ready = sem("qn_ready"), sem("qr_ready"), sem("kn_ready"), sem("v_ready")
        qs_ready, ks_ready = sem("qs_ready"), sem("ks_ready")
        s_done, nmax_ready, exp_done, p_ready = sem("s_done"), sem("nmax_ready"), sem("exp_done"), sem("p_ready")
        nmx_seq, rinv_seq = sem("nmx_seq"), sem("rinv_seq")
        pT_done, pT_ready, pv_done, o_hi, o_lo = sem("pT_done"), sem("pT_ready"), sem("pv_done"), sem("o_hi"), sem("o_lo")
        sg_full = [sem("sg_full0"), sem("sg_full1")]
        diag_ready, row_done, row_ready = sem("diag_ready"), sem("row_done"), sem("row_ready")
        mT_ready, m_hi, m_lo, x1_in, x1_ready = sem("mT_ready"), sem("m_hi"), sem("m_lo"), sem("x1_in"), sem("x1_ready")
        wr_in, std2_ready, rstd2_ready, xn2_ready = sem("wr_in"), sem("std2_ready"), sem("rstd2_ready"), sem("xn2_ready")
        h2T_done, h2T_ready, logit_done = sem("h2T_done"), sem("h2T_ready"), sem("logit_done")
        lsub_ready, lexp_ready, aff_ready, affT_done, slotT_ready, slots_done = (
            sem("lsub_ready"), sem("lexp_ready"), sem("aff_ready"), sem("affT_done"), sem("slotT_ready"), sem("slots_done"))
        sel_ready, selT_done, selT_ready, val_done, val_ready = sem("sel_ready"), sem("selT_done"), sem("selT_ready"), sem("val_done"), sem("val_ready")
        gather_done, xg32_ready, xg_hi, xg_ready = sem("gather_done"), sem("xg32_ready"), sem("xg_hi"), sem("xg_ready")
        fold_done, sgm_ready, he32_ready, he_hi, he_ready = (
            sem("fold_done"), sem("sgm_ready"), sem("he32_ready"), sem("he_hi"), sem("he_ready"))
        he_mid = sem("he_mid")
        ytmp_ready, y32_ready, yhi_ready, ylo_ready = sem("ytmp_ready"), sem("y32_ready"), sem("yhi_ready"), sem("ylo_ready")
        scat_done, scat_added = sem("scat_done"), sem("scat_added")
        gf_in, std3_ready, rstd3_ready, res_ready = sem("gf_in"), sem("std3_ready"), sem("rstd3_ready"), sem("res_ready")
        stored = [sem("stored0"), sem("stored1")]

        block = ctx.enter_context(nc.Block())

        def wait_bank(eng, blk, b, n_end):
            if b < 3:
                eng.wait_ge(acc_done, 3 * blk + b + 1)
            else:
                eng.wait_ge(chunk_used, n_end + NSPLIT)

        @block.sync
        def _(sp):
            def load_chunk(n, c, src):
                sp.wait_ge(lo_ready, n + 1)
                width = src.shape[2]
                sp.dma_start(stage[:, c % NSTAGE, :, 0:width], src).then_inc(stage_full[c % NSTAGE], 16)

            def load_ada(m, k, r):
                sp.wait_ge(ada_done, m + 1)
                sp.dma_start(ada_tile[:, k % NADA, :], w_ada_v[:, k, ds(r * ADA_W, ADA_W)]).then_inc(ada_full[k % NADA], 16)

            for row, n, src in ((0, 16, g_mix[0]), (16, 16, g_ffn[0]), (32, 16, c[0]), (48, 4, g_cq[0]), (52, 2, g_ckv[0])):
                sp.dma_start(prow[row:row + n, :], src.rearrange("(k p) -> k p", p=P)).then_inc(rows_in, 16)
            sp.dma_start(brow[:, :], b_ada[0].rearrange("(k p) -> k p", p=P)).then_inc(rows_in, 16)
            for dst, a, b in ((ident, C_ID, C_FOLD), (foldm, C_FOLD, C_IOTA), (iota, C_IOTA, C_QTAB), (qtab, C_QTAB, C_KC)):
                sp.dma_start(dst[:, :], consts[:, a:b]).then_inc(consts_in, 16)
            for t in range(T):
                sp.dma_start(x_sb[:, t, :], x_v[:, t, :]).then_inc(x_in, 16)
            with sp.Fori(0, ADA_FIRST) as r:
                for k in range(KD):
                    load_ada(KD * r + k, k, r)
            for c8 in range(8):
                load_chunk(N_Z + c8, c8, w_in_v[:, 2 * c8:2 * c8 + 2, 0:QR])
            for c8 in range(8):
                load_chunk(N_Z + 8 + c8, c8, w_in_v[:, 2 * c8:2 * c8 + 2, QR:LAT])
            with sp.Fori(0, 3) as j:
                for c8 in range(8):
                    load_chunk(N_Z + 16 + 8 * j + c8, c8, w_in_v[:, 2 * c8:2 * c8 + 2, ds(LAT + W * j, W)])
            with sp.Fori(0, 8) as j:
                for c8 in range(8):
                    load_chunk(N_GATE + 8 * j + c8, c8, w_in_v[:, 2 * c8:2 * c8 + 2, ds(LAT + GQ + W * j, W)])
                    for k in (2 * c8, 2 * c8 + 1):
                        load_ada(KD * (j + ADA_FIRST) + k, k, j + ADA_FIRST)

            def head_weights(b, H):
                sp.dma_start(wq[:, b, :, 0:192], w_uq_v[:, :, ds(H * 192, 192)]).then_inc(hw_full[b], 16)
                sp.dma_start(wq[:, b, :, 192:224], w_uq_v[:, :, ds(H * 192 + 160, 32)]).then_inc(hw_full[b], 16)
                sp.dma_start(wq[:, b, :, 224:256], w_uq_v[:, :, ds(H * 192 + 128, 32)]).then_inc(hw_full[b], 16)
                sp.dma_start(wkv[:, b, :, :], w_ukv_v[:, :, ds(H * 256, 256)]).then_inc(hw_full[b], 16)

            for c4 in range(4):
                load_chunk(N_BR + c4, c4, w_bra_v[:, 2 * c4:2 * c4 + 2, 0:W])
            for c4 in range(4):
                load_chunk(N_BR + 4 + c4, 4 + c4, w_brb_v[:, 2 * c4:2 * c4 + 2, 0:W])
            sp.wait_ge(ada_done, NADA + KD * ADA_BLOCKS)
            head_weights(0, 0)
            head_weights(1, 1)
            with sp.Fori(0, 3) as i:
                for b in range(2):
                    sp.wait_ge(v_done, 2 * i + b + 1)
                    head_weights(b, 2 * i + 2 + b)

            def load_gates(ab, j):
                sp.dma_start(sg_in[:, ab, :, :], sig_v[:, ds(KD * ab + 4 * j, 4), :]).then_inc(sg_full[ab], 16)

            for i in range(4):
                sp.wait_ge(sig_out[i], 16 * 9)
            sp.wait_ge(o_lo, 2 + HM + HG)
            load_gates(0, 0)
            load_gates(1, 0)
            with sp.Fori(1, 4) as j:
                for c4 in range(4):
                    load_chunk(N_BR + 8 * j + c4, c4, w_bra_v[:, 2 * c4:2 * c4 + 2, ds(W * j, W)])
                sp.wait_ge(acc_free, G_BR + 8 * j)
                load_gates(0, j)
                for c4 in range(4):
                    load_chunk(N_BR + 8 * j + 4 + c4, 4 + c4, w_brb_v[:, 2 * c4:2 * c4 + 2, ds(W * j, W)])
                sp.wait_ge(acc_free, G_BR + 8 * j + 4)
                load_gates(1, j)
            for c8 in range(8):
                load_chunk(N_OUT + c8, c8, w_out_v[:, 2 * c8:2 * c8 + 2, 0:W])
            sp.wait_ge(m_lo, KD)
            for t in range(T):
                sp.dma_start(x1[:, t, :], x_v[:, t, :]).then_inc(x1_in, 16)
            with sp.Fori(1, 4) as j:
                for c8 in range(8):
                    load_chunk(N_OUT + 8 * j + c8, c8, w_out_v[:, 2 * c8:2 * c8 + 2, ds(W * j, W)])
            sp.dma_start(w_rt[:, :, :], w_router_v).then_inc(wr_in, 16)
            def load_expert_chunk(p, e, cc, src):
                n, c = N_EXP + 96 * p + 48 * e + cc, cc % NSTAGE
                before = cc - NSTAGE
                if c in RAW_SLOTS:
                    sp.wait_ge(chunk_used, n - NSTAGE + 1 + NSPLIT)
                else:
                    sp.wait_ge(lo_ready, N_EXP + SPLIT_PER_EXPERT * (2 * p + e) + split_index(before) + 1 + NSTAGE)
                sp.dma_start(stage[:, c, :, :], src).then_inc(stage_full[c], 16)

            def load_pair(p, first):
                for e in range(2):
                    for cc in range(48):
                        if cc < 32:
                            a, c8 = cc // 8, cc % 8
                            w_v, jb, k0 = (w_gate_v, w_up_v)[a % 2], a // 2, 2 * c8
                        else:
                            w_v, (jb, kc) = w_down_v, DOWN[cc - 32]
                            k0 = 2 * kc
                        src = w_v[2 * p + e][:, k0:k0 + 2, jb * W:(jb + 1) * W]
                        if first and e == 0 and cc < NSTAGE:
                            load_chunk(N_EXP + cc, cc, src)
                        else:
                            load_expert_chunk(p, e, cc, src)

            load_pair(0, True)
            with sp.Fori(1, PAIRS) as p:
                load_pair(p, False)
            sp.wait_ge(xg_ready, 4 * PAIRS)
            sp.dma_start(gf_row[:, :], g_final.partition_broadcast(P)).then_inc(gf_in, 16)
            for t in range(T):
                sp.wait_ge(res_ready, t + 1)
                sp.dma_start(out_v[:, t, :], res[:, t % 2, :]).then_inc(stored[t % 2], 16)
            for i in range(2):
                sp.wait_ge(stored[i], 16 * T // 2)

        @block.tensor
        def _(pe):
            mm = nc.tensor.matmul
            pe.sem_inc(chunk_used, NSPLIT)
            pe.wait_ge(rows_in, 16 * 6)
            pe.wait_ge(consts_in, 16 * 4)
            nc.tensor.transpose(bank[5][:, 0:54], prow[:, :], ident[0:54, 0:54])
            nc.tensor.transpose(bank[5][:, 64:160], brow[:, :], ident[0:96, 0:96]).then_inc(cols_done, 1)

            def ada_columns(r):
                pe.wait_ge(ada_done, KD * r + KD + NADA)
                pe.wait_ge(ada_col_ready, r + 1)
                for i in range(8):
                    last = mm(bank[4][:, i:i + 1], ada_acc[:, i * P:(i + 1) * P], ones[:, 0:1], start=True, stop=True)
                last.then_inc(ada_col_done, 1)

            with pe.Fori(0, ADA_FIRST) as r:
                ada_columns(r)

            def dense_block(n0, g0, chunks, k0, act_hi, act_lo, weights_stationary, width=W, ready=None, before=None):
                for cc in range(chunks):
                    if before is not None:
                        before(cc)
                    if ready is not None:
                        pe.wait_ge(ready, 2 * cc + 2)
                    pe.wait_ge(hi_ready, n0 + cc + 1)
                    s = (k0 // 2 + cc) % NSPLIT
                    for b in range(4):
                        if cc == 0:
                            pe.wait_ge(acc_free, g0 + b + 1)
                        passes = [(act_hi, w_hi), (act_lo, w_hi), (act_hi, w_lo)]
                        for i, (a, w) in enumerate(passes):
                            if b == 0 and i == 2:
                                pe.wait_ge(lo_ready, n0 + cc + 1 + NSTAGE)
                            for kk in range(2):
                                first = cc == 0 and i == 0 and kk == 0
                                end = cc == chunks - 1 and i == 2 and kk == 1
                                k = 2 * cc + kk + k0
                                if weights_stationary:
                                    last = mm(bank[b][:, :], w[:, s, kk, b * P:(b + 1) * P], a[:, k, :], start=first, stop=end)
                                else:
                                    last = mm(bank[b][:, 0:width], a[:, k, b * P:(b + 1) * P], w[:, s, kk, 0:width], start=first, stop=end)
                        if b == 3:
                            last.then_inc(chunk_used, 1)
                        elif cc == chunks - 1:
                            last.then_inc(acc_done, 1)

            pe.wait_ge(xn_ready, T)
            pe.wait_ge(ada_col_ready, ADA_FIRST + 1)
            def transpose_x(k):
                if k >= 4:
                    pe.wait_ge(h32_ready, k - 3)
                for t in range(T):
                    last = nc.tensor.transpose(bank[4 + k % 4][:, t * P:(t + 1) * P], x_sb[:, t, k * P:(k + 1) * P], ident[:, :])
                last.then_inc(xT_done, 1)

            for k in range(4):
                transpose_x(k)

            def transposes_ahead(cc):
                for k in (2 * cc + 4, 2 * cc + 5):
                    if k < KD:
                        transpose_x(k)

            dense_block(N_Z, G_Z, 8, 0, hT_hi, hT_lo, False, ready=hT_lo_ready, before=transposes_ahead)
            dense_block(N_Z + 8, G_Z + 4, 8, 0, hT_hi, hT_lo, False, width=LAT - QR)
            with pe.Fori(0, 3) as j:
                dense_block(N_Z + 16 + 8 * j, G_Z + 8 + 4 * j, 8, 0, hT_hi, hT_lo, False)
            with pe.Fori(0, 8) as j:
                dense_block(N_GATE + 8 * j, G_GATE + 4 * j, 8, 0, hT_hi, hT_lo, True)
                ada_columns(j + ADA_FIRST)

            pe.wait_ge(zpost_ready, 1)
            pe.wait_ge(ada_col_ready, ADA_BLOCKS + 1)
            for i in range(7):
                if i >= 4:
                    pe.wait_ge(pro_ready, i - 3)
                for t in range(T):
                    src = kr2[:, t, :] if i == 6 else zc[:, t, i * P:(i + 1) * P]
                    last = nc.tensor.transpose(bank[4 + i % 4][:, t * P:(t + 1) * P], src, ident[:, :])
                last.then_inc(pro_done, 1)

            def project_mla(H, b, use):
                pe.wait_ge(hw_full[b], 64 * use)
                pe.wait_ge(o_lo, H + 1)
                for k in range(4):
                    last = mm(bank[4][:, :], wq[:, b, k, 0:P], cqT[:, k, :], start=k == 0, stop=k == 3)
                last.then_inc(qn_done, 1)
                pe.wait_ge(v_ready, H + 1)
                for k in range(4):
                    last = mm(bank[5][:, :], wq[:, b, k, P:2 * P], cqT[:, k, :], start=k == 0, stop=k == 3)
                last.then_inc(qr_done, 1)
                pe.wait_ge(qn_ready, H + 1)
                for k in range(2):
                    last = mm(bank[4][:, :], wkv[:, b, k, 0:P], ckvT[:, k, :], start=k == 0, stop=k == 1)
                last.then_inc(kn_done, 1)
                pe.wait_ge(qr_ready, H + 1)
                for t in range(T):
                    for k in range(2):
                        last = mm(bank[5][:, t * P:(t + 1) * P], ckvT[:, k, t * P:(t + 1) * P], wkv[:, b, k, P:2 * P],
                                  start=k == 0, stop=k == 1)
                last.then_inc(v_done, 1)

            def scores_mla(H):
                pe.wait_ge(kn_ready, H + 1)
                for qb in range(4):
                    pe.wait_ge(exp_done, 4 * H + qb + 1)
                    mm(bank[qb][:, :], qn[:, qb * P:(qb + 1) * P], kn[:, :], start=True, stop=False)
                    mm(bank[qb][:, :], qr[:, qb * P:(qb + 1) * P], krT[:, :], start=False, stop=True).then_inc(s_done, 1)

            def attend(Hp, b):
                pe.wait_ge(p_ready, Hp + 1)

                def times_v(kt):
                    pe.wait_ge(pT_ready, 4 * Hp + kt + 3)
                    mm(bank[4][:, :], v_sb[:, b, kt, :], pT[:, kt % 2, :], start=kt == 0, stop=kt == 3).then_inc(pv_done, 1)

                for kt in range(4):
                    pe.wait_ge(pT_ready, 4 * Hp + kt + 1)
                    for qb in range(4):
                        last = nc.tensor.transpose(bank[6 + kt % 2][:, qb * P:(qb + 1) * P],
                                                   probs[b][:, qb, kt * P:(kt + 1) * P], ident[:, :])
                    last.then_inc(pT_done, 1)
                    if kt >= 1:
                        times_v(kt - 1)
                times_v(3)

            pe.wait_ge(pro_ready, 7)
            project_mla(0, 0, 1)
            scores_mla(0)
            with pe.Fori(0, 3) as i:
                project_mla(2 * i + 1, 1, i + 1)
                scores_mla(2 * i + 1)
                attend(2 * i, 0)
                project_mla(2 * i + 2, 0, i + 2)
                scores_mla(2 * i + 2)
                attend(2 * i + 1, 1)
            project_mla(7, 1, 4)
            scores_mla(7)
            attend(6, 0)
            with pe.Fori(0, 2) as n:
                for g in range(4):
                    H = 4 * n + g + HM
                    pe.wait_ge(qs_ready, 4 * n + g + 1)
                    pe.wait_ge(o_lo, H + 1)
                    for t in range(T):
                        last = nc.tensor.transpose(bank[4][:, t * P:(t + 1) * P], q_stage[:, t, :], ident[:, :])
                    last.then_inc(qn_done, 1)
                    if g == 0:
                        pe.wait_ge(ks_ready, n + 1)
                        pe.wait_ge(v_ready, HM + 1)
                        for t in range(T):
                            last = nc.tensor.transpose(bank[5][:, t * P:(t + 1) * P], k_stage[:, t, :], ident[:, :])
                        last.then_inc(kn_done, 1)
                        pe.wait_ge(kn_ready, n + HM + 1)
                    pe.wait_ge(qn_ready, H + 1)
                    for qb in range(4):
                        pe.wait_ge(exp_done, 4 * H + qb + 1)
                        mm(bank[qb][:, :], qn[:, qb * P:(qb + 1) * P], kn[:, :], start=True, stop=True).then_inc(s_done, 1)
                    pe.wait_ge(v_ready, H + 1)
                    attend(H - 1, (g + 1) % 2)
            pe.wait_ge(v_ready, HM + HG + 1)
            attend(HM + HG - 1, 1)

            def gate_row(m):
                for q in range(4):
                    pe.wait_ge(diag_ready, 4 * m + q + 1)
                    if q or m:
                        pe.wait_ge(row_ready, 4 * m + q)
                    mm(bank[5][:, :], ones[:, :], diag[:, :, :], start=True, stop=True).then_inc(row_done, 1)

            gate_row(0)
            pe.wait_ge(o_lo, HM + HG + 2)
            with pe.Fori(0, 4) as j:
                dense_block(N_BR + 8 * j, G_BR + 8 * j, 4, 0, oT_hi, oT_lo, True)
                dense_block(N_BR + 4 + 8 * j, G_BR + 4 + 8 * j, 4, 8, oT_hi, oT_lo, True)
            with pe.Fori(0, 4) as j:
                dense_block(N_OUT + 8 * j, G_OUT + 4 * j, 8, 0, mT_hi, mT_lo, False, ready=m_lo)

            gate_row(1)
            pe.wait_ge(xn2_ready, T)
            pe.wait_ge(wr_in, 16)
            pe.wait_ge(acc_free, G_EXP + 4)
            for k in range(KD + 1):
                if k < KD:
                    if k >= 4:
                        pe.wait_ge(h2T_ready, k - 3)
                    elif k == 1:
                        pe.wait_ge(row_ready, 8)
                    for t in range(T):
                        last = nc.tensor.transpose(bank[4 + k % 4][:, t * P:(t + 1) * P], xn[:, t, k * P:(k + 1) * P], ident[:, :])
                    last.then_inc(h2T_done, 1)
                if k >= 1:
                    pe.wait_ge(h2T_ready, k)
                    for t in range(T):
                        last = mm(bank[t][:, 0:NE], h2T[:, (k - 1) % 2, t * P:(t + 1) * P], w_rt[:, k - 1, :],
                                  start=k == 1, stop=k == KD)
                    last.then_inc(logit_done, 1)
            pe.wait_ge(aff_ready, 1)
            for t in range(T):
                last = nc.tensor.transpose(bank[4][0:NE, t * P:(t + 1) * P], aff[:, t, 0:NE], ident[:, :])
            last.then_inc(affT_done, 1)
            pe.wait_ge(slotT_ready, 1)
            for t in range(T):
                last = nc.tensor.transpose(bank[5][:, t * NE:(t + 1) * NE], slotT[:, t * P:(t + 1) * P], ident[0:NE, 0:NE])
            last.then_inc(slots_done, 1)

            def gather(b, u, tiles=range(4)):
                for i in tiles:
                    for t in range(T):
                        last = mm(bank[b][:, i * P:(i + 1) * P], xn[:, t, (4 * u + i) * P:(4 * u + i + 1) * P],
                                  sel[:, t, :, :], start=t == 0, stop=t == T - 1)
                if 3 in tiles:
                    last.then_inc(gather_done, 1)

            def scatter(p, jd):
                pe.wait_ge(ylo_ready, 4 * p + jd + 1)
                for t in range(T):
                    pe.wait_ge(scat_added, 16 * p + 4 * jd + t + 1)
                    mm(bank[4 + t][:, :], selT[:, t * P:(t + 1) * P], y_hi[:, jd, :], start=True, stop=False)
                    mm(bank[4 + t][:, :], selT[:, t * P:(t + 1) * P], y_lo[:, jd, :], start=False, stop=True)\
                        .then_inc(scat_done, 1)

            def expert_chunk(p, e, cc, b, first, end, acts):
                c = cc % NSTAGE
                if first:
                    g0 = G_EXP + 16 * p + 8 * e
                    pe.wait_ge(acc_free, g0 + (cc // 8 if cc < 32 else 4 + DOWN[cc - 32][0]) + 1)
                if c in RAW_SLOTS:
                    pe.wait_ge(stage_full[c], 2 * (N_EXP + 96 * p + 48 * e + cc - c) + 16)
                    for kk in range(2):
                        last = mm(bank[b][:, :], acts[kk].bitcast(F32), stage[:, c, kk, :], start=first and kk == 0, stop=end and kk == 1)
                else:
                    k = N_EXP + SPLIT_PER_EXPERT * (2 * p + e) + split_index(cc)
                    s = split_index(cc) % NSPLIT
                    pe.wait_ge(hi_ready, k + 1)
                    for kk in range(2):
                        mm(bank[b][:, :], acts[kk], w_hi[:, s, kk, :], start=first and kk == 0, stop=False)
                    pe.wait_ge(lo_ready, k + 1 + NSTAGE)
                    for kk in range(2):
                        last = mm(bank[b][:, :], acts[kk], w_lo[:, s, kk, :], start=False, stop=end and kk == 1)
                last.then_inc(chunk_used, 1)

            def fold(p, e, jb):
                pe.wait_ge(acc_free, G_EXP + 16 * p + 8 * e + 2 * jb + 6)
                if jb == 0 and e == 0:
                    pe.wait_ge(scat_added, 16 * p + 4)
                for s in range(2):
                    for f in range(4):
                        last = mm(bank[4][:, s * 256 + f * 64:s * 256 + (f + 1) * 64], gu[:, s, f * P:(f + 1) * P],
                                  foldm[:, :], start=True, stop=True)
                last.then_inc(fold_done, 1)

            def pe_pair(p, turn, first, last_pair):
                for e in range(2):
                    for cc in range(48):
                        if cc == 0 and e == 0:
                            pe.wait_ge(xg_ready, 4 * p + 4)
                        if cc < 32:
                            a, c8 = cc // 8, cc % 8
                            expert_chunk(p, e, cc, a, c8 == 0, c8 == 7, [xgT[turn][:, 2 * c8 + kk, e, :] for kk in range(2)])
                        else:
                            jd, kc = DOWN[cc - 32]
                            if cc == 32:
                                pe.wait_ge(he_ready, 4 * p + 2 * e + 3)
                            if cc == 38:
                                pe.wait_ge(he_ready, 4 * p + 2 * e + 4)
                            expert_chunk(p, e, cc, jd, kc == 0, kc == 3, [heT[:, 2 * kc + kk, :] for kk in range(2)])
                        if cc == 18:
                            fold(p, e, 0)
                        if cc == 33:
                            fold(p, e, 1)
                        if e == 0:
                            if not first and cc in (3, 7, 11, 15):
                                scatter(p - 1, cc // 4)
                            if cc == 22:
                                pe.wait_ge(scat_added, 16 * p + 4)
                                for t in range(T):
                                    last = nc.tensor.transpose(bank[6][:, t * P:(t + 1) * P], sel[:, t, :, :], ident[:, :])
                                last.then_inc(selT_done, 1)
                                for t in range(T):
                                    last = mm(bank[7][:, 0:2], sel[:, t, :, :], aff[:, t, ds(2 * p, 2)], start=t == 0, stop=t == T - 1)
                                last.then_inc(val_done, 1)
                        elif not last_pair:
                            if cc < 32 and cc % 8 in (0, 1, 3, 4):
                                u, i = cc // 8, (0, 1, 3, 4).index(cc % 8)
                                if cc == 0:
                                    pe.wait_ge(sel_ready, p + 2)
                                if i == 0:
                                    pe.wait_ge(xg32_ready, 4 * p + 4 + u)
                                gather(5, u, [i])
                        else:
                            if cc == 40:
                                pe.wait_ge(he32_ready, 4 * p + 4)
                                pe.wait_ge(selT_ready, p + 1)
                            if cc in (43, 45, 47):
                                scatter(p, (cc - 43) // 2)
                    if e == 0:
                        pe.wait_ge(selT_ready, p + 1)
                        pe.wait_ge(val_ready, p + 1)
                if last_pair:
                    scatter(p, 3)

            pe.wait_ge(sel_ready, 1)
            for u in range(4):
                gather(4 + u, u)
            pe_pair(0, 0, True, False)
            with pe.Fori(0, PAIRS // 2 - 1) as i:
                for turn in (1, 0):
                    pe_pair(2 * i + 2 - turn, turn, False, False)
            pe_pair(PAIRS - 1, 1, False, True)

        @block.scalar
        def _(act):
            A = nc.scalar.activation

            def hi(n, c, width=W):
                act.wait_ge(stage_full[c % NSTAGE], 2 * (n - c % NSTAGE) + 16)
                act.wait_ge(chunk_used, n + 1)
                A(w_hi[:, c % NSPLIT, :, 0:width], stage[:, c % NSTAGE, :, 0:width], ACT.Copy).then_inc(hi_ready, 1)

            act.sem_inc(acc_free, 4)
            act.sem_inc(exp_done, 4)
            act.sem_inc(v_ready, 1)
            act.wait_ge(cols_ready, 2)
            A(siluc[:, :], pcol[:, 32:48], ACT.Sigmoid).then_inc(sigc_ready, 1)
            for t in range(T):
                act.wait_ge(x_in, 16 * T)
                if t:
                    act.wait_ge(act_seq, t)
                A(junk[:, :], x_sb[:, t, :], ACT.Square, accum_out=ssq[:, t:t + 1]).then_inc(act_seq, 1)
            act.wait_ge(act_seq, 4)
            A(rstd[:, 0:T], ssq[:, 0:T], ACT.Sqrt, bias=eps_c[:, :], scale=1.0 / D).then_inc(std_ready, 1)
            act.wait_ge(rstd_ready, 1)
            for t in range(T):
                A(x_sb[:, t, :], x_sb[:, t, :], ACT.Copy, scale=rstd[:, 4 + t:5 + t]).then_inc(xn_ready, 1)

            for cc in range(8):
                for k in (2 * cc, 2 * cc + 1):
                    act.wait_ge(h32_ready, k + 1)
                    A(hT_hi[:, k, :], h32[:, k % 4, :], ACT.Copy).then_inc(hT_hi_ready, 1)
                hi(N_Z + cc, cc)

            def latent_block(g, n_next, width_next, col, parts, squares):
                for b in range(4):
                    wait_bank(act, g // 4, b, n_next)
                    w = sum(q for q, _ in parts)
                    A(zc[:, b, col:col + w], bank[b][:, 0:w], ACT.Copy).then_inc(acc_free, 1)
                    if b == 0:
                        hi(n_next, 0, width_next)
                for b in range(4):
                    act.wait_ge(acc_free, g + b + 5)
                    act.wait_ge(act_seq, squares + b)
                    size, stat = parts[0]
                    A(junk[:, 0:size], zc[:, b, col:col + size], ACT.Square, accum_out=zssq[:, stat, b:b + 1]).then_inc(act_seq, 1)

            latent_block(G_Z, N_Z + 8, LAT - QR, 0, [(QR, 12)], 4)
            for cc in range(1, 8):
                hi(N_Z + 8 + cc, cc, LAT - QR)
            latent_block(G_Z + 4, N_Z + 16, W, QR, [(KVR, 13), (ROPE, 15)], 8)
            with act.Fori(0, 3) as j:
                for cc in range(1, 8):
                    hi(N_Z + 16 + 8 * j + cc, cc)
                for b in range(4):
                    wait_bank(act, 2 + j, b, N_Z + 24 + 8 * j)
                    A(zg[:, b, ds(W * j, W)], bank[b][:, :], ACT.Copy).then_inc(acc_free, 1)
                    if b == 0:
                        hi(N_Z + 24 + 8 * j, 0)
                for b in range(4):
                    act.wait_ge(acc_free, G_Z + 8 + 4 * j + b + 5)
                    for i in range(4):
                        act.wait_ge(act_seq, 12 + 16 * j + 4 * b + i)
                        A(junk[:, 0:P], zg[:, b, ds(W * j + P * i, P)], ACT.Square,
                          accum_out=zssq[:, ds(4 * j + i, 1), b]).then_inc(act_seq, 1)
            act.wait_ge(act_seq, 4 + 8 + 48)
            A(zr[:, 0:12, :], zssq[:, 0:12, :], ACT.Sqrt, bias=eps_c[:, :], scale=1.0 / DH)
            A(zr[:, 12, :], zssq[:, 12, :], ACT.Sqrt, bias=eps_c[:, :], scale=1.0 / QR)
            A(zr[:, 13, :], zssq[:, 13, :], ACT.Sqrt, bias=eps_c[:, :], scale=1.0 / KVR).then_inc(zstd_ready, 1)

            with act.Fori(0, 8) as j:
                for cc in range(1, 8):
                    hi(N_GATE + 8 * j + cc, cc)
                for b in range(4):
                    wait_bank(act, G_GATE // 4 + j, b, N_GATE + 8 + 8 * j)
                    act.wait_ge(sig_out[b], 16 * j + 16)
                    A(sig[:, b, :], bank[b][:, :], ACT.Sigmoid).then_inc(acc_free, 1)
                    if b == 0:
                        hi(N_GATE + 8 + 8 * j, 0)
                    act.wait_ge(acc_free, G_GATE + 4 * j + b + 5)
                    act.dma_start(sig_v[:, ds(4 * j + b, 1), :], sig[:, b:b + 1, :]).then_inc(sig_out[b], 16)

            def head_inputs_mla(H, b):
                act.wait_ge(qn_done, H + 1)
                A(qn[:, :], bank[4][:, :], ACT.Copy).then_inc(qn_ready, 1)
                act.wait_ge(kn_done, H + 1)
                A(kn[:, :], bank[4][:, :], ACT.Copy).then_inc(kn_ready, 1)
                act.wait_ge(v_done, H + 1)
                A(v_sb[:, b, :, :], bank[5][:, :].rearrange("p (t d) -> p t d", t=T), ACT.Copy).then_inc(v_ready, 1)

            def exponentials(H, b, scale):
                for qb in range(4):
                    act.wait_ge(nmax_ready, 4 * H + qb + 1)
                    A(probs[b][:, qb, :], bank[qb][:, :], ACT.Exp, bias=nmax[:, b, 4 + qb:5 + qb], scale=scale,
                      accum_out=rsum[:, b, qb:qb + 1]).then_inc(exp_done, 1)

            def output_hi(Hp):
                act.wait_ge(pv_done, 4 * Hp + 6)
                A(oT_hi[:, ds(Hp, 1), :], bank[4][:, :].unsqueeze(1), ACT.Copy).then_inc(o_hi, 1)

            for i in range(4):
                act.wait_ge(sig_out[i], 16 * 9)
            act.wait_ge(pro_ready, 7)
            head_inputs_mla(0, 0)
            exponentials(0, 0, MLA_SCALE)
            with act.Fori(0, 3) as i:
                for b in (1, 0):
                    H = 2 * i + 2 - b
                    head_inputs_mla(H, b)
                    exponentials(H, b, MLA_SCALE)
                    output_hi(H - 1)
            head_inputs_mla(7, 1)
            exponentials(7, 1, MLA_SCALE)
            output_hi(6)
            with act.Fori(0, 2) as n:
                for g in range(4):
                    H = 4 * n + g + HM
                    act.wait_ge(qn_done, H + 1)
                    A(qn[:, :], bank[4][:, :], ACT.Copy).then_inc(qn_ready, 1)
                    if g == 0:
                        act.wait_ge(kn_done, n + HM + 1)
                        A(kn[:, :], bank[5][:, :], ACT.Copy).then_inc(kn_ready, 1)
                    exponentials(H, g % 2, GQA_SCALE)
                    output_hi(H - 1)
            output_hi(HM + HG - 1)

            with act.Fori(0, 4) as j:
                for half in range(2):
                    for cc in range(1, 4):
                        hi(N_BR + 8 * j + 4 * half + cc, 4 * half + cc)
                    hi(N_BR + 8 * j + 4 * half + 4, (4 * half + 4) % 8)
            act.wait_ge(chunk_used, N_OUT + NSPLIT)
            for cc in range(8):
                for k in (2 * cc, 2 * cc + 1):
                    act.wait_ge(mT_ready, k + 1)
                    A(mT_hi[:, k, :], mT[:, k, :], ACT.Copy).then_inc(m_hi, 1)
                if cc:
                    hi(N_OUT + cc, cc)
            with act.Fori(0, 3) as j:
                for cc in range(8):
                    hi(N_OUT + 8 + 8 * j + cc, cc)

            for t in range(T):
                act.wait_ge(x1_ready, 4 * T)
                act.wait_ge(act_seq, 60 + t)
                A(junk2[:, :], x1[:, t, :], ACT.Square, accum_out=ssq[:, 4 + t:5 + t]).then_inc(act_seq, 1)
            act.wait_ge(act_seq, 64)
            A(rstd[:, 8:12], ssq[:, 4:8], ACT.Sqrt, bias=eps_c[:, :], scale=1.0 / D).then_inc(std2_ready, 1)
            act.wait_ge(rstd2_ready, 1)
            for t in range(T):
                A(xn[:, t, :], x1[:, t, :], ACT.Copy, scale=rstd[:, 12 + t:13 + t]).then_inc(xn2_ready, 1)
            hi(N_EXP, 0)
            hi(N_EXP + 1, 1)
            act.wait_ge(lsub_ready, 1)
            A(aff[:, :, 0:NE], slots[:, :, 0:NE], ACT.Exp).then_inc(lexp_ready, 1)

            def tokens(turn, b, u, count):
                act.wait_ge(gather_done, count)
                if not isinstance(count, int) or count > 1:
                    act.wait_ge(xg_ready, count - 1)
                for i in range(4):
                    k = 4 * u + i
                    last = A(xg32[:, i, :], bank[b][:, i * P:(i + 1) * P], ACT.Identity, scale=a1[:, k:k + 1], bias=modcol[:, 48 + k:49 + k])
                last.then_inc(xg32_ready, 1)
                act.wait_ge(xg32_ready, count)
                A(xgT[turn][:, 4 * u:4 * u + 4, :, 0:64], xg32[:, :, :].rearrange("p k (e c) -> p k e c", e=2), ACT.Copy).then_inc(xg_hi, 1)

            def hi_expert(p, e, cc):
                c, n0 = cc % NSTAGE, N_EXP + 96 * p + 48 * e
                s = split_index(cc) % NSPLIT
                act.wait_ge(stage_full[c], 2 * (n0 + cc - c) + 16)
                act.wait_ge(chunk_used, n0 + SPLIT_CC[SPLIT_CC.index(cc) - NSPLIT] + 1 + NSPLIT)
                A(w_hi[:, s, :, :], stage[:, c, :, :], ACT.Copy).then_inc(hi_ready, 1)

            def gu_copy(p, e, a):
                act.wait_ge(chunk_used, N_EXP + 96 * p + 48 * e + 8 * a + 8 + NSPLIT)
                if a >= 2:
                    act.wait_ge(fold_done, 4 * p + 2 * e + 1)
                else:
                    act.wait_ge(he_ready, 4 * p + 2 * e + 2)
                A(gu[:, a % 2, :], bank[a][:, :], ACT.Copy).then_inc(acc_free, 1)

            def sigmoid_gate(p, e, jb):
                act.wait_ge(fold_done, 4 * p + 2 * e + jb + 1)
                A(sgm[:, :], bank[4][:, 0:256], ACT.Sigmoid).then_inc(sgm_ready, 1)

            def he_round(p, e, jb):
                act.wait_ge(he32_ready, 4 * p + 2 * e + jb + 1)
                A(heT[:, 4 * jb:4 * jb + 4, 0:64], h32e[:, :].rearrange("p (f c) -> p f c", f=4), ACT.Copy).then_inc(he_hi, 1)

            def y_lower(p, e, jd):
                act.wait_ge(chunk_used, N_EXP + 96 * p + 48 * e + 33 + DOWN.index((jd, 3)) + NSPLIT)
                act.wait_ge(acc_free, G_EXP + 16 * p + 8 * e + jd + 8)
                A(ytmp[:, :], bank[jd][64:128, :], ACT.Copy).then_inc(ytmp_ready, 1)

            def y_round(p, jd):
                act.wait_ge(y32_ready, 4 * p + jd + 1)
                A(y_hi[:, jd, :], ysum[:, jd, :], ACT.Copy).then_inc(yhi_ready, 1)

            def act_pair(p, turn, first, last_pair):
                for e in range(2):
                    for cc in range(48):
                        if cc % NSTAGE not in RAW_SLOTS and not (first and e == 0 and cc < 2):
                            hi_expert(p, e, cc)
                        if cc == 1 and e == 1:
                            y_lower(p, 0, 3)
                        if e == 0 and not first:
                            if cc == 1:
                                y_lower(p - 1, 1, 3)
                            if cc == 2:
                                y_round(p - 1, 3)
                        if cc == 24 and e == 0:
                            act.wait_ge(selT_done, p + 1)
                            A(selT[:, :], bank[6][:, :], ACT.Copy).then_inc(selT_ready, 1)
                        if cc in (9, 17, 25, 33):
                            gu_copy(p, e, cc // 8 - 1)
                        if cc == 20:
                            sigmoid_gate(p, e, 0)
                        if cc == 22:
                            he_round(p, e, 0)
                        if cc == 35:
                            sigmoid_gate(p, e, 1)
                        if cc == 36:
                            he_round(p, e, 1)
                        if cc in (41, 43, 45):
                            y_lower(p, e, (cc - 41) // 2)
                        if e == 1:
                            if cc in (42, 44, 46):
                                y_round(p, (cc - 42) // 2)
                            if not last_pair and cc < 32 and cc % 8 == 6:
                                tokens(1 - turn, 5, cc // 8, 4 * p + 5 + cc // 8)
                if last_pair:
                    y_lower(p, 1, 3)
                    y_round(p, 3)

            for u in range(4):
                tokens(0, 4 + u, u, u + 1)
            act_pair(0, 0, True, False)
            with act.Fori(0, PAIRS // 2 - 1) as i:
                for turn in (1, 0):
                    act_pair(2 * i + 2 - turn, turn, False, False)
            act_pair(PAIRS - 1, 1, False, True)

            for t in range(T):
                act.wait_ge(scat_added, 4 + 16 * PAIRS - 3 + t)
                act.wait_ge(act_seq, 64 + t)
                A(junk2[:, :], x1[:, t, :], ACT.Square, accum_out=ssq[:, 8 + t:9 + t]).then_inc(act_seq, 1)
                act.wait_ge(act_seq, 64 + t + 1)
                A(ssq[:, 12 + t:13 + t], ssq[:, 8 + t:9 + t], ACT.Sqrt, bias=eps_c[:, :], scale=1.0 / D).then_inc(std3_ready, 1)

        @block.vector
        def _(dve):
            V = nc.vector
            seq = [0]

            def link(ins):
                seq[0] += 1
                ins.then_inc(dve_seq, 1)
                dve.wait_ge(dve_seq, seq[0])

            def lo(n, c, width=W):
                dve.wait_ge(hi_ready, n + 1)
                V.tensor_tensor(w_lo[:, c % NSPLIT, :, 0:width], stage[:, c % NSTAGE, :, 0:width],
                                w_hi[:, c % NSPLIT, :, 0:width].bitcast(F32), ALU.subtract).then_inc(lo_ready, 1)

            dve.sem_inc(lo_ready, NSTAGE)
            dve.sem_inc(ada_done, NADA)
            dve.sem_inc(ada_col_done, 1)
            dve.sem_inc(ada_col_ready, 1)
            dve.sem_inc(o_lo, 2)
            dve.sem_inc(pT_ready, 2)
            dve.sem_inc(pv_done, 2)
            for s in sig_out:
                dve.sem_inc(s, 16)
            dve.sem_inc(he_ready, 2)
            dve.sem_inc(scat_added, 4)
            V.memset(ones[:, :], 1.0)
            V.memset(aff[:, :, NE:NE + 2], 0.0)
            V.memset(eps_c[:, :], EPS)
            dve.wait_ge(cols_done, 1)
            V.tensor_copy(pcol[:, :], bank[5][:, 0:54]).then_inc(cols_ready, 1)
            V.tensor_copy(bcol[:, :], bank[5][:, 64:160]).then_inc(cols_ready, 1)
            dve.wait_ge(sigc_ready, 1)
            V.tensor_tensor(siluc[:, :], siluc[:, :], pcol[:, 32:48], ALU.mult).then_inc(siluc_ready, 1)
            dve.wait_ge(siluc_ready, 1)

            def ada_step(m, k, r, turn):
                dve.wait_ge(ada_full[k % NADA], 16 * turn)
                if k == 0:
                    dve.wait_ge(ada_col_done, r + 1)
                    V.tensor_scalar(ada_acc[:, :], ada_tile[:, 0, :], siluc[:, 0:1], None, ALU.mult).then_inc(ada_done, 1)
                else:
                    dve.wait_ge(ada_done, m + NADA)
                    V.scalar_tensor_tensor(ada_acc[:, :], ada_tile[:, k % NADA, :], siluc[:, k:k + 1], ada_acc[:, :],
                                           ALU.mult, ALU.add).then_inc(ada_done, 1)

            def ada_finish(r):
                dve.wait_ge(ada_col_done, r + 2)
                V.tensor_tensor(modcol[:, ds(8 * r, 8)], bank[4][:, 0:8], bcol[:, ds(8 * r, 8)], ALU.add).then_inc(ada_col_ready, 1)

            with dve.Fori(0, ADA_FIRST) as r:
                for k in range(KD):
                    ada_step(KD * r + k, k, r, 4 * r + k // NADA + 1)
                ada_finish(r)
            dve.wait_ge(std_ready, 1)
            V.reciprocal(rstd[:, 4:8], rstd[:, 0:4]).then_inc(rstd_ready, 1)
            dve.wait_ge(ada_col_ready, ADA_FIRST + 1)
            link(V.scalar_tensor_tensor(a1[:, :], modcol[:, 16:32], 1.0, pcol[:, 0:16], ALU.add, ALU.mult))
            def h_lo(k):
                dve.wait_ge(hT_hi_ready, k + 1)
                V.tensor_tensor(hT_lo[:, k, :], h32[:, k % 4, :], hT_hi[:, k, :].bitcast(F32), ALU.subtract).then_inc(hT_lo_ready, 1)

            for k in range(KD):
                dve.wait_ge(xT_done, k + 1)
                V.tensor_scalar(h32[:, k % 4, :], bank[4 + k % 4][:, :], a1[:, k:k + 1], modcol[:, k:k + 1],
                                ALU.mult, ALU.add).then_inc(h32_ready, 1)
                if k >= 1:
                    h_lo(k - 1)
                if k >= 3 and k % 2:
                    lo(N_Z + k // 2 - 1, k // 2 - 1)
            h_lo(KD - 1)
            lo(N_Z + 7, 7)
            for cc in range(8):
                lo(N_Z + 8 + cc, cc, LAT - QR)
            lo(N_Z + 16, 0)
            with dve.Fori(0, 3) as j:
                for cc in range(1, 9):
                    lo(N_Z + 16 + 8 * j + cc, cc)
            dve.wait_ge(zstd_ready, 1)
            V.reciprocal(zr[:, 0:14, :], zr[:, 0:14, :]).then_inc(zr_ready, 1)
            with dve.Fori(0, 8) as j:
                for cc in range(8):
                    lo(N_GATE + 1 + 8 * j + cc, cc + 1)
                    for k in (2 * cc, 2 * cc + 1):
                        ada_step(KD * (j + ADA_FIRST) + k, k, j + ADA_FIRST, 4 * (j + ADA_FIRST) + k // NADA + 1)
                ada_finish(j + ADA_FIRST)

            for i in range(4):
                dve.wait_ge(sig_out[i], 16 * 9)
            for i in range(7):
                dve.wait_ge(pro_done, i + 1)
                src = bank[4 + i % 4][:, :]
                if i < 4:
                    ins = V.tensor_scalar(cqT[:, i, :], src, pcol[:, 48 + i:49 + i], None, ALU.mult)
                elif i < 6:
                    dve.wait_ge(pro_done, 7)
                    ins = V.tensor_scalar(ckvT[:, i - 4, :], src, pcol[:, 48 + i:49 + i], None, ALU.mult)
                else:
                    ins = V.tensor_copy(krT[:, :], src)
                ins.then_inc(pro_ready, 1)

            def qr_rotate(H):
                dve.wait_ge(qr_done, H + 1)
                V.tensor_tensor(qr[:, :], bank[5][:, :], qtab[:, :], ALU.mult).then_inc(qr_ready, 1)

            def negative_max(H, b, scale):
                for qb in range(4):
                    dve.wait_ge(s_done, 4 * H + qb + 1)
                    V.tensor_reduce(nmax[:, b, qb:qb + 1], bank[qb][:, :], AX.X, ALU.max).then_inc(nmx_seq, 1)
                    dve.wait_ge(nmx_seq, 4 * H + qb + 1)
                    V.tensor_scalar(nmax[:, b, 4 + qb:5 + qb], nmax[:, b, qb:qb + 1], -scale, None, ALU.mult).then_inc(nmax_ready, 1)

            def output_lo(Hp):
                dve.wait_ge(o_hi, Hp + 1)
                V.tensor_tensor(oT_lo[:, ds(Hp, 1), :], bank[4][:, :].unsqueeze(1), oT_hi[:, ds(Hp, 1), :].bitcast(F32),
                                ALU.subtract).then_inc(o_lo, 1)

            def probs_transposed(Hp):
                for kt in range(4):
                    dve.wait_ge(pT_done, 4 * Hp + kt + 1)
                    dve.wait_ge(pv_done, 4 * Hp + kt + 1)
                    V.tensor_copy(pT[:, kt % 2, :], bank[6 + kt % 2][:, :]).then_inc(pT_ready, 1)

            def normalise(H, b):
                dve.wait_ge(exp_done, 4 * H + 8)
                V.reciprocal(rsum[:, b, 4:8], rsum[:, b, 0:4]).then_inc(rinv_seq, 1)
                dve.wait_ge(rinv_seq, H + 1)
                for qb in range(4):
                    last = V.tensor_scalar(probs[b][:, qb, :], probs[b][:, qb, :], rsum[:, b, 4 + qb:5 + qb], None, ALU.mult)
                last.then_inc(p_ready, 1)

            qr_rotate(0)
            negative_max(0, 0, MLA_SCALE)
            normalise(0, 0)
            with dve.Fori(0, 3) as i:
                for b in (1, 0):
                    H = 2 * i + 2 - b
                    qr_rotate(H)
                    negative_max(H, b, MLA_SCALE)
                    probs_transposed(H - 1)
                    output_lo(H - 1)
                    normalise(H, b)
            qr_rotate(7)
            negative_max(7, 1, MLA_SCALE)
            probs_transposed(6)
            output_lo(6)
            normalise(7, 1)
            with dve.Fori(0, 2) as n:
                for g in range(4):
                    H = 4 * n + g + HM
                    negative_max(H, g % 2, GQA_SCALE)
                    probs_transposed(H - 1)
                    output_lo(H - 1)
                    normalise(H, g % 2)
            probs_transposed(HM + HG - 1)
            output_lo(HM + HG - 1)

            def gate_row(m, col):
                for q in range(4):
                    if q or m:
                        dve.wait_ge(row_done, 4 * m + q)
                    V.tensor_tensor(diag[:, :, :], ident[:, :].unsqueeze(1).broadcast_to([P, 4, P]),
                                    modcol[:, col + 4 * q:col + 4 * q + 4].unsqueeze(2).broadcast_to([P, 4, P]),
                                    ALU.mult).then_inc(diag_ready, 1)
                    dve.wait_ge(row_done, 4 * m + q + 1)
                    V.tensor_copy(gt_row[:, q * W:(q + 1) * W], bank[5][:, :]).then_inc(row_ready, 1)

            gate_row(0, 32)
            with dve.Fori(0, 4) as j:
                for half in range(2):
                    n0 = N_BR + 8 * j + 4 * half
                    g0 = G_BR + 8 * j + 4 * half
                    for cc in range(1, 4):
                        lo(n0 + cc, 4 * half + cc)
                    dve.wait_ge(sg_full[half], 16 * j + 16)
                    for b in range(4):
                        wait_bank(dve, G_BR // 4 + 2 * j + half, b, n0 + 4)
                        m_b = mT[:, ds(4 * j + b, 1), :]
                        gate = sg_in[:, half, b:b + 1, :]
                        prod = bank[b][:, :].unsqueeze(1)
                        if half == 0:
                            V.tensor_tensor(m_b, prod, gate, ALU.mult).then_inc(acc_free, 1)
                        else:
                            V.tensor_tensor(m_tmp[:, :].unsqueeze(1), prod, gate, ALU.mult).then_inc(acc_free, 1)
                            dve.wait_ge(acc_free, g0 + b + 5)
                            V.tensor_tensor(m_b, m_b, m_tmp[:, :].unsqueeze(1), ALU.add).then_inc(mT_ready, 1)
                            dve.wait_ge(mT_ready, 4 * j + b + 1)
                        if b == 0:
                            lo(n0 + 4, (4 * half + 4) % 8)
            for k in range(KD):
                dve.wait_ge(m_hi, k + 1)
                V.tensor_tensor(mT_lo[:, k, :], mT[:, k, :], mT_hi[:, k, :].bitcast(F32), ALU.subtract).then_inc(m_lo, 1)
                if k >= 3 and k % 2:
                    lo(N_OUT + k // 2, k // 2)

            def add_out(j, n_next):
                for b in range(4):
                    wait_bank(dve, G_OUT // 4 + j, b, N_OUT + 8 * j + 8)
                    V.tensor_tensor(m_tmp[:, :], bank[b][:, :], gt_row[:, ds(W * j, W)], ALU.mult).then_inc(acc_free, 1)
                    dve.wait_ge(acc_free, G_OUT + 4 * j + b + 5)
                    V.tensor_tensor(x1[:, b, ds(W * j, W)], x1[:, b, ds(W * j, W)], m_tmp[:, :], ALU.add).then_inc(x1_ready, 1)
                    dve.wait_ge(x1_ready, 4 * j + b + 1)
                    if b == 0 and n_next is not None:
                        lo(n_next, 0)

            dve.wait_ge(x1_in, 16 * T)
            add_out(0, N_OUT + 8)
            with dve.Fori(1, 3) as j:
                for cc in range(1, 8):
                    lo(N_OUT + 8 * j + cc, cc)
                add_out(j, N_OUT + 8 + 8 * j)
            for cc in range(1, 8):
                lo(N_OUT + 24 + cc, cc)
            add_out(3, None)

            dve.wait_ge(x1_ready, 16)
            gate_row(1, 80)
            dve.wait_ge(std2_ready, 1)
            V.reciprocal(rstd[:, 12:16], rstd[:, 8:12]).then_inc(rstd2_ready, 1)
            link(V.scalar_tensor_tensor(a1[:, :], modcol[:, 64:80], 1.0, pcol[:, 16:32], ALU.add, ALU.mult))
            for k in range(KD):
                dve.wait_ge(h2T_done, k + 1)
                if k >= 2:
                    dve.wait_ge(logit_done, k - 1)
                V.tensor_scalar(h2T[:, k % 2, :], bank[4 + k % 4][:, :], a1[:, k:k + 1], modcol[:, 48 + k:49 + k],
                                ALU.mult, ALU.add).then_inc(h2T_ready, 1)
            dve.wait_ge(logit_done, KD)
            for t in range(T):
                last = V.tensor_copy(slots[:, t, 0:NE], bank[t][:, 0:NE])
            link(last)
            link(V.tensor_reduce(lmx[:, 0:4], slots[:, :, 0:NE], AX.X, ALU.max))
            V.tensor_tensor(slots[:, :, 0:NE], slots[:, :, 0:NE], lmx[:, 0:4].unsqueeze(2).broadcast_to([P, T, NE]),
                            ALU.subtract).then_inc(lsub_ready, 1)
            lo(N_EXP, 0)
            lo(N_EXP + 1, 1)
            dve.wait_ge(lexp_ready, 1)
            link(V.tensor_reduce(lmx[:, 4:8], aff[:, :, 0:NE], AX.X, ALU.add))
            link(V.reciprocal(lmx[:, 0:4], lmx[:, 4:8]))
            V.tensor_tensor(aff[:, :, 0:NE], aff[:, :, 0:NE], lmx[:, 0:4].unsqueeze(2).broadcast_to([P, T, NE]),
                            ALU.mult).then_inc(aff_ready, 1)
            dve.wait_ge(affT_done, 1)
            link(V.tensor_copy(affT[:, :], bank[4][0:NE, :]))
            src = affT[:, :]
            for i in range(CAP // 8):
                link(V.max(m8[:, :], src))
                if i < CAP // 8 - 1:
                    link(V.match_replace(work[:, i % 2, :], m8[:, :], src, -1.0))
                    src = work[:, i % 2, :]
            link(V.tensor_scalar(gt_m[:, :], affT[:, :], m8[:, 7:8], 0.0, ALU.is_gt, ALU.add, accum_out=cnt[:, 0:1]))
            link(V.tensor_scalar(cnt[:, 1:2], cnt[:, 0:1], -1.0, float(CAP), ALU.mult, ALU.add))
            link(V.tensor_scalar(eq_m[:, :], affT[:, :], m8[:, 7:8], None, ALU.is_equal))
            link(V.tensor_tensor_scan(rank[:, :], eq_m[:, :], eq_m[:, :], 0.0, ALU.add, ALU.bypass))
            link(V.scalar_tensor_tensor(eq_m[:, :], rank[:, :], cnt[:, 1:2], eq_m[:, :], ALU.is_le, ALU.mult))
            link(V.tensor_tensor(gt_m[:, :], gt_m[:, :], eq_m[:, :], ALU.add))
            link(V.tensor_tensor_scan(rank[:, :], gt_m[:, :], gt_m[:, :], 0.0, ALU.add, ALU.bypass))
            link(V.tensor_tensor(rank[:, :], rank[:, :], gt_m[:, :], ALU.mult))
            V.tensor_scalar(slotT[:, :], rank[:, :], -1.0, None, ALU.add).then_inc(slotT_ready, 1)
            V.memset(slots[:, :, NE:NE + 2], -1.0)
            dve.wait_ge(slots_done, 1)
            link(V.tensor_copy(slots[:, :, 0:NE], bank[5][:, 0:T * NE].rearrange("p (t e) -> p t e", t=T)))

            def select(p):
                for t in range(T):
                    last = V.tensor_tensor(sel[:, t, :, :], iota[:, :].unsqueeze(1).broadcast_to([P, 2, CAP]),
                                           slots[:, t, ds(2 * p, 2)].unsqueeze(2).broadcast_to([P, 2, CAP]), ALU.is_equal)
                last.then_inc(sel_ready, 1)

            def tokens_lo(turn, u, count):
                dve.wait_ge(xg_hi, count)
                V.tensor_tensor(xgT[turn][:, 4 * u:4 * u + 4, :, 64:128], xg32[:, :, :].rearrange("p k (e c) -> p k e c", e=2),
                                xgT[turn][:, 4 * u:4 * u + 4, :, 0:64].bitcast(F32), ALU.subtract).then_inc(xg_ready, 1)

            def lo_expert(p, e, cc):
                s = split_index(cc) % NSPLIT
                dve.wait_ge(hi_ready, N_EXP + SPLIT_PER_EXPERT * (2 * p + e) + split_index(cc) + 1)
                V.tensor_tensor(w_lo[:, s, :, :], stage[:, cc % NSTAGE, :, :], w_hi[:, s, :, :].bitcast(F32), ALU.subtract)\
                    .then_inc(lo_ready, 1)

            def swiglu(p, e, jb):
                dve.wait_ge(sgm_ready, 4 * p + 2 * e + jb + 1)
                dve.wait_ge(he_ready, 4 * p + 2 * e + jb + 2)
                V.tensor_tensor(h32e[:, :], bank[4][:, 0:256], sgm[:, :], ALU.mult).then_inc(he_mid, 1)
                dve.wait_ge(he_mid, 4 * p + 2 * e + jb + 1)
                V.tensor_tensor(h32e[:, :], bank[4][:, 256:512], h32e[:, :], ALU.mult).then_inc(he32_ready, 1)

            def he_lo(p, e, jb):
                dve.wait_ge(he_hi, 4 * p + 2 * e + jb + 1)
                V.tensor_tensor(heT[:, 4 * jb:4 * jb + 4, 64:128], h32e[:, :].rearrange("p (f c) -> p f c", f=4),
                                heT[:, 4 * jb:4 * jb + 4, 0:64].bitcast(F32), ALU.subtract).then_inc(he_ready, 1)

            def y_add(p, e, jd):
                dve.wait_ge(ytmp_ready, 8 * p + 4 * e + jd + 1)
                V.tensor_tensor(ysum[64 * e:64 * e + 64, jd, :], bank[jd][0:64, :], ytmp[:, :], ALU.add)\
                    .then_inc(acc_free, 1)
                if e == 1:
                    dve.wait_ge(acc_free, G_EXP + 16 * p + 8 + jd + 9)
                    if jd == 0:
                        dve.wait_ge(val_ready, p + 1)
                    V.scalar_tensor_tensor(ysum[:, jd, :], ysum[:, jd, :], val[:, 0:1], gt_row[:, jd * W:(jd + 1) * W],
                                           ALU.mult, ALU.mult).then_inc(y32_ready, 1)

            def y_lo_part(p, jd):
                dve.wait_ge(yhi_ready, 4 * p + jd + 1)
                V.tensor_tensor(y_lo[:, jd, :], ysum[:, jd, :], y_hi[:, jd, :].bitcast(F32), ALU.subtract).then_inc(ylo_ready, 1)

            def add_scattered(p, jd, tiles=range(T)):
                for t in tiles:
                    dve.wait_ge(scat_done, 16 * p + 4 * jd + t + 1)
                    V.tensor_tensor(x1[:, t, jd * W:(jd + 1) * W], x1[:, t, jd * W:(jd + 1) * W], bank[4 + t][:, :],
                                    ALU.add).then_inc(scat_added, 1)

            def dve_pair(p, turn, first, last_pair):
                for e in range(2):
                    for cc in range(48):
                        if cc % NSTAGE not in RAW_SLOTS and not (first and e == 0 and cc < 2):
                            lo_expert(p, e, cc)
                        if cc == 1 and e == 1:
                            y_add(p, 0, 3)
                        if e == 0 and not first:
                            if cc == 1:
                                y_add(p - 1, 1, 3)
                            if cc == 2:
                                y_lo_part(p - 1, 3)
                            if 4 <= cc < 20 and cc % 4 < 2:
                                add_scattered(p - 1, cc // 4 - 1, ((0, 1), (2, 3))[cc % 4])
                        if cc == 24 and e == 0:
                            dve.wait_ge(val_done, p + 1)
                            V.tensor_copy(val[0:64, :], bank[7][0:64, 0:1])
                            V.tensor_copy(val[64:128, :], bank[7][64:128, 1:2]).then_inc(val_ready, 1)
                        if cc == 20:
                            swiglu(p, e, 0)
                        if cc == 22:
                            he_lo(p, e, 0)
                        if cc == 35:
                            swiglu(p, e, 1)
                        if cc == 36:
                            he_lo(p, e, 1)
                        if cc == 28 and e == 0 and not last_pair:
                            select(p + 1)
                        if cc in (41, 43, 45):
                            y_add(p, e, (cc - 41) // 2)
                        if e == 1:
                            if cc in (42, 44, 46):
                                y_lo_part(p, (cc - 42) // 2)
                            if not last_pair and cc < 32 and cc % 8 == 6:
                                tokens_lo(1 - turn, cc // 8, 4 * p + 5 + cc // 8)
                            if last_pair and cc in (44, 46):
                                add_scattered(p, (cc - 44) // 2)
                if last_pair:
                    y_add(p, 1, 3)
                    add_scattered(p, 2)
                    y_lo_part(p, 3)
                    add_scattered(p, 3)

            select(0)
            for u in range(4):
                tokens_lo(0, u, u + 1)
            dve_pair(0, 0, True, False)
            with dve.Fori(0, PAIRS // 2 - 1) as i:
                for turn in (1, 0):
                    dve_pair(2 * i + 2 - turn, turn, False, False)
            dve_pair(PAIRS - 1, 1, False, True)

            dve.wait_ge(gf_in, 16)
            for t in range(T):
                dve.wait_ge(std3_ready, t + 1)
                if t >= 2:
                    dve.wait_ge(stored[t % 2], 16 * (t // 2))
                link(V.reciprocal(rstd[:, t:t + 1], ssq[:, 12 + t:13 + t]))
                V.scalar_tensor_tensor(res[:, t % 2, :], x1[:, t, :], rstd[:, t:t + 1], gf_row[:, :], ALU.mult, ALU.mult)\
                    .then_inc(res_ready, 1)

        @block.gpsimd
        def _(pool):
            G = nc.gpsimd
            seq = [0]

            def link(ins):
                seq[0] += 1
                ins.then_inc(pool_seq, 1)
                pool.wait_ge(pool_seq, seq[0])

            pool.wait_ge(cols_done, 1)
            pool.wait_ge(h32_ready, KD)
            pool.wait_ge(zr_ready, 1)
            loads = [(rope_kc[:, :, :], consts[:, C_KC:C_KS]), (rope_ks[:, :, :], consts[:, C_KS:C_GC]),
                     (rope_gc[:, :, :, :], consts[:, C_GC:C_GS]), (rope_gs[:, :, :, :], consts[:, C_GS:C_END])]
            for dst, src in loads[:2]:
                pool.dma_start(dst, src.rearrange("p (t f) -> p t f", t=T)).then_inc(tab_in, 16)
            for dst, src in loads[2:]:
                pool.dma_start(dst, src.rearrange("p (t h f) -> p t h f", t=T, h=2)).then_inc(tab_in, 16)
            for h in range(HG + KVG):
                g = g_qn if h < HG else g_kn
                pool.dma_start(g_row[:, h, :], g[0].partition_broadcast(P)).then_inc(tab_in, 16)
            pool.wait_ge(tab_in, 16 * (4 + HG + KVG))
            for t in range(T):
                G.tensor_scalar(zc[:, t, 0:QR], zc[:, t, 0:QR], zr[:, 12, t:t + 1], None, ALU.mult)
                G.tensor_scalar(zc[:, t, QR:QR + KVR], zc[:, t, QR:QR + KVR], zr[:, 13, t:t + 1], None, ALU.mult)
            kr1, kr_2 = zc[:, :, 768:800], zc[:, :, 800:832]
            ta, tb = r_a[:, 0:4, 0, :], r_b[:, 0:4, 0, :]
            tc_, td = r_c[:, 0:4, 0, :], r_d[:, 0:4, 0, :]
            G.tensor_tensor(ta, kr1, rope_kc[:, :, :], ALU.mult)
            G.tensor_tensor(tb, kr_2, rope_ks[:, :, :], ALU.mult)
            G.tensor_tensor(tc_, kr1, rope_ks[:, :, :], ALU.mult)
            link(G.tensor_tensor(td, kr_2, rope_kc[:, :, :], ALU.mult))
            for o in (0, 64):
                G.tensor_tensor(kr2[:, :, o:o + 32], ta, tb, ALU.subtract)
                ins = G.tensor_tensor(kr2[:, :, o + 32:o + 64], tc_, td, ALU.add)
            link(ins)
            NH = HG + KVG
            for t in range(T):
                z4 = zg[:, t, 0:NH * DH].rearrange("p (h d) -> p h d", h=NH)
                z5 = zg[:, t, 0:NH * DH].rearrange("p (h r d) -> p h r d", h=NH, r=2)
                x1_, x2_ = z5[:, :, :, 0:32], z5[:, :, :, 32:64]
                cos = rope_gc[:, t, :, :].unsqueeze(1).broadcast_to([P, NH, 2, 32])
                sin = rope_gs[:, t, :, :].unsqueeze(1).broadcast_to([P, NH, 2, 32])
                link(G.tensor_tensor(z4, z4, zr[:, 0:NH, t].unsqueeze(2).broadcast_to([P, NH, DH]), ALU.mult))
                link(G.tensor_tensor(z4, z4, g_row[:, :, :], ALU.mult))
                G.tensor_tensor(r_a[:, :, :, :], x1_, cos, ALU.mult)
                G.tensor_tensor(r_b[:, :, :, :], x2_, sin, ALU.mult)
                G.tensor_tensor(r_c[:, :, :, :], x1_, sin, ALU.mult)
                link(G.tensor_tensor(r_d[:, :, :, :], x2_, cos, ALU.mult))
                G.tensor_tensor(x1_, r_a[:, :, :, :], r_b[:, :, :, :], ALU.subtract)
                ins = G.tensor_tensor(x2_, r_c[:, :, :, :], r_d[:, :, :, :], ALU.add)
                if t < T - 1:
                    link(ins)
                else:
                    ins.then_inc(zpost_ready, 1)
            pool.wait_ge(zpost_ready, 1)
            for h in range(HG):
                H = HM + h
                pool.wait_ge(qn_done, H)
                if h % 4 == 0:
                    pool.wait_ge(v_done, HM)
                    pool.wait_ge(kn_done, h // 4 + HM)
                    k_head = (HG + h // 4) * DH
                    G.tensor_copy(k_stage[:, :, :], zg[:, :, k_head:k_head + DH]).then_inc(ks_ready, 1)
                G.tensor_copy(q_stage[:, :, :], zg[:, :, h * DH:(h + 1) * DH]).then_inc(qs_ready, 1)
                pool.wait_ge(pv_done, 4 * H - 2)
                v_head = (HG + KVG + h // 4) * DH
                G.tensor_copy(v_sb[:, h % 2, :, :], zg[:, :, v_head:v_head + DH]).then_inc(v_ready, 1)


_INS = ["x", "c", "w_ada", "b_ada", "g_mix", "w_in", "g_cq", "g_ckv", "w_uq", "w_ukv", "g_qn", "g_kn",
        "w_br_a", "w_br_b", "w_out", "g_ffn", "w_router", "w_e_gate", "w_e_up", "w_e_down", "g_final"]


def kernel(**inputs):
    import numpy as _np
    import concourse.bacc as _bacc
    from concourse import mybir as _mybir
    from concourse.bass_utils import run_bass_kernel_spmd as _run

    nc = _bacc.Bacc("TRN2", target_bir_lowering=False, num_devices=1)
    arrays, args = {}, []
    for name in _INS:
        a = _np.ascontiguousarray(inputs[name])
        arrays[f"in_{name}"] = a
        args.append(nc.dram_tensor(f"in_{name}", a.shape, _mybir.dt.from_np(a.dtype), kind="ExternalInput").ap())
    k = shape_constants()
    arrays["in_consts"] = k
    args.append(nc.dram_tensor("in_consts", k.shape, _mybir.dt.float32, kind="ExternalInput").ap())
    args.append(nc.dram_tensor("sig_gates", (2 * D, S), _mybir.dt.float32, kind="Internal").ap())
    args.append(nc.dram_tensor("out_0", (1, S, D), _mybir.dt.float32, kind="ExternalOutput").ap())
    encoder_block(nc, *args)
    r = _run(nc, [arrays], core_ids=[0])
    return r.results[0]["out_0"]
```

```python
import math
from contextlib import ExitStack

import numpy as np
import concourse.bass as bass
from concourse import mybir

P = 128
D = 2048
S = 512
T = S // P
KD = D // P
QR, KVR, ROPE, DH = 512, 256, 64, 128
HM, HG, KVG = 8, 8, 2
LAT = QR + KVR + ROPE
GQ = (HG + 2 * KVG) * DH
NE, FF = 16, 1024
CAP = 2 * S // NE
W = 512
EPS = 1e-6
MLA_SCALE = float(DH + ROPE) ** -0.5
GQA_SCALE = float(DH) ** -0.5
NSTAGE, NSPLIT = 8, 2
ADA_W, NADA = 1024, 4
ADA_BLOCKS = 6 * D // ADA_W
ADA_ORDER = (0, 2, 1, 3)
ADA_FIRST = len(ADA_ORDER)
AHEAD = 5
ADA_AT = [(0, 1), (2, 3, 4), (5, 6, 7), (8, 9), (10, 11), (12, 13), (14, 15), ()]
N_Z, N_GATE = 0, 40
N_BR = N_GATE + 64
N_OUT = N_BR + 32
N_EXP = N_OUT + 32
G_Z, G_GATE = 0, 20
G_BR = G_GATE + 32
G_OUT = G_BR + 32
G_EXP = G_OUT + 16
PAIRS = NE // 2
DOWN = [(j, k) for j in range(3) for k in (0, 1)] + [(j, k) for j in range(3) for k in (2, 3)] + [(3, k) for k in range(4)]
FOLD_AT = (18, 33)
SCATTER_AT = (3, 8, 13, 20)
GATHER_FROM = 40
RAW_SLOTS = (2, 5, 7)
YET_SPLIT = (42, 50, 58, 66)


def unsplit(c):
    return c % NSTAGE in RAW_SLOTS and c not in YET_SPLIT


SPLIT_CHUNKS = [c for c in range(-NSTAGE, 96) if not unsplit(c)]
SPLIT_PER_PAIR = sum(c >= 0 for c in SPLIT_CHUNKS)
assert SPLIT_PER_PAIR % NSPLIT == 0


def split_index(c):
    return SPLIT_CHUNKS.index(c) - SPLIT_CHUNKS.index(0)


C_ID, C_FOLD, C_IOTA, C_QTAB = 0, 128, 192, 256
C_KC, C_KS, C_GC, C_GS, C_END = 768, 896, 1024, 1280, 1536


def shape_constants():
    half = ROPE // 2
    freqs = (np.float32(10000.0) ** (-np.arange(half, dtype=np.float32) / np.float32(half))).astype(np.float32)

    def tables(pos):
        a = pos.astype(np.float32)[:, None] * freqs[None, :]
        return np.cos(a).astype(np.float32), np.sin(a).astype(np.float32)

    t = np.arange(S)
    c1, s1 = tables(t)
    cr, sr = tables(t // 64)
    cc, sc = tables(t % 64)
    k = np.zeros((P, C_END), np.float32)
    k[:, C_ID:C_ID + P] = np.eye(P)
    k[:, C_FOLD:C_FOLD + 64] = np.concatenate([np.eye(64), np.eye(64)])
    k[:, C_IOTA:C_IOTA + 64] = np.arange(64)[None, :]
    k[:, C_QTAB:C_QTAB + S] = np.concatenate([c1.T, c1.T, -s1.T, s1.T])

    def by_tile(a):
        return a.reshape(T, P, -1).transpose(1, 0, 2).reshape(P, -1)

    k[:, C_KC:C_KS] = by_tile(c1)
    k[:, C_KS:C_GC] = by_tile(s1)
    k[:, C_GC:C_GS] = by_tile(np.concatenate([cr, cc], 1))
    k[:, C_GS:C_END] = by_tile(np.concatenate([sr, sc], 1))
    return k


def encoder_block(nc, x, c, w_ada, b_ada, g_mix, w_in, g_cq, g_ckv, w_uq, w_ukv, g_qn, g_kn,
                  w_br_a, w_br_b, w_out, g_ffn, w_router, w_e_gate, w_e_up, w_e_down, g_final,
                  consts, sig_gates, out):
    F32, F32R = mybir.dt.float32, mybir.dt.float32r
    ALU, ACT, AX = mybir.AluOpType, mybir.ActivationFunctionType, mybir.AxisListType
    ds = bass.ds

    x_v = x[0].rearrange("(t p) d -> p t d", p=P)
    out_v = out[0].rearrange("(t p) d -> p t d", p=P)
    w_ada_v = w_ada[0].rearrange("(k p) n -> p k n", p=P)
    w_in_v = w_in[0].rearrange("(k p) n -> p k n", p=P)
    w_uq_v = w_uq[0].rearrange("(k p) n -> p k n", p=P)
    w_ukv_v = w_ukv[0].rearrange("(k p) n -> p k n", p=P)
    w_bra_v = w_br_a[0].rearrange("(k p) n -> p k n", p=P)
    w_brb_v = w_br_b[0].rearrange("(k p) n -> p k n", p=P)
    w_out_v = w_out[0].rearrange("(k p) n -> p k n", p=P)
    w_router_v = w_router[0].rearrange("(k p) n -> p k n", p=P)
    w_gate_v = w_e_gate[0].rearrange("e (k p) n -> e p k n", p=P)
    w_up_v = w_e_up[0].rearrange("e (k p) n -> e p k n", p=P)
    w_down_v = w_e_down[0].rearrange("e (k p) n -> e p k n", p=P)
    sig_v = sig_gates.rearrange("(m p) s -> p m s", p=P)

    ctx = ExitStack()
    with ctx:
        KB = 1024
        sizes = {"ring": 48 * KB, "ada": 20 * KB, "A": 64 * KB, "B": 37 * KB, "C": 32 * KB, "small": 6 * KB + 512}
        arena_at = (nc.sbuf_base + 31) // 32 * 32
        ctx.enter_context(nc.sbuf_tensor("arena", [P, sum(sizes.values()) // 4], F32))
        start = arena_at
        base = {}
        for name, size in sizes.items():
            base[name] = start
            start += size

        def at(region, offset, name, shape, dt=F32):
            size = 4 * math.prod(shape[1:])
            assert offset + size <= sizes[region], (name, offset, size)
            return nc.alloc_sbuf_tensor_at(name, shape, dt, offset=base[region] + offset)

        stage = at("ring", 0, "stage", [P, NSTAGE, 2, W])
        w_hi = at("ring", 32 * KB, "w_hi", [P, NSPLIT, 2, W], F32R)
        w_lo = at("ring", 40 * KB, "w_lo", [P, NSPLIT, 2, W], F32R)
        ada_tile = at("ada", 0, "ada_tile", [P, NADA, ADA_W])
        ada_acc = at("ada", 16 * KB, "ada_acc", [P, ADA_W])
        acc_first = [at("A", (48 + 4 * i) * KB, f"acc_first{i}", [P, ADA_W]) for i in range(ADA_FIRST)]
        wq = at("ada", 0, "wq", [P, 2, 4, 256])
        wkv = at("ada", 8 * KB, "wkv", [P, 2, 2, 256])
        q_stage = at("ada", 0, "q_stage", [P, T, DH])
        k_stage = at("ada", 2 * KB, "k_stage", [P, T, DH])
        cqT = at("ada", 12 * KB, "cqT", [P, 4, S])
        gt_row = at("ada", 0, "gt_row", [P, D])
        sel = at("ada", 8 * KB, "sel", [P, T, 2, CAP])
        selT = at("ada", 10 * KB, "selT", [P, S], F32R)
        gu = at("ada", 12 * KB, "gu", [P, 2, W])
        sgm = at("ada", 16 * KB, "sgm", [P, 256])
        h32e = at("ada", 17 * KB, "h32e", [P, 256])
        xg32 = at("ada", 18 * KB, "xg32", [P, 4, P])
        h2T = at("ada", 12 * KB, "h2T", [P, 2, S])
        w_rt = at("ada", 16 * KB, "w_rt", [P, KD, NE])
        shiftT = at("ada", 17 * KB, "shiftT", [NE, P])
        shift_row = at("ada", 17 * KB + 512, "shift_row", [P, NE])
        hT_hi = at("A", 0, "hT_hi", [P, KD, S], F32R)
        hT_lo = at("A", 32 * KB, "hT_lo", [P, KD, S], F32R)
        oT_hi = at("A", 0, "oT_hi", [P, KD, S], F32R)
        oT_lo = at("A", 32 * KB, "oT_lo", [P, KD, S], F32R)
        mT_hi = at("A", 0, "mT_hi", [P, KD, S], F32R)
        mT_lo = at("A", 32 * KB, "mT_lo", [P, KD, S], F32R)
        xgT = [at("A", 0, "xgT0", [P, KD, 2, P], F32R), at("A", 48 * KB, "xgT1", [P, KD, 2, P], F32R)]
        heT = at("A", 16 * KB, "heT", [P, 8, P], F32R)
        diag1 = at("A", 22 * KB, "diag1", [P, 4, P])
        ysum = at("A", 24 * KB, "ysum", [P, 4, W])
        y_hi = at("A", 32 * KB, "y_hi", [P, 4, W], F32R)
        y_lo = at("A", 40 * KB, "y_lo", [P, 4, W], F32R)
        ytmp = at("A", 20 * KB, "ytmp", [64, W])
        affT = at("A", 20 * KB, "affT", [NE, S])
        work = at("A", 22 * KB, "work", [NE, 2, S])
        gt_m = at("A", 26 * KB, "gt_m", [NE, S])
        eq_m = at("A", 28 * KB, "eq_m", [NE, S])
        rank = at("A", 30 * KB, "rank", [NE, S])
        slotT = at("A", 58 * KB, "slotT", [NE, S])
        res = [at("A", 8 * i * KB, f"res{i}", [P, D]) for i in (0, 1, 6, 7)]
        x_sb = at("B", 0, "x_sb", [P, T, D])
        zc = at("B", 0, "zc", [P, T, LAT])
        zg = at("B", 13 * KB, "zg", [P, T, GQ])
        mT = at("B", 0, "mT", [P, KD, S])
        x1 = at("B", 0, "x1", [P, T, D])
        probs1 = at("B", 0, "probs1", [P, T, S])
        h32 = at("C", 0, "h32", [P, 4, S])
        junk = at("C", 8 * KB, "junk", [P, D])
        sig = at("C", 0, "sig", [P, 4, S])
        g_row = at("C", 16 * KB, "g_row", [P, HG + KVG, DH])
        rope_kc = at("C", 21 * KB, "rope_kc", [P, T, 32])
        rope_ks = at("C", 21 * KB + 512, "rope_ks", [P, T, 32])
        rope_gc = at("C", 22 * KB, "rope_gc", [P, T, 2, 32])
        rope_gs = at("C", 23 * KB, "rope_gs", [P, T, 2, 32])
        NR = (HG + KVG) * 2 * 32
        r_a = at("C", 8 * KB, "r_a", [P, HG + KVG, 2, 32])
        r_b = at("C", 8 * KB + 4 * NR, "r_b", [P, HG + KVG, 2, 32])
        r_c = at("C", 24 * KB, "r_c", [P, HG + KVG, 2, 32])
        r_d = at("C", 24 * KB + 4 * NR, "r_d", [P, HG + KVG, 2, 32])
        kr2 = at("C", 30 * KB, "kr2", [P, T, P])
        probs0 = at("C", 0, "probs0", [P, T, S])
        pT = at("C", 8 * KB, "pT", [P, 2, S])
        qn = at("C", 12 * KB, "qn", [P, S])
        qr = at("C", 14 * KB, "qr", [P, S])
        kn = at("C", 16 * KB, "kn", [P, S])
        v_sb = at("C", 18 * KB, "v_sb", [P, 2, T, DH])
        krT = at("C", 22 * KB, "krT", [P, S])
        ckvT = at("C", 24 * KB, "ckvT", [P, 2, S])
        sg_in = at("C", 0, "sg_in", [P, 2, 4, S])
        m_tmp = at("C", 16 * KB, "m_tmp", [P, S])
        diag0 = at("C", 18 * KB, "diag0", [P, 4, P])
        junk3 = at("C", 20 * KB, "junk3", [P, W])
        xn = at("C", 0, "xn", [P, T, D])
        gf_row = at("C", 0, "gf_row", [P, D])
        probs = [probs0, probs1]

        small_at = [0]

        def small(name, shape, dt=F32):
            o = small_at[0]
            small_at[0] += (4 * math.prod(shape[1:]) + 31) // 32 * 32
            return at("small", o, name, shape, dt)

        ident = small("ident", [P, P])
        foldm = small("foldm", [P, 64])
        iota = small("iota", [P, 64])
        qtab = small("qtab", [P, S])
        ones = small("ones", [P, P])
        modcol = small("modcol", [P, 96])
        bcol = small("bcol", [P, 96])
        pcol = small("pcol", [P, 54])
        siluc = small("siluc", [P, 16])
        a1 = small("a1", [P, KD])
        ssq = small("ssq", [P, 16])
        rstd = small("rstd", [P, 16])
        unused = small("unused", [P, 1])
        ssq2 = small("ssq2", [P, T, 4])
        zssq = small("zssq", [P, 16, T])
        zr = small("zr", [P, 16, T])
        eps_c = small("eps_c", [P, 1])
        nmax = small("nmax", [P, 2, 8])
        rsum = small("rsum", [P, 2, 8])
        aff = small("aff", [P, T, NE + 2])
        slots = small("slots", [P, T, NE + 2])
        lmx = small("lmx", [P, 8])
        val = small("val", [P, 1])
        m8 = small("m8", [NE, 8])
        cnt = small("cnt", [NE, 2])
        prow = at("C", 24 * KB, "prow", [54, P])
        brow = at("C", 26 * KB, "brow", [96, P])

        bank = [ctx.enter_context(nc.psum_tensor(f"bank{i}", [P, W], F32)) for i in range(8)]

        def sem(name):
            return ctx.enter_context(nc.semaphore(name))

        stage_full = [sem(f"stage_full{i}") for i in range(NSTAGE)]
        hi_ready, lo_ready, chunk_used = sem("hi_ready"), sem("lo_ready"), sem("chunk_used")
        acc_done, acc_free = sem("acc_done"), sem("acc_free")
        consts_in, x_in, rows_in = sem("consts_in"), sem("x_in"), sem("rows_in")
        cols_done, cols_ready, sigc_ready, siluc_ready = sem("cols_done"), sem("cols_ready"), sem("sigc_ready"), sem("siluc_ready")
        ada_full = [sem(f"ada_full{i}") for i in range(NADA)]
        ada_done, ada_col_done, ada_col_ready = sem("ada_done"), sem("ada_col_done"), sem("ada_col_ready")
        act_seq, dve_seq, pool_seq = sem("act_seq"), sem("dve_seq"), sem("pool_seq")
        a1_ready = sem("a1_ready")
        std_ready, rstd_ready, xn_ready = sem("std_ready"), sem("rstd_ready"), sem("xn_ready")
        xT_done, h32_ready, hT_hi_ready, hT_lo_ready = sem("xT_done"), sem("h32_ready"), sem("hT_hi_ready"), sem("hT_lo_ready")
        tab_in = sem("tab_in")
        zstd_ready, zr_ready, zpost_ready = sem("zstd_ready"), sem("zr_ready"), sem("zpost_ready")
        sig_out = [sem(f"sig_out{i}") for i in range(4)]
        pro_done, pro_ready = sem("pro_done"), sem("pro_ready")
        hw_full = [sem("hw_full0"), sem("hw_full1")]
        qn_done, qr_done, kn_done, v_done = sem("qn_done"), sem("qr_done"), sem("kn_done"), sem("v_done")
        qn_ready, qr_ready, kn_ready, v_ready = sem("qn_ready"), sem("qr_ready"), sem("kn_ready"), sem("v_ready")
        qs_ready, ks_ready = sem("qs_ready"), sem("ks_ready")
        s_done, nmax_ready, exp_done, p_ready = sem("s_done"), sem("nmax_ready"), sem("exp_done"), sem("p_ready")
        nmx_seq, rinv_seq = sem("nmx_seq"), sem("rinv_seq")
        pT_done, pT_ready, pv_done, o_hi, o_lo = sem("pT_done"), sem("pT_ready"), sem("pv_done"), sem("o_hi"), sem("o_lo")
        sg_full = [sem("sg_full0"), sem("sg_full1")]
        diag_ready, row_done, row_ready = sem("diag_ready"), sem("row_done"), sem("row_ready")
        mT_ready, m_hi, m_lo, x1_in, x1_ready = sem("mT_ready"), sem("m_hi"), sem("m_lo"), sem("x1_in"), sem("x1_ready")
        sq2_seq, shift_done, shift_ready, lgT_ready, lg_done = (
            sem("sq2_seq"), sem("shift_done"), sem("shift_ready"), sem("lgT_ready"), sem("lg_done"))
        wr_in, std2_ready, rstd2_ready, xn2_ready = sem("wr_in"), sem("std2_ready"), sem("rstd2_ready"), sem("xn2_ready")
        h2T_done, h2T_ready, logit_done = sem("h2T_done"), sem("h2T_ready"), sem("logit_done")
        lsub_ready, lexp_ready, aff_ready, affT_done, slotT_ready, slots_done = (
            sem("lsub_ready"), sem("lexp_ready"), sem("aff_ready"), sem("affT_done"), sem("slotT_ready"), sem("slots_done"))
        sel_ready, selT_done, selT_ready, val_done, val_ready = sem("sel_ready"), sem("selT_done"), sem("selT_ready"), sem("val_done"), sem("val_ready")
        gather_done, xg32_ready, xg_hi, xg_ready = sem("gather_done"), sem("xg32_ready"), sem("xg_hi"), sem("xg_ready")
        fold_done, sgm_ready, he32_ready, he_hi, he_ready = (
            sem("fold_done"), sem("sgm_ready"), sem("he32_ready"), sem("he_hi"), sem("he_ready"))
        he_mid = sem("he_mid")
        ytmp_ready, y32_ready, yhi_ready, ylo_ready = sem("ytmp_ready"), sem("y32_ready"), sem("yhi_ready"), sem("ylo_ready")
        scat_done, scat_added = sem("scat_done"), sem("scat_added")
        gf_in, std3_ready, rstd3_ready, res_ready = sem("gf_in"), sem("std3_ready"), sem("rstd3_ready"), sem("res_ready")
        stored = sem("stored")

        block = ctx.enter_context(nc.Block())

        def wait_bank(eng, blk, b, n_end):
            if b < 3:
                eng.wait_ge(acc_done, 3 * blk + b + 1)
            else:
                eng.wait_ge(chunk_used, n_end + NSPLIT)

        @block.sync
        def _(sp):
            def load_chunk(n, c, src):
                sp.wait_ge(lo_ready, n + 1)
                width = src.shape[2]
                sp.dma_start(stage[:, c % NSTAGE, :, 0:width], src).then_inc(stage_full[c % NSTAGE], 16)

            def load_ada(m, k, r):
                sp.wait_ge(ada_done, m + 1)
                sp.dma_start(ada_tile[:, k % NADA, :], w_ada_v[:, k, ds(r * ADA_W, ADA_W)]).then_inc(ada_full[k % NADA], 16)

            for t in range(2):
                sp.dma_start(x_sb[:, t, :], x_v[:, t, :]).then_inc(x_in, 16)
            for row, n, src in ((0, 16, g_mix[0]), (16, 16, g_ffn[0]), (32, 16, c[0]), (48, 4, g_cq[0]), (52, 2, g_ckv[0])):
                sp.dma_start(prow[row:row + n, :], src.rearrange("(k p) -> k p", p=P)).then_inc(rows_in, 16)
            sp.dma_start(brow[:, :], b_ada[0].rearrange("(k p) -> k p", p=P)).then_inc(rows_in, 16)
            for dst, a, b in ((ident, C_ID, C_FOLD), (foldm, C_FOLD, C_IOTA), (iota, C_IOTA, C_QTAB), (qtab, C_QTAB, C_KC)):
                sp.dma_start(dst[:, :], consts[:, a:b]).then_inc(consts_in, 16)
            for t in range(2, T):
                sp.dma_start(x_sb[:, t, :], x_v[:, t, :]).then_inc(x_in, 16)
            for i, r in enumerate(ADA_ORDER):
                for k in range(KD):
                    load_ada(KD * i + k, k, r)
                for c8 in ((), range(4), (), range(4, 8))[i]:
                    load_chunk(N_Z + c8, c8, w_in_v[:, 2 * c8:2 * c8 + 2, 0:QR])
            for c8 in range(8):
                load_chunk(N_Z + 8 + c8, c8, w_in_v[:, 2 * c8:2 * c8 + 2, QR:LAT])
            with sp.Fori(0, 3) as j:
                for c8 in range(8):
                    load_chunk(N_Z + 16 + 8 * j + c8, c8, w_in_v[:, 2 * c8:2 * c8 + 2, ds(LAT + W * j, W)])
            def load_gate(j, c8):
                load_chunk(N_GATE + 8 * j + c8, c8, w_in_v[:, 2 * c8:2 * c8 + 2, ds(LAT + GQ + W * j, W)])

            def load_branches(first, end):
                for c in range(first, end):
                    load_chunk(N_BR + c, c, (w_bra_v, w_brb_v)[c // 4][:, 2 * (c % 4):2 * (c % 4) + 2, 0:W])

            def load_ada_at(j, c8):
                for k in ADA_AT[c8]:
                    load_ada(KD * (j + ADA_FIRST) + k, k, j + ADA_FIRST)

            for c8 in range(AHEAD):
                load_gate(0, c8)
            with sp.Fori(0, 7) as j:
                for c8 in range(8):
                    load_gate(j + (c8 + AHEAD) // 8, (c8 + AHEAD) % 8)
                    load_ada_at(j, c8)
            for c8 in range(8):
                if c8 + AHEAD < 8:
                    load_gate(7, c8 + AHEAD)
                else:
                    load_branches(c8 + AHEAD - 8, c8 + AHEAD - 7)
                load_ada_at(7, c8)
            load_branches(AHEAD, 8)

            def head_weights(b, H):
                sp.dma_start(wq[:, b, :, 0:192], w_uq_v[:, :, ds(H * 192, 192)]).then_inc(hw_full[b], 16)
                sp.dma_start(wq[:, b, :, 192:224], w_uq_v[:, :, ds(H * 192 + 160, 32)]).then_inc(hw_full[b], 16)
                sp.dma_start(wq[:, b, :, 224:256], w_uq_v[:, :, ds(H * 192 + 128, 32)]).then_inc(hw_full[b], 16)
                sp.dma_start(wkv[:, b, :, :], w_ukv_v[:, :, ds(H * 256, 256)]).then_inc(hw_full[b], 16)

            sp.wait_ge(ada_done, NADA + KD * ADA_BLOCKS)
            head_weights(0, 0)
            head_weights(1, 1)
            with sp.Fori(0, 3) as i:
                for b in range(2):
                    sp.wait_ge(kn_done, 2 * i + b + 1)
                    head_weights(b, 2 * i + 2 + b)

            def load_gates(ab, j):
                sp.dma_start(sg_in[:, ab, :, :], sig_v[:, ds(KD * ab + 4 * j, 4), :]).then_inc(sg_full[ab], 16)

            for i in range(4):
                sp.wait_ge(sig_out[i], 16 * 9)
            sp.wait_ge(o_lo, 2 + HM + HG)
            load_gates(0, 0)
            load_gates(1, 0)
            with sp.Fori(1, 4) as j:
                for c4 in range(4):
                    load_chunk(N_BR + 8 * j + c4, c4, w_bra_v[:, 2 * c4:2 * c4 + 2, ds(W * j, W)])
                sp.wait_ge(acc_free, G_BR + 8 * j)
                load_gates(0, j)
                for c4 in range(4):
                    load_chunk(N_BR + 8 * j + 4 + c4, 4 + c4, w_brb_v[:, 2 * c4:2 * c4 + 2, ds(W * j, W)])
                sp.wait_ge(acc_free, G_BR + 8 * j + 4)
                load_gates(1, j)
            for c8 in range(8):
                load_chunk(N_OUT + c8, c8, w_out_v[:, 2 * c8:2 * c8 + 2, 0:W])
            sp.dma_start(w_rt[:, :, :], w_router_v).then_inc(wr_in, 16)
            for t in range(T):
                sp.wait_ge(m_lo, 4 * t + 4)
                sp.dma_start(x1[:, t, :], x_v[:, t, :]).then_inc(x1_in, 16)
            with sp.Fori(1, 4) as j:
                for c8 in range(8):
                    load_chunk(N_OUT + 8 * j + c8, c8, w_out_v[:, 2 * c8:2 * c8 + 2, ds(W * j, W)])
            def load_expert_chunk(p, e, cc, src):
                n, c = N_EXP + 96 * p + 48 * e + cc, cc % NSTAGE
                before = 48 * e + cc - NSTAGE
                if unsplit(before):
                    sp.wait_ge(chunk_used, n - NSTAGE + 1 + NSPLIT)
                else:
                    sp.wait_ge(lo_ready, N_EXP + SPLIT_PER_PAIR * p + split_index(before) + 1 + NSTAGE)
                sp.dma_start(stage[:, c, :, :], src).then_inc(stage_full[c], 16)

            def load_pair(p, first):
                for e in range(2):
                    for cc in range(48):
                        if cc < 32:
                            a, c8 = cc // 8, cc % 8
                            w_v, jb, k0 = (w_gate_v, w_up_v)[a % 2], a // 2, 2 * c8
                        else:
                            w_v, (jb, kc) = w_down_v, DOWN[cc - 32]
                            k0 = 2 * kc
                        src = w_v[2 * p + e][:, k0:k0 + 2, jb * W:(jb + 1) * W]
                        if first and e == 0 and cc < NSTAGE:
                            load_chunk(N_EXP + cc, cc, src)
                        else:
                            load_expert_chunk(p, e, cc, src)

            load_pair(0, True)
            with sp.Fori(1, PAIRS) as p:
                load_pair(p, False)
            sp.wait_ge(xg_ready, 4 * PAIRS)
            sp.dma_start(gf_row[:, :], g_final.partition_broadcast(P)).then_inc(gf_in, 16)
            for t in range(T):
                sp.wait_ge(res_ready, t + 1)
                sp.dma_start(out_v[:, t, :], res[t][:, :]).then_inc(stored, 16)
            sp.wait_ge(stored, 16 * T)

        @block.tensor
        def _(pe):
            mm = nc.tensor.matmul
            pe.sem_inc(chunk_used, NSPLIT)
            pe.wait_ge(rows_in, 16 * 6)
            pe.wait_ge(consts_in, 16 * 4)
            nc.tensor.transpose(bank[5][:, 0:54], prow[:, :], ident[0:54, 0:54])
            nc.tensor.transpose(bank[5][:, 64:160], brow[:, :], ident[0:96, 0:96]).then_inc(cols_done, 1)

            def ada_columns(r, ada_acc=ada_acc):
                pe.wait_ge(ada_done, KD * r + KD + NADA)
                pe.wait_ge(ada_col_ready, r + 1)
                for i in range(8):
                    last = mm(bank[4][:, i:i + 1], ada_acc[:, i * P:(i + 1) * P], ones[:, 0:1], start=True, stop=True)
                last.then_inc(ada_col_done, 1)

            for i in range(2):
                ada_columns(i, acc_first[i])

            def dense_block(n0, g0, chunks, k0, act_hi, act_lo, weights_stationary, width=W, ready=None, before=None):
                for cc in range(chunks):
                    if before is not None:
                        before(cc)
                    if ready is not None:
                        pe.wait_ge(ready, 2 * cc + 2)
                    pe.wait_ge(hi_ready, n0 + cc + 1)
                    s = (k0 // 2 + cc) % NSPLIT
                    for b in range(4):
                        if cc == 0:
                            pe.wait_ge(acc_free, g0 + b + 1)
                        passes = [(act_hi, w_hi), (act_lo, w_hi), (act_hi, w_lo)]
                        for i, (a, w) in enumerate(passes):
                            if b == 0 and i == 2:
                                pe.wait_ge(lo_ready, n0 + cc + 1 + NSTAGE)
                            for kk in range(2):
                                first = cc == 0 and i == 0 and kk == 0
                                end = cc == chunks - 1 and i == 2 and kk == 1
                                k = 2 * cc + kk + k0
                                if weights_stationary:
                                    last = mm(bank[b][:, :], w[:, s, kk, b * P:(b + 1) * P], a[:, k, :], start=first, stop=end)
                                else:
                                    last = mm(bank[b][:, 0:width], a[:, k, b * P:(b + 1) * P], w[:, s, kk, 0:width], start=first, stop=end)
                        if b == 3:
                            last.then_inc(chunk_used, 1)
                        elif cc == chunks - 1:
                            last.then_inc(acc_done, 1)

            pe.wait_ge(xn_ready, T)

            def transpose_x(k):
                if k >= 3:
                    pe.wait_ge(h32_ready, k - 2)
                for t in range(T):
                    last = nc.tensor.transpose(bank[5 + k % 3][:, t * P:(t + 1) * P], x_sb[:, t, k * P:(k + 1) * P], ident[:, :])
                last.then_inc(xT_done, 1)

            for k in range(3):
                transpose_x(k)

            def transposes_ahead(cc):
                if cc == 4:
                    for i in (2, 3):
                        ada_columns(i, acc_first[i])
                for k in (2 * cc + 3, 2 * cc + 4):
                    if k < KD:
                        transpose_x(k)

            dense_block(N_Z, G_Z, 8, 0, hT_hi, hT_lo, False, ready=hT_lo_ready, before=transposes_ahead)
            dense_block(N_Z + 8, G_Z + 4, 8, 0, hT_hi, hT_lo, False, width=LAT - QR)
            with pe.Fori(0, 3) as j:
                dense_block(N_Z + 16 + 8 * j, G_Z + 8 + 4 * j, 8, 0, hT_hi, hT_lo, False)
            with pe.Fori(0, 8) as j:
                dense_block(N_GATE + 8 * j, G_GATE + 4 * j, 8, 0, hT_hi, hT_lo, True)
                ada_columns(j + ADA_FIRST)

            pe.wait_ge(zpost_ready, 1)
            pe.wait_ge(ada_col_ready, ADA_BLOCKS + 1)
            for i in range(7):
                if i >= 4:
                    pe.wait_ge(pro_ready, i - 3)
                for t in range(T):
                    src = kr2[:, t, :] if i == 6 else zc[:, t, i * P:(i + 1) * P]
                    last = nc.tensor.transpose(bank[4 + i % 4][:, t * P:(t + 1) * P], src, ident[:, :])
                last.then_inc(pro_done, 1)

            def project_mla(H, b, use):
                pe.wait_ge(hw_full[b], 64 * use)
                pe.wait_ge(v_ready, H + 1)
                for k in range(4):
                    last = mm(bank[5][:, :], wq[:, b, k, P:2 * P], cqT[:, k, :], start=k == 0, stop=k == 3)
                last.then_inc(qr_done, 1)
                pe.wait_ge(o_lo, H + 1)
                for k in range(4):
                    last = mm(bank[4][:, :], wq[:, b, k, 0:P], cqT[:, k, :], start=k == 0, stop=k == 3)
                last.then_inc(qn_done, 1)
                pe.wait_ge(qr_ready, H + 1)
                for t in range(T):
                    for k in range(2):
                        last = mm(bank[5][:, t * P:(t + 1) * P], ckvT[:, k, t * P:(t + 1) * P], wkv[:, b, k, P:2 * P],
                                  start=k == 0, stop=k == 1)
                last.then_inc(v_done, 1)
                pe.wait_ge(qn_ready, H + 1)
                for k in range(2):
                    last = mm(bank[4][:, :], wkv[:, b, k, 0:P], ckvT[:, k, :], start=k == 0, stop=k == 1)
                last.then_inc(kn_done, 1)

            def scores_mla(H):
                for qb in range(4):
                    pe.wait_ge(exp_done, 4 * H + qb + 1)
                    mm(bank[qb][:, :], qr[:, qb * P:(qb + 1) * P], krT[:, :], start=True, stop=False)
                    if qb == 0:
                        pe.wait_ge(kn_ready, H + 1)
                    mm(bank[qb][:, :], qn[:, qb * P:(qb + 1) * P], kn[:, :], start=False, stop=True).then_inc(s_done, 1)

            def attend(Hp, b):
                pe.wait_ge(p_ready, Hp + 1)

                def times_v(kt):
                    pe.wait_ge(pT_ready, 4 * Hp + kt + 3)
                    if kt == 0:
                        pe.wait_ge(o_lo, Hp + 2)
                    mm(bank[4][:, :], v_sb[:, b, kt, :], pT[:, kt % 2, :], start=kt == 0, stop=kt == 3).then_inc(pv_done, 1)

                for kt in range(4):
                    pe.wait_ge(pT_ready, 4 * Hp + kt + 1)
                    for qb in range(4):
                        last = nc.tensor.transpose(bank[6 + kt % 2][:, qb * P:(qb + 1) * P],
                                                   probs[b][:, qb, kt * P:(kt + 1) * P], ident[:, :])
                    last.then_inc(pT_done, 1)
                    if kt >= 1:
                        times_v(kt - 1)
                times_v(3)

            pe.wait_ge(pro_ready, 7)
            project_mla(0, 0, 1)
            scores_mla(0)
            with pe.Fori(0, 3) as i:
                project_mla(2 * i + 1, 1, i + 1)
                scores_mla(2 * i + 1)
                attend(2 * i, 0)
                project_mla(2 * i + 2, 0, i + 2)
                scores_mla(2 * i + 2)
                attend(2 * i + 1, 1)
            def transpose_q(H):
                pe.wait_ge(qs_ready, H - HM + 1)
                for t in range(T):
                    last = nc.tensor.transpose(bank[5][:, t * P:(t + 1) * P], q_stage[:, t, :], ident[:, :])
                last.then_inc(qn_done, 1)

            project_mla(7, 1, 4)
            scores_mla(7)
            pe.wait_ge(v_ready, HM + 1)
            transpose_q(HM)
            attend(6, 0)
            with pe.Fori(0, 2) as n:
                for g in range(4):
                    H = 4 * n + g + HM
                    if g == 0:
                        pe.wait_ge(ks_ready, n + 1)
                        pe.wait_ge(o_lo, H + 1)
                        for t in range(T):
                            last = nc.tensor.transpose(bank[4][:, t * P:(t + 1) * P], k_stage[:, t, :], ident[:, :])
                        last.then_inc(kn_done, 1)
                        pe.wait_ge(kn_ready, n + HM + 1)
                    pe.wait_ge(qn_ready, H + 1)
                    for qb in range(4):
                        pe.wait_ge(exp_done, 4 * H + qb + 1)
                        mm(bank[qb][:, :], qn[:, qb * P:(qb + 1) * P], kn[:, :], start=True, stop=True).then_inc(s_done, 1)
                    transpose_q(H + 1)
                    pe.wait_ge(v_ready, H + 1)
                    attend(H - 1, (g + 1) % 2)
            pe.wait_ge(v_ready, HM + HG + 1)
            attend(HM + HG - 1, 1)

            def gate_row(q, diag):
                pe.wait_ge(diag_ready, q + 1)
                mm(bank[5][:, :], ones[:, :], diag[:, :, :], start=True, stop=True).then_inc(row_done, 1)

            pe.wait_ge(o_lo, HM + HG + 2)
            with pe.Fori(0, 4) as j:
                dense_block(N_BR + 8 * j, G_BR + 8 * j, 4, 0, oT_hi, oT_lo, True)
                gate_row(j, diag0)
                dense_block(N_BR + 4 + 8 * j, G_BR + 4 + 8 * j, 4, 8, oT_hi, oT_lo, True)
            def transpose_x1(jb, i):
                k = 4 * jb + i
                if i == 0:
                    pe.wait_ge(x1_ready, 4 * jb + 4)
                if k >= 2:
                    pe.wait_ge(h2T_ready, k - 1)
                for t in range(T):
                    last = nc.tensor.transpose(bank[4 + i % 2][:, t * P:(t + 1) * P], x1[:, t, k * P:(k + 1) * P], ident[:, :])
                last.then_inc(h2T_done, 1)

            def logits(jb, i):
                k = 4 * jb + i
                pe.wait_ge(h2T_ready, k + 1)
                mm(bank[6][0:NE, :], w_rt[:, k, :], h2T[:, i % 2, :], start=k == 0, stop=k == KD - 1)\
                    .then_inc(logit_done, 1)

            def route_beside(jb):
                def before(cc):
                    if 2 <= cc < 6:
                        transpose_x1(jb, cc - 2)
                    if cc >= 4:
                        logits(jb, cc - 4)
                return before

            dense_block(N_OUT, G_OUT, 8, 0, mT_hi, mT_lo, False, ready=m_lo)
            pe.wait_ge(row_ready, 4)
            pe.wait_ge(wr_in, 16)
            for k in range(KD):
                last = mm(bank[7][0:NE, 0:1], w_rt[:, k, :], modcol[:, 48 + k:49 + k], start=k == 0, stop=k == KD - 1)
            last.then_inc(shift_done, 1)
            dense_block(N_OUT + 8, G_OUT + 4, 8, 0, mT_hi, mT_lo, False, before=route_beside(0))
            pe.wait_ge(shift_ready, 1)
            mm(bank[7][:, 64:64 + NE], shiftT[:, :], ident[0:NE, 0:NE], start=True, stop=True).then_inc(shift_done, 1)
            for j in (2, 3):
                dense_block(N_OUT + 8 * j, G_OUT + 4 * j, 8, 0, mT_hi, mT_lo, False, before=route_beside(j - 1))
            for i in range(6):
                if i < 4:
                    transpose_x1(3, i)
                if i >= 2:
                    logits(3, i - 2)
            pe.wait_ge(lgT_ready, 1)
            for t in range(T):
                last = nc.tensor.transpose(bank[7][:, t * NE:(t + 1) * NE], work[:, 0, t * P:(t + 1) * P], ident[0:NE, 0:NE])
            last.then_inc(lg_done, 1)
            pe.wait_ge(aff_ready, 1)
            for t in range(T):
                last = nc.tensor.transpose(bank[4][0:NE, t * P:(t + 1) * P], aff[:, t, 0:NE], ident[:, :])
            last.then_inc(affT_done, 1)
            pe.wait_ge(slotT_ready, 1)
            for t in range(T):
                last = nc.tensor.transpose(bank[5][:, t * NE:(t + 1) * NE], slotT[:, t * P:(t + 1) * P], ident[0:NE, 0:NE])
            last.then_inc(slots_done, 1)

            def gather(b, u, tiles=range(4)):
                for i in tiles:
                    for t in range(T):
                        last = mm(bank[b][:, i * P:(i + 1) * P], xn[:, t, (4 * u + i) * P:(4 * u + i + 1) * P],
                                  sel[:, t, :, :], start=t == 0, stop=t == T - 1)
                if 3 in tiles:
                    last.then_inc(gather_done, 1)

            def scatter(p, jd):
                pe.wait_ge(ylo_ready, 4 * p + jd + 1)
                for t in range(T):
                    pe.wait_ge(scat_added, 16 * p + 4 * jd + t + 1)
                    mm(bank[4 + t][:, :], selT[:, t * P:(t + 1) * P], y_hi[:, jd, :], start=True, stop=False)
                    mm(bank[4 + t][:, :], selT[:, t * P:(t + 1) * P], y_lo[:, jd, :], start=False, stop=True)\
                        .then_inc(scat_done, 1)

            def expert_chunk(p, e, cc, b, first, end, acts):
                c = cc % NSTAGE
                if first:
                    g0 = G_EXP + 16 * p + 8 * e
                    pe.wait_ge(acc_free, g0 + (cc // 8 if cc < 32 else 4 + DOWN[cc - 32][0]) + 1)
                if unsplit(48 * e + cc):
                    pe.wait_ge(stage_full[c], 2 * (N_EXP + 96 * p + 48 * e + cc - c) + 16)
                    for kk in range(2):
                        last = mm(bank[b][:, :], acts[kk].bitcast(F32), stage[:, c, kk, :], start=first and kk == 0, stop=end and kk == 1)
                else:
                    k = N_EXP + SPLIT_PER_PAIR * p + split_index(48 * e + cc)
                    s = split_index(48 * e + cc) % NSPLIT
                    pe.wait_ge(hi_ready, k + 1)
                    for kk in range(2):
                        mm(bank[b][:, :], acts[kk], w_hi[:, s, kk, :], start=first and kk == 0, stop=False)
                    pe.wait_ge(lo_ready, k + 1 + NSTAGE)
                    for kk in range(2):
                        last = mm(bank[b][:, :], acts[kk], w_lo[:, s, kk, :], start=False, stop=end and kk == 1)
                last.then_inc(chunk_used, 1)

            def fold(p, e, jb):
                pe.wait_ge(acc_free, G_EXP + 16 * p + 8 * e + 2 * jb + 6)
                if jb == 0 and e == 0 and not (isinstance(p, int) and p == 0):
                    pe.wait_ge(scat_added, 16 * (p - 1) + 4 * sum(c < FOLD_AT[0] for c in SCATTER_AT) + 4)
                for s in range(2):
                    for f in range(4):
                        last = mm(bank[4][:, s * 256 + f * 64:s * 256 + (f + 1) * 64], gu[:, s, f * P:(f + 1) * P],
                                  foldm[:, :], start=True, stop=True)
                last.then_inc(fold_done, 1)

            def pe_pair(p, turn, first, last_pair):
                for e in range(2):
                    for cc in range(48):
                        if first and e == 0 and cc in (2, 4):
                            gather(5 + cc // 2, 1 + cc // 2)
                        if first and e == 0 and cc < 8 and cc % 2 == 0:
                            pe.wait_ge(xg_ready, cc // 2 + 1)
                        if cc == 0 and e == 0 and not first:
                            pe.wait_ge(xg_ready, 4 * p + 4)
                        if cc < 32:
                            a, c8 = cc // 8, cc % 8
                            expert_chunk(p, e, cc, a, c8 == 0, c8 == 7, [xgT[turn][:, 2 * c8 + kk, e, :] for kk in range(2)])
                        else:
                            jd, kc = DOWN[cc - 32]
                            if cc == 32:
                                pe.wait_ge(he_ready, 4 * p + 2 * e + 3)
                            if cc == 38:
                                pe.wait_ge(he_ready, 4 * p + 2 * e + 4)
                            expert_chunk(p, e, cc, jd, kc == 0, kc == 3, [heT[:, 2 * kc + kk, :] for kk in range(2)])
                        if cc == FOLD_AT[0]:
                            fold(p, e, 0)
                        if cc == FOLD_AT[1]:
                            fold(p, e, 1)
                        if e == 0:
                            if not first and cc in SCATTER_AT:
                                if cc > FOLD_AT[0]:
                                    pe.wait_ge(he32_ready, 4 * p + 1)
                                scatter(p - 1, SCATTER_AT.index(cc))
                            if cc == 26:
                                pe.wait_ge(scat_added, 16 * p + 4)
                                for t in range(T):
                                    last = nc.tensor.transpose(bank[6][:, t * P:(t + 1) * P], sel[:, t, :, :], ident[:, :])
                                last.then_inc(selT_done, 1)
                                for t in range(T):
                                    last = mm(bank[7][:, 0:2], sel[:, t, :, :], aff[:, t, ds(2 * p, 2)], start=t == 0, stop=t == T - 1)
                                last.then_inc(val_done, 1)
                            if first and cc in (5, 9, 13, 17):
                                gate_row(4 + cc // 4 - 1, diag1)
                        if not last_pair:
                            if GATHER_FROM <= 48 * e + cc < GATHER_FROM + 32 and cc % 8 in (0, 1, 3, 4):
                                u, i = (48 * e + cc - GATHER_FROM) // 8, (0, 1, 3, 4).index(cc % 8)
                                if u == 0 and i == 0:
                                    pe.wait_ge(sel_ready, p + 2)
                                if i == 0:
                                    pe.wait_ge(xg32_ready, 4 * p + 4 + u)
                                gather(5, u, [i])
                        elif e == 1:
                            if cc == 40:
                                pe.wait_ge(he32_ready, 4 * p + 4)
                                pe.wait_ge(selT_ready, p + 1)
                            if cc in (43, 45, 47):
                                scatter(p, (cc - 43) // 2)
                    if e == 0:
                        pe.wait_ge(selT_ready, p + 1)
                        pe.wait_ge(val_ready, p + 1)
                if last_pair:
                    scatter(p, 3)

            pe.wait_ge(sel_ready, 1)
            pe.wait_ge(xn2_ready, T)
            for u in range(2):
                gather(4 + u, u)
            pe_pair(0, 0, True, False)
            with pe.Fori(0, PAIRS // 2 - 1) as i:
                for turn in (1, 0):
                    pe_pair(2 * i + 2 - turn, turn, False, False)
            pe_pair(PAIRS - 1, 1, False, True)

        @block.scalar
        def _(act):
            A = nc.scalar.activation

            def hi(n, c, width=W):
                act.wait_ge(stage_full[c % NSTAGE], 2 * (n - c % NSTAGE) + 16)
                act.wait_ge(chunk_used, n + 1)
                A(w_hi[:, c % NSPLIT, :, 0:width], stage[:, c % NSTAGE, :, 0:width], ACT.Copy).then_inc(hi_ready, 1)

            def load_table(function):
                A(unused[:, :], ones[:, 0:1], function)

            act.sem_inc(acc_free, 4)
            act.sem_inc(exp_done, 4)
            act.sem_inc(v_ready, 1)
            act.wait_ge(cols_ready, 2)
            A(siluc[:, :], pcol[:, 32:48], ACT.Sigmoid).then_inc(sigc_ready, 1)
            for t in range(T):
                act.wait_ge(x_in, 16 * T)
                if t:
                    act.wait_ge(act_seq, t)
                A(junk[:, :], x_sb[:, t, :], ACT.Square, accum_out=ssq[:, t:t + 1]).then_inc(act_seq, 1)
            act.wait_ge(act_seq, 4)
            A(rstd[:, 0:T], ssq[:, 0:T], ACT.Sqrt, bias=eps_c[:, :], scale=1.0 / D).then_inc(std_ready, 1)
            act.wait_ge(rstd_ready, 1)
            for t in range(T):
                A(x_sb[:, t, :], x_sb[:, t, :], ACT.Copy, scale=rstd[:, 4 + t:5 + t]).then_inc(xn_ready, 1)

            for cc in range(8):
                if cc % 4 == 0:
                    act.wait_ge(a1_ready, cc // 4 + 1)
                for k in (2 * cc, 2 * cc + 1):
                    act.wait_ge(xT_done, k + 1)
                    if k >= 4:
                        act.wait_ge(hT_lo_ready, k - 3)
                    A(h32[:, k % 4, :], bank[5 + k % 3][:, :], ACT.Identity, scale=a1[:, k:k + 1], bias=modcol[:, k:k + 1])\
                        .then_inc(h32_ready, 1)
                    act.wait_ge(h32_ready, k + 1)
                    A(hT_hi[:, k, :], h32[:, k % 4, :], ACT.Copy).then_inc(hT_hi_ready, 1)
                hi(N_Z + cc, cc)

            def latent_block(g, n_next, width_next, col, parts, squares):
                for b in range(4):
                    wait_bank(act, g // 4, b, n_next)
                    w = sum(q for q, _ in parts)
                    A(zc[:, b, col:col + w], bank[b][:, 0:w], ACT.Copy).then_inc(acc_free, 1)
                    if b == 0:
                        hi(n_next, 0, width_next)
                hi(n_next + 1, 1, width_next)
                for b in range(4):
                    act.wait_ge(acc_free, g + b + 5)
                    act.wait_ge(act_seq, squares + b)
                    size, stat = parts[0]
                    A(junk[:, 0:size], zc[:, b, col:col + size], ACT.Square, accum_out=zssq[:, stat, b:b + 1]).then_inc(act_seq, 1)

            latent_block(G_Z, N_Z + 8, LAT - QR, 0, [(QR, 12)], 4)
            for cc in range(2, 8):
                hi(N_Z + 8 + cc, cc, LAT - QR)
            latent_block(G_Z + 4, N_Z + 16, W, QR, [(KVR, 13), (ROPE, 15)], 8)
            with act.Fori(0, 3) as j:
                for cc in range(2, 8):
                    hi(N_Z + 16 + 8 * j + cc, cc)
                for b in range(4):
                    wait_bank(act, 2 + j, b, N_Z + 24 + 8 * j)
                    A(zg[:, b, ds(W * j, W)], bank[b][:, :], ACT.Copy).then_inc(acc_free, 1)
                    if b == 0:
                        hi(N_Z + 24 + 8 * j, 0)
                hi(N_Z + 25 + 8 * j, 1)
                for b in range(4):
                    act.wait_ge(acc_free, G_Z + 8 + 4 * j + b + 5)
                    for i in range(4):
                        act.wait_ge(act_seq, 12 + 16 * j + 4 * b + i)
                        A(junk[:, 0:P], zg[:, b, ds(W * j + P * i, P)], ACT.Square,
                          accum_out=zssq[:, ds(4 * j + i, 1), b]).then_inc(act_seq, 1)

            def gate_block(j, first):
                for cc in range(2, 8):
                    hi(N_GATE + 8 * j + cc, cc)
                    if first and cc == 4:
                        act.wait_ge(act_seq, 4 + 8 + 48)
                        A(zr[:, 0:12, :], zssq[:, 0:12, :], ACT.Sqrt, bias=eps_c[:, :], scale=1.0 / DH)
                        A(zr[:, 12, :], zssq[:, 12, :], ACT.Sqrt, bias=eps_c[:, :], scale=1.0 / QR)
                        A(zr[:, 13, :], zssq[:, 13, :], ACT.Sqrt, bias=eps_c[:, :], scale=1.0 / KVR).then_inc(zstd_ready, 1)
                for b in range(4):
                    wait_bank(act, G_GATE // 4 + j, b, N_GATE + 8 + 8 * j)
                    act.wait_ge(sig_out[b], 16 * j + 16)
                    A(sig[:, b, :], bank[b][:, :], ACT.Sigmoid).then_inc(acc_free, 1)
                    if b == 0:
                        hi(N_GATE + 8 + 8 * j, 0)
                    act.wait_ge(acc_free, G_GATE + 4 * j + b + 5)
                    act.dma_start(sig_v[:, ds(4 * j + b, 1), :], sig[:, b:b + 1, :]).then_inc(sig_out[b], 16)
                hi(N_GATE + 9 + 8 * j, 1)

            gate_block(0, True)
            with act.Fori(1, 8) as j:
                gate_block(j, False)

            def head_inputs_mla(H, b):
                act.wait_ge(qn_done, H + 1)
                A(qn[:, :], bank[4][:, :], ACT.Copy).then_inc(qn_ready, 1)
                act.wait_ge(v_done, H + 1)
                A(v_sb[:, b, :, :], bank[5][:, :].rearrange("p (t d) -> p t d", t=T), ACT.Copy).then_inc(v_ready, 1)
                act.wait_ge(kn_done, H + 1)
                A(kn[:, :], bank[4][:, :], ACT.Copy).then_inc(kn_ready, 1)

            def exponentials(H, b, scale):
                for qb in range(4):
                    act.wait_ge(nmax_ready, 4 * H + qb + 1)
                    A(probs[b][:, qb, :], bank[qb][:, :], ACT.Exp, bias=nmax[:, b, 4 + qb:5 + qb], scale=scale,
                      accum_out=rsum[:, b, qb:qb + 1]).then_inc(exp_done, 1)

            def output_hi(Hp):
                act.wait_ge(pv_done, 4 * Hp + 6)
                A(oT_hi[:, ds(Hp, 1), :], bank[4][:, :].unsqueeze(1), ACT.Copy).then_inc(o_hi, 1)

            for i in range(4):
                act.wait_ge(sig_out[i], 16 * 9)
            act.wait_ge(pro_ready, 7)
            def normalise(H, b):
                act.wait_ge(rinv_seq, H + 1)
                for qb in range(4):
                    last = A(probs[b][:, qb, :], probs[b][:, qb, :], ACT.Copy, scale=rsum[:, b, 4 + qb:5 + qb])
                last.then_inc(p_ready, 1)

            def query(H):
                act.wait_ge(qn_done, H + 1)
                A(qn[:, :], bank[5][:, :], ACT.Copy).then_inc(qn_ready, 1)

            head_inputs_mla(0, 0)
            exponentials(0, 0, MLA_SCALE)
            normalise(0, 0)
            with act.Fori(0, 3) as i:
                for b in (1, 0):
                    H = 2 * i + 2 - b
                    head_inputs_mla(H, b)
                    exponentials(H, b, MLA_SCALE)
                    normalise(H, b)
                    output_hi(H - 1)
            head_inputs_mla(7, 1)
            exponentials(7, 1, MLA_SCALE)
            query(HM)
            normalise(7, 1)
            output_hi(6)
            with act.Fori(0, 2) as n:
                for g in range(4):
                    H = 4 * n + g + HM
                    if g == 0:
                        act.wait_ge(kn_done, n + HM + 1)
                        A(kn[:, :], bank[4][:, :], ACT.Copy).then_inc(kn_ready, 1)
                    exponentials(H, g % 2, GQA_SCALE)
                    query(H + 1)
                    normalise(H, g % 2)
                    output_hi(H - 1)
            output_hi(HM + HG - 1)

            def merged_hi(tiles, n):
                act.wait_ge(chunk_used, n + NSPLIT)
                for k in tiles:
                    act.wait_ge(mT_ready, k + 1)
                    A(mT_hi[:, k, :], mT[:, k, :], ACT.Copy).then_inc(m_hi, 1)

            with act.Fori(0, 3) as j:
                for cc in range(2, 10):
                    hi(N_BR + 8 * j + cc, cc % 8)
            for cc in range(2, 10):
                hi(N_BR + 24 + cc, cc % 8)
                if cc == 6:
                    merged_hi(range(0, 4), N_OUT - 4)
                if cc == 7:
                    merged_hi(range(4, 8), N_OUT - 4)
            merged_hi(range(8, 12), N_OUT)
            for cc in range(2, 8):
                hi(N_OUT + cc, cc)
                if cc == 2:
                    merged_hi(range(12, 16), N_OUT)
            def square_out(j, t):
                act.wait_ge(x1_ready, 4 * j + t + 1)
                if not isinstance(j, int) or j + t > 0:
                    act.wait_ge(sq2_seq, 4 * j + t)
                A(junk3[:, :], x1[:, t, ds(W * j, W)], ACT.Square, accum_out=ssq2[:, t, ds(j, 1)]).then_inc(sq2_seq, 1)

            for cc in range(8):
                hi(N_OUT + 8 + cc, cc)
                if cc >= 4:
                    square_out(0, cc - 4)
            with act.Fori(1, 3) as j:
                for cc in range(8):
                    hi(N_OUT + 8 + 8 * j + cc, cc)
                    if cc >= 4:
                        square_out(j, cc - 4)
            hi(N_EXP, 0)
            load_table(ACT.Sqrt)
            hi(N_EXP + 1, 1)
            for t in range(T):
                square_out(3, t)

            act.wait_ge(std2_ready, 1)
            A(rstd[:, 8:12], ssq[:, 4:8], ACT.Sqrt, bias=eps_c[:, :], scale=1.0 / D).then_inc(std2_ready, 1)

            def normalised(t):
                A(xn[:, t, :], x1[:, t, :], ACT.Copy, scale=rstd[:, 12 + t:13 + t]).then_inc(xn2_ready, 1)

            load_table(ACT.Exp)
            act.wait_ge(lsub_ready, 1)
            A(aff[:, :, 0:NE], slots[:, :, 0:NE], ACT.Exp).then_inc(lexp_ready, 1)
            act.wait_ge(rstd2_ready, 1)
            for t in range(T):
                normalised(t)

            def tokens(turn, b, u, count):
                act.wait_ge(gather_done, count)
                if not isinstance(count, int) or count > 1:
                    act.wait_ge(xg_ready, count - 1)
                for i in range(4):
                    k = 4 * u + i
                    last = A(xg32[:, i, :], bank[b][:, i * P:(i + 1) * P], ACT.Identity, scale=a1[:, k:k + 1], bias=modcol[:, 48 + k:49 + k])
                last.then_inc(xg32_ready, 1)
                act.wait_ge(xg32_ready, count)
                A(xgT[turn][:, 4 * u:4 * u + 4, :, 0:64], xg32[:, :, :].rearrange("p k (e c) -> p k e c", e=2), ACT.Copy).then_inc(xg_hi, 1)

            def hi_expert(p, e, cc):
                c, n0 = cc % NSTAGE, N_EXP + 96 * p + 48 * e
                s = split_index(48 * e + cc) % NSPLIT
                before = SPLIT_CHUNKS[SPLIT_CHUNKS.index(48 * e + cc) - NSPLIT]
                act.wait_ge(stage_full[c], 2 * (n0 + cc - c) + 16)
                act.wait_ge(chunk_used, N_EXP + 96 * p + before + 1 + NSPLIT)
                A(w_hi[:, s, :, :], stage[:, c, :, :], ACT.Copy).then_inc(hi_ready, 1)

            def gu_copy(p, e, a):
                act.wait_ge(chunk_used, N_EXP + 96 * p + 48 * e + 8 * a + 8 + NSPLIT)
                if a >= 2:
                    act.wait_ge(fold_done, 4 * p + 2 * e + 1)
                else:
                    act.wait_ge(he_ready, 4 * p + 2 * e + 2)
                A(gu[:, a % 2, :], bank[a][:, :], ACT.Copy).then_inc(acc_free, 1)

            def sigmoid_gate(p, e, jb):
                act.wait_ge(fold_done, 4 * p + 2 * e + jb + 1)
                A(sgm[:, :], bank[4][:, 0:256], ACT.Sigmoid).then_inc(sgm_ready, 1)

            def he_round(p, e, jb):
                act.wait_ge(he32_ready, 4 * p + 2 * e + jb + 1)
                A(heT[:, 4 * jb:4 * jb + 4, 0:64], h32e[:, :].rearrange("p (f c) -> p f c", f=4), ACT.Copy).then_inc(he_hi, 1)

            def y_lower(p, e, jd):
                act.wait_ge(chunk_used, N_EXP + 96 * p + 48 * e + 33 + DOWN.index((jd, 3)) + NSPLIT)
                act.wait_ge(acc_free, G_EXP + 16 * p + 8 * e + jd + 8)
                A(ytmp[:, :], bank[jd][64:128, :], ACT.Copy).then_inc(ytmp_ready, 1)

            def y_round(p, jd):
                act.wait_ge(y32_ready, 4 * p + jd + 1)
                A(y_hi[:, jd, :], ysum[:, jd, :], ACT.Copy).then_inc(yhi_ready, 1)

            def final_squares(jd):
                for t in range(T):
                    act.wait_ge(scat_added, 16 * (PAIRS - 1) + 4 + 4 * jd + t + 1)
                    act.wait_ge(sq2_seq, 16 + 4 * jd + t)
                    A(junk3[:, :], x1[:, t, jd * W:(jd + 1) * W], ACT.Square, accum_out=ssq2[:, t, jd:jd + 1]).then_inc(sq2_seq, 1)

            def act_pair(p, turn, first, last_pair):
                for e in range(2):
                    for cc in range(48):
                        if not unsplit(48 * e + cc) and not (first and e == 0 and cc < 2):
                            hi_expert(p, e, cc)
                        if first and e == 0 and cc == 5:
                            for u in (2, 3):
                                tokens(0, 4 + u, u, u + 1)
                        if cc == 1 and e == 1:
                            y_lower(p, 0, 3)
                        if e == 0 and not first:
                            if cc == 1:
                                y_lower(p - 1, 1, 3)
                            if cc == 2:
                                y_round(p - 1, 3)
                        if cc == 28 and e == 0:
                            act.wait_ge(selT_done, p + 1)
                            A(selT[:, :], bank[6][:, :], ACT.Copy).then_inc(selT_ready, 1)
                        if cc in (9, 17, 25, 33):
                            gu_copy(p, e, cc // 8 - 1)
                        if cc == 20:
                            sigmoid_gate(p, e, 0)
                        if cc == 22:
                            he_round(p, e, 0)
                        if cc == 35:
                            sigmoid_gate(p, e, 1)
                        if cc == 36:
                            he_round(p, e, 1)
                        if cc in (41, 43, 45):
                            y_lower(p, e, (cc - 41) // 2)
                        if e == 1:
                            if cc in (42, 44, 46):
                                y_round(p, (cc - 42) // 2)
                        if not last_pair and GATHER_FROM <= 48 * e + cc < GATHER_FROM + 32 and cc % 8 == 6:
                            u = (48 * e + cc - GATHER_FROM) // 8
                            tokens(1 - turn, 5, u, 4 * p + 5 + u)
                if last_pair:
                    final_squares(0)
                    y_lower(p, 1, 3)
                    final_squares(1)
                    y_round(p, 3)
                    final_squares(2)
                    final_squares(3)

            for u in range(2):
                tokens(0, 4 + u, u, u + 1)
            act_pair(0, 0, True, False)
            with act.Fori(0, PAIRS // 2 - 1) as i:
                for turn in (1, 0):
                    act_pair(2 * i + 2 - turn, turn, False, False)
            act_pair(PAIRS - 1, 1, False, True)

            act.wait_ge(std3_ready, 1)
            A(ssq[:, 12:16], ssq[:, 8:12], ACT.Sqrt, bias=eps_c[:, :], scale=1.0 / D).then_inc(std3_ready, 1)

        @block.vector
        def _(dve):
            V = nc.vector
            seq = [0]

            def link(ins):
                seq[0] += 1
                ins.then_inc(dve_seq, 1)
                dve.wait_ge(dve_seq, seq[0])

            def lo(n, c, width=W):
                dve.wait_ge(hi_ready, n + 1)
                V.tensor_tensor(w_lo[:, c % NSPLIT, :, 0:width], stage[:, c % NSTAGE, :, 0:width],
                                w_hi[:, c % NSPLIT, :, 0:width].bitcast(F32), ALU.subtract).then_inc(lo_ready, 1)

            dve.sem_inc(lo_ready, NSTAGE)
            dve.sem_inc(ada_done, NADA)
            dve.sem_inc(ada_col_done, 1)
            dve.sem_inc(ada_col_ready, 1)
            dve.sem_inc(o_lo, 2)
            dve.sem_inc(pT_ready, 2)
            dve.sem_inc(pv_done, 2)
            for s in sig_out:
                dve.sem_inc(s, 16)
            dve.sem_inc(he_ready, 2)
            dve.sem_inc(scat_added, 4)
            V.memset(ones[:, :], 1.0)
            V.memset(aff[:, :, NE:NE + 2], 0.0)
            V.memset(eps_c[:, :], EPS)
            dve.wait_ge(cols_done, 1)
            V.tensor_copy(pcol[:, :], bank[5][:, 0:54]).then_inc(cols_ready, 1)
            V.tensor_copy(bcol[:, :], bank[5][:, 64:160]).then_inc(cols_ready, 1)
            dve.wait_ge(sigc_ready, 1)
            V.tensor_tensor(siluc[:, :], siluc[:, :], pcol[:, 32:48], ALU.mult).then_inc(siluc_ready, 1)
            dve.wait_ge(siluc_ready, 1)

            def ada_step(m, k, r, turn, ada_acc=ada_acc):
                dve.wait_ge(ada_full[k % NADA], 16 * turn)
                if k == 0:
                    if not isinstance(r, int) or r >= ADA_FIRST:
                        dve.wait_ge(ada_col_done, r + 1)
                    V.tensor_scalar(ada_acc[:, :], ada_tile[:, 0, :], siluc[:, 0:1], None, ALU.mult).then_inc(ada_done, 1)
                else:
                    dve.wait_ge(ada_done, m + NADA)
                    V.scalar_tensor_tensor(ada_acc[:, :], ada_tile[:, k % NADA, :], siluc[:, k:k + 1], ada_acc[:, :],
                                           ALU.mult, ALU.add).then_inc(ada_done, 1)

            def ada_finish(i, r):
                dve.wait_ge(ada_col_done, i + 2)
                V.tensor_tensor(modcol[:, ds(8 * r, 8)], bank[4][:, 0:8], bcol[:, ds(8 * r, 8)], ALU.add).then_inc(ada_col_ready, 1)

            def h_lo(k):
                dve.wait_ge(hT_hi_ready, k + 1)
                V.tensor_tensor(hT_lo[:, k, :], h32[:, k % 4, :], hT_hi[:, k, :].bitcast(F32), ALU.subtract).then_inc(hT_lo_ready, 1)

            def half_finished(i, half):
                ada_finish(i, ADA_ORDER[i])
                dve.wait_ge(ada_col_ready, i + 2)
                k = 8 * half
                V.scalar_tensor_tensor(a1[:, k:k + 8], modcol[:, 16 + k:24 + k], 1.0, pcol[:, k:k + 8], ALU.add, ALU.mult)\
                    .then_inc(a1_ready, 1)

            def h_piece(n):
                if n % 3 < 2:
                    h_lo(2 * (n // 3) + n % 3)
                else:
                    lo(N_Z + n // 3, n // 3)

            for i in range(ADA_FIRST):
                for k in range(KD):
                    ada_step(KD * i + k, k, i, 4 * i + k // NADA + 1, acc_first[i])
                    if i == 1 and k == 2:
                        ada_finish(0, ADA_ORDER[0])
                    if i == 2 and k == 2:
                        half_finished(1, 0)
                    n = KD * (i - 2) + k - 7
                    if 0 <= n < 12:
                        h_piece(n)
                    if i == 0 and k == KD - 1:
                        dve.wait_ge(std_ready, 1)
                        V.reciprocal(rstd[:, 4:8], rstd[:, 0:4]).then_inc(rstd_ready, 1)
            ada_finish(2, ADA_ORDER[2])
            half_finished(3, 1)
            for n in range(12, 24):
                h_piece(n)
            for cc in range(8):
                lo(N_Z + 8 + cc, cc, LAT - QR)
            lo(N_Z + 16, 0)
            with dve.Fori(0, 3) as j:
                for cc in range(1, 9):
                    lo(N_Z + 16 + 8 * j + cc, cc)

            def gate_block(j, first):
                for cc in range(8):
                    lo(N_GATE + 1 + 8 * j + cc, cc + 1)
                    if first and cc == 4:
                        dve.wait_ge(zstd_ready, 1)
                        V.reciprocal(zr[:, 0:14, :], zr[:, 0:14, :]).then_inc(zr_ready, 1)
                    for k in ADA_AT[cc]:
                        ada_step(KD * (j + ADA_FIRST) + k, k, j + ADA_FIRST, 4 * (j + ADA_FIRST) + k // NADA + 1)
                ada_finish(j + ADA_FIRST, j + ADA_FIRST)

            gate_block(0, True)
            with dve.Fori(1, 8) as j:
                gate_block(j, False)

            for i in range(4):
                dve.wait_ge(sig_out[i], 16 * 9)
            for i in range(7):
                dve.wait_ge(pro_done, i + 1)
                src = bank[4 + i % 4][:, :]
                if i < 4:
                    ins = V.tensor_scalar(cqT[:, i, :], src, pcol[:, 48 + i:49 + i], None, ALU.mult)
                elif i < 6:
                    dve.wait_ge(pro_done, 7)
                    ins = V.tensor_scalar(ckvT[:, i - 4, :], src, pcol[:, 48 + i:49 + i], None, ALU.mult)
                else:
                    ins = V.tensor_copy(krT[:, :], src)
                ins.then_inc(pro_ready, 1)

            def qr_rotate(H):
                dve.wait_ge(qr_done, H + 1)
                V.tensor_tensor(qr[:, :], bank[5][:, :], qtab[:, :], ALU.mult).then_inc(qr_ready, 1)

            def negative_max(H, b, scale):
                for qb in range(4):
                    dve.wait_ge(s_done, 4 * H + qb + 1)
                    V.tensor_reduce(nmax[:, b, qb:qb + 1], bank[qb][:, :], AX.X, ALU.max).then_inc(nmx_seq, 1)
                    dve.wait_ge(nmx_seq, 4 * H + qb + 1)
                    V.tensor_scalar(nmax[:, b, 4 + qb:5 + qb], nmax[:, b, qb:qb + 1], -scale, None, ALU.mult).then_inc(nmax_ready, 1)

            def output_lo(Hp):
                dve.wait_ge(o_hi, Hp + 1)
                V.tensor_tensor(oT_lo[:, ds(Hp, 1), :], bank[4][:, :].unsqueeze(1), oT_hi[:, ds(Hp, 1), :].bitcast(F32),
                                ALU.subtract).then_inc(o_lo, 1)

            def inverse_sums(H, b):
                dve.wait_ge(exp_done, 4 * H + 8)
                V.reciprocal(rsum[:, b, 4:8], rsum[:, b, 0:4]).then_inc(rinv_seq, 1)

            def probs_transposed(Hp, b=None):
                for kt in range(4):
                    dve.wait_ge(pT_done, 4 * Hp + kt + 1)
                    dve.wait_ge(pv_done, 4 * Hp + kt + 1)
                    V.tensor_copy(pT[:, kt % 2, :], bank[6 + kt % 2][:, :]).then_inc(pT_ready, 1)
                    if kt == 0 and b is not None:
                        inverse_sums(Hp + 1, b)

            qr_rotate(0)
            negative_max(0, 0, MLA_SCALE)
            inverse_sums(0, 0)
            with dve.Fori(0, 3) as i:
                for b in (1, 0):
                    H = 2 * i + 2 - b
                    qr_rotate(H)
                    negative_max(H, b, MLA_SCALE)
                    probs_transposed(H - 1, b)
                    output_lo(H - 1)
            qr_rotate(7)
            negative_max(7, 1, MLA_SCALE)
            probs_transposed(6, 1)
            output_lo(6)
            with dve.Fori(0, 2) as n:
                for g in range(4):
                    H = 4 * n + g + HM
                    negative_max(H, g % 2, GQA_SCALE)
                    probs_transposed(H - 1, g % 2)
                    output_lo(H - 1)
            probs_transposed(HM + HG - 1)
            output_lo(HM + HG - 1)

            def gate_diag(col, dst):
                V.tensor_tensor(dst[:, :, :], ident[:, :].unsqueeze(1).broadcast_to([P, 4, P]),
                                modcol[:, ds(col, 4)].unsqueeze(2).broadcast_to([P, 4, P]), ALU.mult).then_inc(diag_ready, 1)

            def gate_row(q, j):
                dve.wait_ge(row_done, q + 1)
                V.tensor_copy(gt_row[:, ds(j * W, W)], bank[5][:, :]).then_inc(row_ready, 1)

            def merged_lo(k):
                dve.wait_ge(m_hi, k + 1)
                V.tensor_tensor(mT_lo[:, k, :], mT[:, k, :], mT_hi[:, k, :].bitcast(F32), ALU.subtract).then_inc(m_lo, 1)

            def branch_block(j, last_block):
                gate_diag(32 + 4 * j, diag0)
                for half in range(2):
                    n0 = N_BR + 8 * j + 4 * half
                    g0 = G_BR + 8 * j + 4 * half
                    for cc in range(1, 4):
                        lo(n0 + cc, 4 * half + cc)
                        if last_block and half == 1 and cc >= 2:
                            for k in range(4 * cc - 8, 4 * cc - 4):
                                merged_lo(k)
                    if half == 1:
                        gate_row(j, j)
                    dve.wait_ge(sg_full[half], 16 * j + 16)
                    for b in range(4):
                        wait_bank(dve, G_BR // 4 + 2 * j + half, b, n0 + 4)
                        m_b = mT[:, ds(4 * j + b, 1), :]
                        gate = sg_in[:, half, b:b + 1, :]
                        prod = bank[b][:, :].unsqueeze(1)
                        if half == 0:
                            V.tensor_tensor(m_b, prod, gate, ALU.mult).then_inc(acc_free, 1)
                        else:
                            V.tensor_tensor(m_tmp[:, :].unsqueeze(1), prod, gate, ALU.mult).then_inc(acc_free, 1)
                            dve.wait_ge(acc_free, g0 + b + 5)
                            V.tensor_tensor(m_b, m_b, m_tmp[:, :].unsqueeze(1), ALU.add).then_inc(mT_ready, 1)
                            dve.wait_ge(mT_ready, 4 * j + b + 1)
                        if b == 0:
                            lo(n0 + 4, (4 * half + 4) % 8)

            with dve.Fori(0, 3) as j:
                branch_block(j, False)
            branch_block(3, True)
            lo(N_OUT + 1, 1)
            for k in range(8, 12):
                merged_lo(k)
            lo(N_OUT + 2, 2)
            for k in range(12, 16):
                merged_lo(k)
            for cc in range(3, 8):
                lo(N_OUT + cc, cc)

            def add_out(j, n_next):
                for b in range(4):
                    wait_bank(dve, G_OUT // 4 + j, b, N_OUT + 8 * j + 8)
                    V.tensor_tensor(m_tmp[:, :], bank[b][:, :], gt_row[:, ds(W * j, W)], ALU.mult).then_inc(acc_free, 1)
                    dve.wait_ge(acc_free, G_OUT + 4 * j + b + 5)
                    V.tensor_tensor(x1[:, b, ds(W * j, W)], x1[:, b, ds(W * j, W)], m_tmp[:, :], ALU.add).then_inc(x1_ready, 1)
                    dve.wait_ge(x1_ready, 4 * j + b + 1)
                    if b == 0 and n_next is not None:
                        lo(n_next, 0)

            def scale_x1(jb, i):
                k = 4 * jb + i
                dve.wait_ge(h2T_done, k + 1)
                if k >= 2:
                    dve.wait_ge(logit_done, k - 1)
                V.tensor_scalar(h2T[:, i % 2, :], bank[4 + i % 2][:, :], a1[:, k:k + 1], None, ALU.mult).then_inc(h2T_ready, 1)

            def out_block(j):
                for cc in range(1, 8):
                    lo(N_OUT + 8 * j + cc, cc)
                    if 3 <= cc < 7:
                        scale_x1(j - 1, cc - 3)

            dve.wait_ge(x1_in, 16 * T)
            add_out(0, N_OUT + 8)
            link(V.scalar_tensor_tensor(a1[:, :], modcol[:, 64:80], 1.0, pcol[:, 16:32], ALU.add, ALU.mult))
            out_block(1)
            dve.wait_ge(shift_done, 1)
            V.tensor_scalar(shiftT[:, :], ones[0:NE, :], bank[7][0:NE, 0:1], None, ALU.mult).then_inc(shift_ready, 1)
            add_out(1, N_OUT + 16)
            out_block(2)
            add_out(2, N_OUT + 24)
            out_block(3)
            add_out(3, None)

            for i in range(4):
                scale_x1(3, i)
            dve.wait_ge(sq2_seq, 16)
            V.tensor_reduce(ssq[:, 4:8], ssq2[:, :, :], AX.X, ALU.add).then_inc(std2_ready, 1)
            dve.wait_ge(shift_done, 2)
            V.tensor_copy(shift_row[:, :], bank[7][:, 64:64 + NE]).then_inc(shift_ready, 1)
            dve.wait_ge(std2_ready, 2)
            link(V.reciprocal(rstd[:, 12:16], rstd[:, 8:12]))
            dve.sem_inc(rstd2_ready, 1)
            dve.wait_ge(logit_done, KD)
            V.tensor_copy(work[:, 0, :], bank[6][0:NE, :]).then_inc(lgT_ready, 1)
            dve.wait_ge(lg_done, 1)
            dve.wait_ge(shift_ready, 2)
            link(V.tensor_tensor(slots[:, :, 0:NE], bank[7][:, 0:T * NE].rearrange("p (t e) -> p t e", t=T),
                                 rstd[:, 12:16].unsqueeze(2).broadcast_to([P, T, NE]), ALU.mult))
            link(V.tensor_tensor(slots[:, :, 0:NE], slots[:, :, 0:NE], shift_row[:, :].unsqueeze(1).broadcast_to([P, T, NE]), ALU.add))
            link(V.tensor_reduce(lmx[:, 0:4], slots[:, :, 0:NE], AX.X, ALU.max))
            V.tensor_tensor(slots[:, :, 0:NE], slots[:, :, 0:NE], lmx[:, 0:4].unsqueeze(2).broadcast_to([P, T, NE]),
                            ALU.subtract).then_inc(lsub_ready, 1)
            lo(N_EXP, 0)
            dve.wait_ge(lexp_ready, 1)
            link(V.tensor_reduce(lmx[:, 4:8], aff[:, :, 0:NE], AX.X, ALU.add))
            link(V.reciprocal(lmx[:, 0:4], lmx[:, 4:8]))
            V.tensor_tensor(aff[:, :, 0:NE], aff[:, :, 0:NE], lmx[:, 0:4].unsqueeze(2).broadcast_to([P, T, NE]),
                            ALU.mult).then_inc(aff_ready, 1)
            lo(N_EXP + 1, 1)
            dve.wait_ge(affT_done, 1)
            link(V.tensor_copy(affT[:, :], bank[4][0:NE, :]))
            src = affT[:, :]
            for i in range(CAP // 8):
                link(V.max(m8[:, :], src))
                if i < CAP // 8 - 1:
                    link(V.match_replace(work[:, i % 2, :], m8[:, :], src, -1.0))
                    src = work[:, i % 2, :]
            link(V.tensor_scalar(gt_m[:, :], affT[:, :], m8[:, 7:8], 0.0, ALU.is_gt, ALU.add, accum_out=cnt[:, 0:1]))
            link(V.tensor_scalar(cnt[:, 1:2], cnt[:, 0:1], -1.0, float(CAP), ALU.mult, ALU.add))
            link(V.tensor_scalar(eq_m[:, :], affT[:, :], m8[:, 7:8], None, ALU.is_equal))
            link(V.tensor_tensor_scan(rank[:, :], eq_m[:, :], eq_m[:, :], 0.0, ALU.add, ALU.bypass))
            link(V.scalar_tensor_tensor(eq_m[:, :], rank[:, :], cnt[:, 1:2], eq_m[:, :], ALU.is_le, ALU.mult))
            link(V.tensor_tensor(gt_m[:, :], gt_m[:, :], eq_m[:, :], ALU.add))
            link(V.tensor_tensor_scan(rank[:, :], gt_m[:, :], gt_m[:, :], 0.0, ALU.add, ALU.bypass))
            link(V.tensor_tensor(rank[:, :], rank[:, :], gt_m[:, :], ALU.mult))
            V.tensor_scalar(slotT[:, :], rank[:, :], -1.0, None, ALU.add).then_inc(slotT_ready, 1)
            V.memset(slots[:, :, NE:NE + 2], -1.0)
            dve.wait_ge(slots_done, 1)
            link(V.tensor_copy(slots[:, :, 0:NE], bank[5][:, 0:T * NE].rearrange("p (t e) -> p t e", t=T)))

            def select(p):
                for t in range(T):
                    last = V.tensor_tensor(sel[:, t, :, :], iota[:, :].unsqueeze(1).broadcast_to([P, 2, CAP]),
                                           slots[:, t, ds(2 * p, 2)].unsqueeze(2).broadcast_to([P, 2, CAP]), ALU.is_equal)
                last.then_inc(sel_ready, 1)

            def tokens_lo(turn, u, count):
                dve.wait_ge(xg_hi, count)
                V.tensor_tensor(xgT[turn][:, 4 * u:4 * u + 4, :, 64:128], xg32[:, :, :].rearrange("p k (e c) -> p k e c", e=2),
                                xgT[turn][:, 4 * u:4 * u + 4, :, 0:64].bitcast(F32), ALU.subtract).then_inc(xg_ready, 1)

            def lo_expert(p, e, cc):
                s = split_index(48 * e + cc) % NSPLIT
                dve.wait_ge(hi_ready, N_EXP + SPLIT_PER_PAIR * p + split_index(48 * e + cc) + 1)
                V.tensor_tensor(w_lo[:, s, :, :], stage[:, cc % NSTAGE, :, :], w_hi[:, s, :, :].bitcast(F32), ALU.subtract)\
                    .then_inc(lo_ready, 1)

            def swiglu(p, e, jb):
                dve.wait_ge(sgm_ready, 4 * p + 2 * e + jb + 1)
                dve.wait_ge(he_ready, 4 * p + 2 * e + jb + 2)
                V.tensor_tensor(h32e[:, :], bank[4][:, 0:256], sgm[:, :], ALU.mult).then_inc(he_mid, 1)
                dve.wait_ge(he_mid, 4 * p + 2 * e + jb + 1)
                V.tensor_tensor(h32e[:, :], bank[4][:, 256:512], h32e[:, :], ALU.mult).then_inc(he32_ready, 1)

            def he_lo(p, e, jb):
                dve.wait_ge(he_hi, 4 * p + 2 * e + jb + 1)
                V.tensor_tensor(heT[:, 4 * jb:4 * jb + 4, 64:128], h32e[:, :].rearrange("p (f c) -> p f c", f=4),
                                heT[:, 4 * jb:4 * jb + 4, 0:64].bitcast(F32), ALU.subtract).then_inc(he_ready, 1)

            def y_add(p, e, jd):
                dve.wait_ge(ytmp_ready, 8 * p + 4 * e + jd + 1)
                V.tensor_tensor(ysum[64 * e:64 * e + 64, jd, :], bank[jd][0:64, :], ytmp[:, :], ALU.add)\
                    .then_inc(acc_free, 1)
                if e == 1:
                    dve.wait_ge(acc_free, G_EXP + 16 * p + 8 + jd + 9)
                    if jd == 0:
                        dve.wait_ge(val_ready, p + 1)
                    V.scalar_tensor_tensor(ysum[:, jd, :], ysum[:, jd, :], val[:, 0:1], gt_row[:, jd * W:(jd + 1) * W],
                                           ALU.mult, ALU.mult).then_inc(y32_ready, 1)

            def y_lo_part(p, jd):
                dve.wait_ge(yhi_ready, 4 * p + jd + 1)
                V.tensor_tensor(y_lo[:, jd, :], ysum[:, jd, :], y_hi[:, jd, :].bitcast(F32), ALU.subtract).then_inc(ylo_ready, 1)

            def add_scattered(p, jd, tiles=range(T)):
                for t in tiles:
                    dve.wait_ge(scat_done, 16 * p + 4 * jd + t + 1)
                    V.tensor_tensor(x1[:, t, jd * W:(jd + 1) * W], x1[:, t, jd * W:(jd + 1) * W], bank[4 + t][:, :],
                                    ALU.add).then_inc(scat_added, 1)

            def dve_pair(p, turn, first, last_pair):
                for e in range(2):
                    for cc in range(48):
                        if not unsplit(48 * e + cc) and not (first and e == 0 and cc < 2):
                            lo_expert(p, e, cc)
                        if first and e == 0 and cc == 5:
                            for u in (2, 3):
                                tokens_lo(0, u, u + 1)
                        if cc == 1 and e == 1:
                            y_add(p, 0, 3)
                        if e == 0 and not first:
                            if cc == 1:
                                y_add(p - 1, 1, 3)
                            if cc == 2:
                                y_lo_part(p - 1, 3)
                            if cc - 1 in SCATTER_AT:
                                add_scattered(p - 1, SCATTER_AT.index(cc - 1), (0, 1))
                            if cc - 2 in SCATTER_AT:
                                add_scattered(p - 1, SCATTER_AT.index(cc - 2), (2, 3))
                        if cc == 28 and e == 0:
                            dve.wait_ge(val_done, p + 1)
                            V.tensor_copy(val[0:64, :], bank[7][0:64, 0:1])
                            V.tensor_copy(val[64:128, :], bank[7][64:128, 1:2]).then_inc(val_ready, 1)
                        if first and e == 0 and 4 <= cc < 20 and cc % 2 == 0:
                            q = cc // 4 - 1
                            if cc % 4 == 0:
                                gate_diag(80 + 4 * q, diag1)
                            else:
                                gate_row(4 + q, q)
                        if cc == 20:
                            swiglu(p, e, 0)
                        if cc == 22:
                            he_lo(p, e, 0)
                        if cc == 35:
                            swiglu(p, e, 1)
                        if cc == 36:
                            he_lo(p, e, 1)
                        if cc == 30 and e == 0 and not last_pair:
                            select(p + 1)
                        if cc in (41, 43, 45):
                            y_add(p, e, (cc - 41) // 2)
                        if e == 1:
                            if cc in (42, 44, 46):
                                y_lo_part(p, (cc - 42) // 2)
                            if last_pair and cc in (44, 46):
                                add_scattered(p, (cc - 44) // 2)
                        if not last_pair and GATHER_FROM <= 48 * e + cc < GATHER_FROM + 32 and cc % 8 == 6:
                            u = (48 * e + cc - GATHER_FROM) // 8
                            tokens_lo(1 - turn, u, 4 * p + 5 + u)
                if last_pair:
                    y_add(p, 1, 3)
                    add_scattered(p, 2)
                    y_lo_part(p, 3)
                    add_scattered(p, 3)

            select(0)
            for u in range(2):
                tokens_lo(0, u, u + 1)
            dve_pair(0, 0, True, False)
            with dve.Fori(0, PAIRS // 2 - 1) as i:
                for turn in (1, 0):
                    dve_pair(2 * i + 2 - turn, turn, False, False)
            dve_pair(PAIRS - 1, 1, False, True)

            dve.wait_ge(sq2_seq, 32)
            V.tensor_reduce(ssq[:, 8:12], ssq2[:, :, :], AX.X, ALU.add).then_inc(std3_ready, 1)
            dve.wait_ge(std3_ready, 2)
            link(V.reciprocal(rstd[:, 0:4], ssq[:, 12:16]))
            dve.wait_ge(gf_in, 16)
            for t in range(T):
                V.scalar_tensor_tensor(res[t][:, :], x1[:, t, :], rstd[:, t:t + 1], gf_row[:, :], ALU.mult, ALU.mult)\
                    .then_inc(res_ready, 1)

        @block.gpsimd
        def _(pool):
            G = nc.gpsimd
            seq = [0]

            def link(ins):
                seq[0] += 1
                ins.then_inc(pool_seq, 1)
                pool.wait_ge(pool_seq, seq[0])

            pool.wait_ge(cols_done, 1)
            pool.wait_ge(h32_ready, KD)
            pool.wait_ge(zr_ready, 1)
            loads = [(rope_kc[:, :, :], consts[:, C_KC:C_KS]), (rope_ks[:, :, :], consts[:, C_KS:C_GC]),
                     (rope_gc[:, :, :, :], consts[:, C_GC:C_GS]), (rope_gs[:, :, :, :], consts[:, C_GS:C_END])]
            for dst, src in loads[:2]:
                pool.dma_start(dst, src.rearrange("p (t f) -> p t f", t=T)).then_inc(tab_in, 16)
            for dst, src in loads[2:]:
                pool.dma_start(dst, src.rearrange("p (t h f) -> p t h f", t=T, h=2)).then_inc(tab_in, 16)
            for h in range(HG + KVG):
                g = g_qn if h < HG else g_kn
                pool.dma_start(g_row[:, h, :], g[0].partition_broadcast(P)).then_inc(tab_in, 16)
            pool.wait_ge(tab_in, 16 * (4 + HG + KVG))
            for t in range(T):
                G.tensor_scalar(zc[:, t, 0:QR], zc[:, t, 0:QR], zr[:, 12, t:t + 1], None, ALU.mult)
                G.tensor_scalar(zc[:, t, QR:QR + KVR], zc[:, t, QR:QR + KVR], zr[:, 13, t:t + 1], None, ALU.mult)
            kr1, kr_2 = zc[:, :, 768:800], zc[:, :, 800:832]
            ta, tb = r_a[:, 0:4, 0, :], r_b[:, 0:4, 0, :]
            tc_, td = r_c[:, 0:4, 0, :], r_d[:, 0:4, 0, :]
            G.tensor_tensor(ta, kr1, rope_kc[:, :, :], ALU.mult)
            G.tensor_tensor(tb, kr_2, rope_ks[:, :, :], ALU.mult)
            G.tensor_tensor(tc_, kr1, rope_ks[:, :, :], ALU.mult)
            link(G.tensor_tensor(td, kr_2, rope_kc[:, :, :], ALU.mult))
            for o in (0, 64):
                G.tensor_tensor(kr2[:, :, o:o + 32], ta, tb, ALU.subtract)
                ins = G.tensor_tensor(kr2[:, :, o + 32:o + 64], tc_, td, ALU.add)
            link(ins)
            NH = HG + KVG
            for t in range(T):
                z4 = zg[:, t, 0:NH * DH].rearrange("p (h d) -> p h d", h=NH)
                z5 = zg[:, t, 0:NH * DH].rearrange("p (h r d) -> p h r d", h=NH, r=2)
                x1_, x2_ = z5[:, :, :, 0:32], z5[:, :, :, 32:64]
                cos = rope_gc[:, t, :, :].unsqueeze(1).broadcast_to([P, NH, 2, 32])
                sin = rope_gs[:, t, :, :].unsqueeze(1).broadcast_to([P, NH, 2, 32])
                link(G.tensor_tensor(z4, z4, zr[:, 0:NH, t].unsqueeze(2).broadcast_to([P, NH, DH]), ALU.mult))
                link(G.tensor_tensor(z4, z4, g_row[:, :, :], ALU.mult))
                G.tensor_tensor(r_a[:, :, :, :], x1_, cos, ALU.mult)
                G.tensor_tensor(r_b[:, :, :, :], x2_, sin, ALU.mult)
                G.tensor_tensor(r_c[:, :, :, :], x1_, sin, ALU.mult)
                link(G.tensor_tensor(r_d[:, :, :, :], x2_, cos, ALU.mult))
                G.tensor_tensor(x1_, r_a[:, :, :, :], r_b[:, :, :, :], ALU.subtract)
                ins = G.tensor_tensor(x2_, r_c[:, :, :, :], r_d[:, :, :, :], ALU.add)
                if t < T - 1:
                    link(ins)
                else:
                    ins.then_inc(zpost_ready, 1)
            pool.wait_ge(zpost_ready, 1)
            for h in range(HG + 1):
                H = HM + h
                pool.wait_ge(qn_done, H)
                if h == HG:
                    G.tensor_copy(q_stage[:, :, :], zg[:, :, (h - 1) * DH:h * DH]).then_inc(qs_ready, 1)
                    break
                if h % 4 == 0:
                    pool.wait_ge(v_done, HM)
                    pool.wait_ge(kn_done, h // 4 + HM)
                    k_head = (HG + h // 4) * DH
                    G.tensor_copy(k_stage[:, :, :], zg[:, :, k_head:k_head + DH]).then_inc(ks_ready, 1)
                G.tensor_copy(q_stage[:, :, :], zg[:, :, h * DH:(h + 1) * DH]).then_inc(qs_ready, 1)
                pool.wait_ge(pv_done, 4 * H - 2)
                v_head = (HG + KVG + h // 4) * DH
                G.tensor_copy(v_sb[:, h % 2, :, :], zg[:, :, v_head:v_head + DH]).then_inc(v_ready, 1)


_INS = ["x", "c", "w_ada", "b_ada", "g_mix", "w_in", "g_cq", "g_ckv", "w_uq", "w_ukv", "g_qn", "g_kn",
        "w_br_a", "w_br_b", "w_out", "g_ffn", "w_router", "w_e_gate", "w_e_up", "w_e_down", "g_final"]


def kernel(**inputs):
    import numpy as _np
    import concourse.bacc as _bacc
    from concourse import mybir as _mybir
    from concourse.bass_utils import run_bass_kernel_spmd as _run

    nc = _bacc.Bacc("TRN2", target_bir_lowering=False, num_devices=1)
    arrays, args = {}, []
    for name in _INS:
        a = _np.ascontiguousarray(inputs[name])
        arrays[f"in_{name}"] = a
        args.append(nc.dram_tensor(f"in_{name}", a.shape, _mybir.dt.from_np(a.dtype), kind="ExternalInput").ap())
    k = shape_constants()
    arrays["in_consts"] = k
    args.append(nc.dram_tensor("in_consts", k.shape, _mybir.dt.float32, kind="ExternalInput").ap())
    args.append(nc.dram_tensor("sig_gates", (2 * D, S), _mybir.dt.float32, kind="Internal").ap())
    args.append(nc.dram_tensor("out_0", (1, S, D), _mybir.dt.float32, kind="ExternalOutput").ap())
    encoder_block(nc, *args)
    r = _run(nc, [arrays], core_ids=[0])
    return r.results[0]["out_0"]
```
